# Optimizing a Trainium2 kernel written in Bass

```python
import jax, jax.numpy as jnp
from jax import lax
import numpy as np

D_MODEL = 1024
BATCH = 1
SEQ = 128
DEPTH = 1
DEC_BATCH = 1
DEC_SEQ = 512
PAST_LEN = 128

GRID_W = 64
N_HEADS_M = 8
HEAD_DIM_M = 128
D_MLSTM = N_HEADS_M * HEAD_DIM_M
CHUNK = 64
POOL_WINDOWS = (2, 4, 8, 16)
N_POOL_GROUPS = 4
POOL_GROUP_DIM = 128
D_POOL = N_POOL_GROUPS * POOL_GROUP_DIM
N_EXPERT_GROUPS = 4
EXPERTS_PER_GROUP = 4
N_EXPERTS = N_EXPERT_GROUPS * EXPERTS_PER_GROUP
D_EXPERT = 512
TOP_K_IN_GROUP = 2
IN_SPLITS = (D_MLSTM, D_MLSTM, D_MLSTM, D_MLSTM, 4 * N_HEADS_M, D_POOL, D_MODEL, D_MODEL)
D_IN = 4 * D_MLSTM + 4 * N_HEADS_M + D_POOL + 2 * D_MODEL
GATE_OFFSET = 4 * D_MLSTM
EPS = 1e-6
NEG = -1e30

kernel_name = "hybrid_mlstm_pool_hiermoe_diffusion_step"

def _rmsnorm(x, g):
    xf = x.astype(jnp.float32)
    y = xf * lax.rsqrt(jnp.mean(xf * xf, axis=-1, keepdims=True) + EPS) * g.astype(jnp.float32)
    return y.astype(x.dtype)

def _mlstm_scan(q, k, v, log_i, log_f, C0, n0, m0):
    B, H, T, Dh = q.shape
    nc = T // CHUNK

    def to_chunks(a):
        return jnp.moveaxis(a.reshape(a.shape[:2] + (nc, CHUNK) + a.shape[3:]), 2, 0)

    xs = (to_chunks(q), to_chunks(k), to_chunks(v), to_chunks(log_i), to_chunks(log_f))
    lower = jnp.tril(jnp.ones((CHUNK, CHUNK), dtype=bool))

    def step(carry, inp):
        C, n, m = carry
        qc, kc, vc, ic, fc = inp
        b = jnp.cumsum(fc, axis=-1)
        dmat = jnp.where(lower, b[..., :, None] - b[..., None, :] + ic[..., None, :], NEG)
        inter = b + m[..., None]
        m_t = jnp.maximum(inter, jnp.max(dmat, axis=-1))
        w_intra = jnp.exp(dmat - m_t[..., None])
        w_inter = jnp.exp(inter - m_t)
        s = jnp.einsum('bhtd,bhsd->bhts', qc, kc) * w_intra
        num = w_inter[..., None] * jnp.einsum('bhtd,bhde->bhte', qc, C) + jnp.einsum('bhts,bhse->bhte', s, vc)
        den = w_inter * jnp.einsum('bhtd,bhd->bht', qc, n) + jnp.sum(s, axis=-1)
        h = num / jnp.maximum(jnp.abs(den), jnp.exp(-m_t))[..., None]
        b_last = b[..., -1]
        m_new = m_t[..., -1]
        w_state = jnp.exp(b_last[..., None] - b + ic - m_new[..., None])
        decay = jnp.exp(b_last + m - m_new)
        C_new = decay[..., None, None] * C + jnp.einsum('bhs,bhsd,bhse->bhde', w_state, kc, vc)
        n_new = decay[..., None] * n + jnp.einsum('bhs,bhsd->bhd', w_state, kc)
        return (C_new, n_new, m_new), h

    (C, n, m), hs = lax.scan(step, (C0, n0, m0), xs)
    h = jnp.moveaxis(hs, 0, 2).reshape(B, H, T, Dh)
    return h, C, n, m

def _mlstm_branch(q_raw, k_raw, v_raw, o_raw, gates, gn_gain, C0, n0, m0):
    B, T, _ = q_raw.shape

    def heads(a):
        return a.reshape(B, T, N_HEADS_M, HEAD_DIM_M).transpose(0, 2, 1, 3).astype(jnp.float32)

    q = heads(q_raw)
    k = heads(k_raw) * (HEAD_DIM_M ** -0.5)
    v = heads(v_raw)
    g = gates.astype(jnp.float32).transpose(0, 2, 1)
    i_f, f_f, i_b, f_b = jnp.split(g, 4, axis=1)
    C0 = C0.astype(jnp.float32); n0 = n0.astype(jnp.float32); m0 = m0.astype(jnp.float32)
    h_f, C_f, n_f, m_f = _mlstm_scan(q, k, v, i_f, jax.nn.log_sigmoid(f_f), C0[:, 0], n0[:, 0], m0[:, 0])

    def flip(a):
        return jnp.flip(a, axis=2)

    h_b, C_b, n_b, m_b = _mlstm_scan(flip(q), flip(k), flip(v), flip(i_b), flip(jax.nn.log_sigmoid(f_b)),
                                     C0[:, 1], n0[:, 1], m0[:, 1])
    h = h_f + flip(h_b)
    h = h * lax.rsqrt(jnp.mean(h * h, axis=-1, keepdims=True) + EPS)
    h = h.transpose(0, 2, 1, 3).reshape(B, T, D_MLSTM) * gn_gain.astype(jnp.float32)
    y = (h * jax.nn.sigmoid(o_raw.astype(jnp.float32))).astype(q_raw.dtype)
    C = jnp.stack([C_f, C_b], axis=1)
    n = jnp.stack([n_f, n_b], axis=1)
    m = jnp.stack([m_f, m_b], axis=1)
    return y, C, n, m

def _window_bounds(size, w):
    idx = jnp.arange(size)
    lo = jnp.clip(idx - w // 2, 0, size)
    hi = jnp.clip(idx - w // 2 + w, 0, size)
    return lo, hi

def _pool_1d(u, w):
    T = u.shape[1]
    cs = jnp.pad(jnp.cumsum(u, axis=1), ((0, 0), (1, 0), (0, 0)))
    lo, hi = _window_bounds(T, w)
    s = jnp.take(cs, hi, axis=1) - jnp.take(cs, lo, axis=1)
    return s / (hi - lo).astype(jnp.float32)[None, :, None]

def _pool_2d(g, w):
    R, W = g.shape[1], g.shape[2]
    integ = jnp.pad(jnp.cumsum(jnp.cumsum(g, axis=1), axis=2), ((0, 0), (1, 0), (1, 0), (0, 0)))
    rl, rh = _window_bounds(R, w)
    cl, ch = _window_bounds(W, w)

    def corner(ri, ci):
        return jnp.take(jnp.take(integ, ri, axis=1), ci, axis=2)

    s = corner(rh, ch) - corner(rl, ch) - corner(rh, cl) + corner(rl, cl)
    cnt = ((rh - rl)[:, None] * (ch - cl)[None, :]).astype(jnp.float32)
    return s / cnt[None, :, :, None]

def _pool_branch(u, w_pool_grp, pool_scale, rows):
    B, T, _ = u.shape
    uf = u.astype(jnp.float32)
    outs = []
    for gi, w in enumerate(POOL_WINDOWS):
        ug = uf[..., gi * POOL_GROUP_DIM:(gi + 1) * POOL_GROUP_DIM]
        if rows is None:
            pooled = _pool_1d(ug, w)
        else:
            pooled = _pool_2d(ug.reshape(B, rows, GRID_W, POOL_GROUP_DIM), w).reshape(B, T, POOL_GROUP_DIM)
        outs.append(pooled - ug)
    p = jnp.stack(outs, axis=2).astype(u.dtype)
    y = jnp.einsum('btgc,gcd->btgd', p, w_pool_grp).reshape(B, T, D_POOL)
    return y * pool_scale

def _hier_moe(h, w_router_grp, b_router_grp, w_router_exp, b_router_exp, w_exp_gate, w_exp_up, w_exp_down):
    B, T, D = h.shape
    ht = h.reshape(B * T, D)
    hf = ht.astype(jnp.float32)
    lg = hf @ w_router_grp.astype(jnp.float32) + b_router_grp.astype(jnp.float32)
    pg = jax.nn.softmax(lg, axis=-1)
    grp_oh = jax.nn.one_hot(jnp.argmax(lg, axis=-1), N_EXPERT_GROUPS, dtype=jnp.float32)
    p_top = jnp.sum(pg * grp_oh, axis=-1, keepdims=True)
    le = jnp.einsum('nd,dge->nge', hf, w_router_exp.astype(jnp.float32)) + b_router_exp.astype(jnp.float32)
    le_sel = jnp.einsum('nge,ng->ne', le, grp_oh)
    top_v, top_i = lax.top_k(le_sel, TOP_K_IN_GROUP)
    w2 = jax.nn.softmax(top_v, axis=-1) * p_top
    w_in_grp = jnp.sum(jax.nn.one_hot(top_i, EXPERTS_PER_GROUP, dtype=jnp.float32) * w2[..., None], axis=1)
    w_dense = (grp_oh[:, :, None] * w_in_grp[:, None, :]).reshape(B * T, N_EXPERTS)
    a = jnp.einsum('nd,edf->nef', ht, w_exp_gate)
    u = jnp.einsum('nd,edf->nef', ht, w_exp_up)
    act = jax.nn.silu(a) * u * w_dense.astype(ht.dtype)[..., None]
    out = jnp.einsum('nef,efd->nd', act, w_exp_down)
    return out.reshape(B, T, D)

def _layer(x, mod, C0, n0, m0, rows, g_norm1, w_in, b_in, gn_gain, w_pool_grp, pool_scale,
           w_proj_a, w_proj_b, w_out, g_norm2, w_router_grp, b_router_grp, w_router_exp,
           b_router_exp, w_exp_gate, w_exp_up, w_exp_down):
    shift1, scale1, gate1, shift2, scale2, gate2 = [m[:, None, :] for m in jnp.split(mod, 6, axis=-1)]
    h = _rmsnorm(x, g_norm1) * (1 + scale1) + shift1
    proj = h @ w_in + b_in
    split_at = [int(s) for s in np.cumsum(IN_SPLITS)[:-1]]
    q_raw, k_raw, v_raw, o_raw, gates, u_pool, g_a, g_b = jnp.split(proj, split_at, axis=-1)
    y_a, C, n, m = _mlstm_branch(q_raw, k_raw, v_raw, o_raw, gates, gn_gain, C0, n0, m0)
    y_b = _pool_branch(u_pool, w_pool_grp, pool_scale, rows)
    merged = jax.nn.sigmoid(g_a) * (y_a @ w_proj_a) + jax.nn.sigmoid(g_b) * (y_b @ w_proj_b)
    x = x + gate1 * (merged @ w_out)
    h2 = _rmsnorm(x, g_norm2) * (1 + scale2) + shift2
    x = x + gate2 * _hier_moe(h2, w_router_grp, b_router_grp, w_router_exp, b_router_exp,
                              w_exp_gate, w_exp_up, w_exp_down)
    return x, C, n, m

def setup_inputs(seed: int = 0) -> dict:
    key = jax.random.key(seed)
    ks = jax.random.split(key, 32)
    f32 = jnp.float32

    def nrm(k, shape, scale):
        return jax.random.normal(k, shape, f32) * scale

    b_in = nrm(ks[10], (DEPTH, D_IN), 0.02)
    fb = jax.random.uniform(ks[11], (DEPTH, 2, N_HEADS_M), f32, 3.0, 6.0)
    b_in = b_in.at[:, GATE_OFFSET + N_HEADS_M:GATE_OFFSET + 2 * N_HEADS_M].add(fb[:, 0])
    b_in = b_in.at[:, GATE_OFFSET + 3 * N_HEADS_M:GATE_OFFSET + 4 * N_HEADS_M].add(fb[:, 1])
    return {
        "x_prompt": nrm(ks[0], (BATCH, SEQ, D_MODEL), 1.0),
        "x_sample": nrm(ks[1], (DEC_BATCH, DEC_SEQ, D_MODEL), 1.0),
        "state_C": nrm(ks[2], (DEC_BATCH, DEPTH, 2, N_HEADS_M, HEAD_DIM_M, HEAD_DIM_M), 0.1),
        "state_n": nrm(ks[3], (DEC_BATCH, DEPTH, 2, N_HEADS_M, HEAD_DIM_M), 0.1),
        "state_m": nrm(ks[4], (DEC_BATCH, DEPTH, 2, N_HEADS_M), 1.0),
        "c": nrm(ks[5], (DEC_BATCH, D_MODEL), 1.0),
        "c_ctx": nrm(ks[6], (D_MODEL,), 1.0),
        "w_mod": nrm(ks[7], (DEPTH, D_MODEL, 6 * D_MODEL), 0.5 * D_MODEL ** -0.5),
        "b_mod": nrm(ks[8], (DEPTH, 6 * D_MODEL), 0.02),
        "g_norm1": 1.0 + nrm(ks[9], (DEPTH, D_MODEL), 0.02),
        "w_in": nrm(ks[12], (DEPTH, D_MODEL, D_IN), D_MODEL ** -0.5),
        "b_in": b_in,
        "gn_gain": 1.0 + nrm(ks[13], (DEPTH, D_MLSTM), 0.02),
        "w_pool_grp": nrm(ks[14], (DEPTH, N_POOL_GROUPS, POOL_GROUP_DIM, POOL_GROUP_DIM), POOL_GROUP_DIM ** -0.5),
        "pool_scale": 1.0 + nrm(ks[15], (DEPTH, D_POOL), 0.1),
        "w_proj_a": nrm(ks[16], (DEPTH, D_MLSTM, D_MODEL), D_MLSTM ** -0.5),
        "w_proj_b": nrm(ks[17], (DEPTH, D_POOL, D_MODEL), D_POOL ** -0.5),
        "w_out": nrm(ks[18], (DEPTH, D_MODEL, D_MODEL), D_MODEL ** -0.5),
        "g_norm2": 1.0 + nrm(ks[19], (DEPTH, D_MODEL), 0.02),
        "w_router_grp": nrm(ks[20], (DEPTH, D_MODEL, N_EXPERT_GROUPS), D_MODEL ** -0.5),
        "b_router_grp": nrm(ks[21], (DEPTH, N_EXPERT_GROUPS), 0.01),
        "w_router_exp": nrm(ks[22], (DEPTH, D_MODEL, N_EXPERT_GROUPS, EXPERTS_PER_GROUP), D_MODEL ** -0.5),
        "b_router_exp": nrm(ks[23], (DEPTH, N_EXPERT_GROUPS, EXPERTS_PER_GROUP), 0.01),
        "w_exp_gate": nrm(ks[24], (DEPTH, N_EXPERTS, D_MODEL, D_EXPERT), D_MODEL ** -0.5),
        "w_exp_up": nrm(ks[25], (DEPTH, N_EXPERTS, D_MODEL, D_EXPERT), D_MODEL ** -0.5),
        "w_exp_down": nrm(ks[26], (DEPTH, N_EXPERTS, D_EXPERT, D_MODEL), D_EXPERT ** -0.5),
        "g_final": 1.0 + nrm(ks[27], (D_MODEL,), 0.02),
    }

def reference(x_prompt, x_sample, state_C, state_n, state_m, c, c_ctx, w_mod, b_mod, g_norm1,
              w_in, b_in, gn_gain, w_pool_grp, pool_scale, w_proj_a, w_proj_b, w_out, g_norm2,
              w_router_grp, b_router_grp, w_router_exp, b_router_exp, w_exp_gate, w_exp_up,
              w_exp_down, g_final):
    rows = x_sample.shape[1] // GRID_W
    bp = x_prompt.shape[0]
    zC = jnp.zeros((bp, 2, N_HEADS_M, HEAD_DIM_M, HEAD_DIM_M), jnp.float32)
    zn = jnp.zeros((bp, 2, N_HEADS_M, HEAD_DIM_M), jnp.float32)
    zm = jnp.full((bp, 2, N_HEADS_M), NEG, jnp.float32)
    xp, xs = x_prompt, x_sample
    Cs, ns, ms = [], [], []
    for l in range(DEPTH):
        lw = (g_norm1[l], w_in[l], b_in[l], gn_gain[l], w_pool_grp[l], pool_scale[l], w_proj_a[l],
              w_proj_b[l], w_out[l], g_norm2[l], w_router_grp[l], b_router_grp[l], w_router_exp[l],
              b_router_exp[l], w_exp_gate[l], w_exp_up[l], w_exp_down[l])
        mod_ctx = jax.nn.silu(c_ctx)[None, :] @ w_mod[l] + b_mod[l]
        mod_lat = jax.nn.silu(c) @ w_mod[l] + b_mod[l]
        xp, C_l, n_l, m_l = _layer(xp, mod_ctx, zC, zn, zm, None, *lw)
        Cs.append(C_l); ns.append(n_l); ms.append(m_l)
        xs, _, _, _ = _layer(xs, mod_lat, state_C[:, l], state_n[:, l], state_m[:, l], rows, *lw)
    new_state_C = jnp.stack(Cs, axis=1)
    new_state_n = jnp.stack(ns, axis=1)
    new_state_m = jnp.stack(ms, axis=1)
    y_prompt = _rmsnorm(xp, g_final)
    y_sample = _rmsnorm(xs, g_final)
    return (y_prompt, y_sample, new_state_C, new_state_n, new_state_m)


_drawn_inputs = setup_inputs


def setup_inputs(seed=0):
    import zlib

    import numpy as np

    out = dict(_drawn_inputs(seed))
    spreads = {}
    factors = {'state_C': 5.872,
     'state_n': 8.0,
     'state_m': 8.0,
     'gn_gain': 8.0,
     'pool_scale': 3.068,
     'g_norm2': 4.693,
     'b_router_grp': 8.0,
     'b_router_exp': 8.0,
     'g_final': 3.116}
    for name, (base, spread) in spreads.items():
        noise = np.random.default_rng([zlib.crc32(name.encode()), seed]).standard_normal(out[name].shape)
        drawn = base * np.exp(spread * noise) if base else spread * noise
        out[name] = __import__('jax').numpy.asarray(drawn.astype(out[name].dtype))
    for name, factor in factors.items():
        out[name] = (out[name] * factor).astype(out[name].dtype)
    return out
```

```python
import concourse.bass as bass
from concourse import mybir
from contextlib import ExitStack
import numpy as np

F32 = mybir.dt.float32
F32R = mybir.dt.float32r
I32 = mybir.dt.int32
ALU = mybir.AluOpType
ACT = mybir.ActivationFunctionType
AX = mybir.AxisListType.X

P = 128
D = 1024
KT = D // P
TC, TL = 128, 512
T = TC + TL
NT = T // P
NL = TL // P
HALF = T // 2
H = 8
DH = 128
V1 = DH + 1
R16 = 2 * H
GP = 48
WIN = (2, 4, 8, 16)
NG = len(WIN)
GW, GR = 64, TL // 64
PAD = 8
CH = 2048
NRAW = 4
EG, EE = 4, 4
NE = EG * EE
DE = 512
FT = DE // P
SLOTS = 128
ROUNDS = -(-T // SLOTS)
ECH = 6
EPS = 1e-6
NEG = -1e30
SCALE = DH ** -0.5

N_MOD1 = 8
N_QK, N_V, N_U = 8, 4, 2
N_MOD2 = 16
N_O, N_G, N_B, N_A, N_OUT = 4, 8, 2, 4, 4
N_DENSE = N_MOD1 + N_QK + N_V + N_U + N_MOD2 + N_O + N_G + N_B + N_A + N_OUT
AT_QK = N_MOD1
AT_V = AT_QK + N_QK
AT_U = AT_V + N_V
AT_MOD2 = AT_U + N_U
AT_O = AT_MOD2 + N_MOD2
AT_G = AT_O + N_O
AT_B = AT_G + N_G
AT_A = AT_B + N_B
AT_OUT = AT_A + N_A

C_ID, C_ONE, C_FWD, C_BWD, C_STRICT, C_IOTA, C_NEGF, C_NEGB = (P * i for i in range(8))
C_MF = 8 * P
C_MB = C_MF + 1
C_WT = C_MF + 2
C_THR = C_WT + 4 * NT
C_EPS = C_THR + ROUNDS
C_END = C_EPS + 1

B_IN, B_MOD, G_1, G_2, G_F, G_N, P_S, W_END = 0, 52, 100, 108, 116, 124, 132, 136


class Steps:

    def __init__(self, eng, sem):
        self.eng, self.sem, self.base, self.n = eng, sem, 0, 0

    def on(self, ins):
        ins.then_inc(self.sem, 1)
        self.n += 1

    def wait(self):
        self.eng.wait_ge(self.sem, self.base + self.n)

    def do(self, ins):
        self.on(ins)
        self.wait()

    def enter(self, base):
        self.base, self.n = base, 0


def layer_kernel(nc, x_d, c_d, wst_d, wg_d, bg_d, col_d, wpool_d, wr_d, br_d, st_d, m0_d, cst_d,
                 rcnt_d, wexp_d, y_d, so_d, mo_d):
    ctx = ExitStack()
    with ctx:
        base = -(-nc.sbuf_base // 32) * 32
        ctx.enter_context(nc.sbuf_tensor("arena", [P, 207 * 256], F32))

        def at(name, kib, shape, dt=F32):
            return nc.alloc_sbuf_tensor_at(name, shape, dt, offset=base + int(kib * 1024))

        def sem(name):
            return ctx.enter_context(nc.semaphore(name))

        cst = at("cst", 0, [P, C_END])
        ident, ones = cst[:, C_ID:C_ID + P], cst[:, C_ONE:C_ONE + P]
        iota = cst[:, C_IOTA:C_IOTA + P]
        eps = cst[:, C_EPS:C_EPS + 1]
        col = at("col", 4.25, [P, W_END])
        mod = at("mod", 4.875, [P, 48, 2])
        gain = at("gain", 5.25, [P, KT, 2])
        cin = at("cin", 5.375, [P, KT, 2])
        csil = at("csil", 5.5, [P, KT, 2])
        half_gate = at("half_gate", 5.625, [P, KT, 2])
        half_gn = at("half_gn", 5.6875, [P, KT])
        a_tok = at("a_tok", 5.75, [P, NT, R16])
        wi_tok = at("wi_tok", 6.0625, [P, NT, R16])
        em_tok = at("em_tok", 6.375, [P, NT, R16])
        ws_tok = at("ws_tok", 6.6875, [P, R16])
        hss = at("hss", 6.75, [P, NT, H])
        rinv = at("rinv", 6.9375, [P, NT, 2])
        bg = at("bg", 7.0, [GP, 1])
        m0 = at("m0", 7.0625, [R16, 1])
        mlast = at("mlast", 7.125, [R16, 4])
        rounds_i = at("rounds_i", 7.1875, [1, 1], I32)
        wslot = at("wslot", 7.21875, [P, 1])
        wr = at("wr", 7.25, [P, KT, EG + NE])
        br = at("br", 7.875, [P, EG + NE])

        raw = [at(f"raw{s}", 8 + 8 * s, [P, CH]) for s in range(NRAW)]
        whi = [at(f"whi{s}", 40 + 16 * s, [P, CH], F32R) for s in range(2)]
        wlo = [at(f"wlo{s}", 48 + 16 * s, [P, CH], F32R) for s in range(2)]
        hhi = at("hhi", 72, [P, KT, T], F32R)
        hlo = at("hlo", 92, [P, KT, T], F32R)
        hn = at("hn", 112, [P, KT, T])
        xT = at("xT", 132, [P, KT, T])
        rstd = at("rstd", 172.5, [P, T])
        QK = at("QK", 112, [P, 2 * H, T])
        Vt = at("Vt", 152, [P, NT, H, V1])
        U = at("U", 172.75, [P, NG, T])
        TMP = 182.75
        wgr = at("wgr", TMP, [P, KT, GP])
        wgh = at("wgh", TMP + 1.5, [P, KT, GP], F32R)
        wgl = at("wgl", TMP + 3, [P, KT, GP], F32R)
        vst = [at(f"vst{s}", TMP + 2.5 * s, [P, T]) for s in range(2)]
        gI, gF, gA, gB, gC, gOne = (at(n, TMP + 5 + 2.5 * i, [R16, T])
                                    for i, n in enumerate(("gI", "gF", "gA", "gB", "gC", "gOne")))
        negM = at("negM", TMP + 22.5, [R16, T])
        DG = [at(f"DG{d}", 40 + 2.5 * d, [P, NT, P]) for d in range(2)]
        OFF = [at(f"OFF{d}", 45 + 3 * d, [P, 6 * P]) for d in range(2)]
        S = at("S", 51, [P, 20 * P])
        num = at("num", 61, [P, NT, 2, V1])
        mrow = [at(f"mrow{d}", 66.25 + 2.5 * d, [R16, T]) for d in range(2)]
        qst = [at(f"qst{s}", TMP + 5 * s, [P, T]) for s in range(2)]
        kst = [at(f"kst{s}", TMP + 2.5 + 5 * s, [P, T]) for s in range(2)]
        stC = at("stC", TMP + 10, [P, 2, H, V1])
        qcw = at("qcw", TMP + 18.125, [P, 2, V1])
        kw = [at(f"kw{d}", TMP + 19.25 + 0.5 * d, [P, P]) for d in range(2)]
        O = at("O", 132, [P, KT, T])
        Y = at("Y", 112, [P, KT, T])
        TH = at("TH", 132, [P, 2 * KT, T])
        XP = [at(f"XP{i}", TMP + 2.5 * i, [P, GR, GW + 2 * PAD]) for i in range(2)]
        RP = [at(f"RP{i}", TMP + 5 + 3.75 * i, [P, 2 * GR - 1, GW]) for i in range(2)]
        rcnt = at("rcnt", TMP + 12.5, [P, NG, T])
        CP = [at(f"CP{i}", TMP + 22.5 + 0.625 * i, [P, TC + 2 * PAD]) for i in range(2)]
        ybh = at("ybh", TMP, [P, NG, T], F32R)
        ybl = at("ybl", TMP + 10, [P, NG, T], F32R)
        wpool = at("wpool", TMP + 22.5, [P, NG, P])
        mgh = at("mgh", 112, [P, KT, T], F32R)
        mgl = at("mgl", TMP, [P, KT, T], F32R)
        xres = at("xres", 132, [P, KT, T])
        n2 = at("n2", 152, [P, KT, T])
        h2 = at("h2", 112, [P, KT, T])
        rs2 = at("rs2", 192.5, [P, T])
        eraw = [at(f"eraw{s}", 72 + 8 * s, [P, CH]) for s in range(3)]
        ehi = [at(f"ehi{s}", 8 + 16 * s, [P, CH], F32R) for s in range(3)]
        elo = [at(f"elo{s}", 16 + 16 * s, [P, CH], F32R) for s in range(3)]
        sel = at("sel", 56, [P, NT, SLOTS], F32R)
        selT = at("selT", 58.5, [P, T], F32R)
        th = at("th", 61, [P, DE])
        act_ = at("act", 63, [P, DE])
        aTh = at("aTh", 65, [P, FT, SLOTS], F32R)
        aTl = at("aTl", 67, [P, FT, SLOTS], F32R)
        xgh = at("xgh", 96, [P, KT, SLOTS], F32R)
        xgl = at("xgl", 100, [P, KT, SLOTS], F32R)
        yh = at("yh", 104, [P, D], F32R)
        yl = at("yl", 108, [P, D], F32R)
        tkh = at("tkh", 152, [P, NT, D], F32R)
        tkl = at("tkl", 172, [P, NT, D], F32R)
        wtok = at("wtok", 195, [P, NT, NE])
        rank = at("rank", 195.5, [P, NT, NE + 1])
        RT = 196
        lg = at("lg", RT, [P, NT, EG + NE])
        r5 = at("r5", RT + 0.5, [P, 12, NT])
        goh = at("goh", RT + 1, [P, NT, EG])
        les = at("les", RT + 1.125, [P, NT, EE])
        o1 = at("o1", RT + 1.25, [P, NT, EE])
        o2 = at("o2", RT + 1.375, [P, NT, EE])
        t4 = at("t4", RT + 1.5, [P, NT, EE])
        t5 = at("t5", RT + 1.625, [P, NT, EE])
        t16 = at("t16", RT + 1.75, [P, NT, EG, EE])
        am = at("am", RT + 2.25, [P, NT, NE])
        thr = at("thr", RT + 2.75, [P, 8])
        mean = at("mean", RT + 3, [P, T])
        yout = at("yout", 152, [P, KT, T])

        ps = ctx.enter_context(nc.psum_tensor("ps", [P, 8, 512], F32))

        def pair(e):
            return ps[:, 2 * (e % 4):2 * (e % 4) + 2, 0:HALF]

        def halves(ap):
            return ap.rearrange("p (a n) -> p a n", a=2)

        def f32(t):
            return t.bitcast(F32)

        d_const, d_x, d_st, d_pool, d_wp, d_xr = (sem(n) for n in (
            "d_const", "d_x", "d_st", "d_pool", "d_wp", "d_xr"))
        raw_full = [sem(f"raw_full{s}") for s in range(NRAW)]
        raw_free = [sem(f"raw_free{s}") for s in range(NRAW)]
        hi_ready = sem("hi_ready")
        blk_ready, blk_free = sem("blk_ready"), sem("blk_free")
        s_csil, s_sq, s_ssq, s_rstd, s_hn, s_hhi, s_hlo = (sem(n) for n in (
            "s_csil", "s_sq", "s_ssq", "s_rstd", "s_hn", "s_hhi", "s_hlo"))
        s_wgh, s_wgl, s_gps, s_gate, s_lsg, s_grow, s_gtok = (sem(n) for n in (
            "s_wgh", "s_wgl", "s_gps", "s_gate", "s_lsg", "s_grow", "s_gtok"))
        s_init = sem("s_init")
        s_mrow, s_qst, s_kst, s_m, s_kw, s_sc, s_sev, s_tdg, s_exp, s_p, s_pv, s_nm = (
            sem(n) for n in ("s_mrow", "s_qst", "s_kst", "s_m", "s_kw", "s_sc", "s_sev", "s_tdg",
                             "s_exp", "s_p", "s_pv", "s_nm"))
        m_free, qc5_free, qc1_free, pv6_free, pv7_free = (sem(n) for n in (
            "m_free", "qc5_free", "qc1_free", "pv6_free", "pv7_free"))
        s_o, s_hd, s_yh, s_yl = (sem(n) for n in ("s_o", "s_hd", "s_yh", "s_yl"))
        s_pool, s_ybh, s_mg, s_mgh, s_mgl, s_xr = (sem(n) for n in (
            "s_pool", "s_ybh", "s_mg", "s_mgh", "s_mgl", "s_xr"))
        s_sq2, s_ssq2, s_rs2, s_h2, s_lg, s_ex, s_am, s_rk, s_tkp, s_tk, s_tkl, s_cnt = (sem(n) for n in (
            "s_sq2", "s_ssq2", "s_rs2", "s_h2", "s_lg", "s_ex", "s_am", "s_rk", "s_tkp", "s_tk",
            "s_tkl", "s_cnt"))
        e_full = [sem(f"e_full{s}") for s in range(3)]
        e_free = [sem(f"e_free{s}") for s in range(3)]
        e_hi, e_mm = sem("e_hi"), sem("e_mm")
        e_th, e_act, e_sel, e_selp, e_selT, e_cmb, e_add, e_gat, e_aTp = (sem(n) for n in (
            "e_th", "e_act", "e_sel", "e_selp", "e_selT", "e_cmb", "e_add", "e_gat", "e_aTp"))
        e_xgh, e_xgl, e_aTh, e_aTl, e_yh, e_yl = (sem(n) for n in (
            "e_xgh", "e_xgl", "e_aTh", "e_aTl", "e_yh", "e_yl"))
        s_round = sem("s_round")
        s_sqf, s_ssf, s_rsf, s_out = sem("s_sqf"), sem("s_ssf"), sem("s_rsf"), sem("s_out")
        s_yo, s_sto = sem("s_yo"), sem("s_sto")
        a_steps, v_steps, g_steps = sem("act_steps"), sem("dve_steps"), sem("pool_steps")
        v_head, v_item, a_head = sem("dve_head_steps"), sem("dve_item_steps"), sem("act_loop_steps")

        block = ctx.enter_context(nc.Block())
        E_V, E_G8, E_U, E_O, E_Y, E_TH, E_PL, E_B, E_A, E_OUT, E_END = (
            16, 32, 33, 37, 45, 53, 69, 73, 81, 89, 97)
        CV, CU, CO, CTH, CB, CA, COUT = 8, 12, 14, 18, 26, 28, 32
        OFF_F, OFF_B = (0, 3 * P, 5 * P), (0, P, 3 * P)
        HEAD_STEPS, ITEM_STEPS = 20, 21

        @block.sync
        def _(sp):
            for s in range(NRAW):
                sp.sem_inc(raw_free[s], 1)
            for s in range(3):
                sp.sem_inc(e_free[s], 1)
            with sp.Fori(0, N_DENSE // NRAW) as i:
                for s in range(NRAW):
                    sp.wait_ge(raw_free[s], i + 1)
                    sp.dma_start(raw[s][:, :], wst_d[i * NRAW + s, :, :]).then_inc(raw_full[s], 16)
            sp.wait_ge(blk_ready, E_OUT)
            for s in range(3):
                sp.dma_start(eraw[s][:, :], wexp_d[0, s, :, :]).then_inc(e_full[s], 16)
            sp.wait_ge(s_cnt, 1)
            rounds = sp.value_load(rounds_i[0:1, 0:1], min_val=1, max_val=ROUNDS)
            with sp.Fori(0, rounds) as r:
                with sp.Fori(0, NE) as e:
                    n = r * NE + e
                    for s in range(3):
                        sp.wait_ge(e_free[s], 2 * n + 2)
                        sp.dma_start(eraw[s][:, :], wexp_d[e, 3 + s, :, :]).then_inc(e_full[s], 16)
                    for s in range(3):
                        sp.wait_ge(e_free[s], 2 * n + 3)
                        sp.dma_start(eraw[s][:, :], wexp_d[e + 1, s, :, :])\
                          .then_inc(e_full[s], 16)
            for k in range(KT):
                sp.wait_ge(s_yo, k + 1)
                sp.dma_start(y_d[:, k, :], yout[:, k, :]).then_inc(s_out, 16)
            sp.wait_ge(s_out, 16 * KT)
            sp.wait_ge(s_sto, 32)

        @block.gpsimd
        def _(gp):
            st = Steps(gp, g_steps)
            gp.memset(gOne[:, :], 1.0).then_inc(s_init, 1)
            gp.memset(Vt[:, :, :, DH:V1], 1.0).then_inc(s_init, 1)
            gp.wait_ge(s_gtok, 1)
            gp.dma_start(stC[:, :, :, :], st_d).then_inc(d_st, 16)
            gp.wait_ge(blk_ready, E_O)
            with gp.Fori(0, H) as h:
                gp.wait_ge(m_free, h + 1)
                for d in range(2):
                    gp.tensor_tensor(mrow[d][:, :], negM[:, :],
                                     cst[0:R16, bass.ds(h + (C_ID + d * H), 1)].broadcast_to([R16, T]),
                                     ALU.mult).then_inc(s_mrow, 1)
            gp.wait_ge(pv7_free, 1 + 3 * H)
            gp.dma_start(so_d, stC[:, :, :, :]).then_inc(s_sto, 16)
            gp.dma_start(mo_d, mlast[:, 2:3]).then_inc(s_sto, 16)
            gp.wait_ge(s_sto, 32)
            gp.dma_start(rcnt[:, :, :], rcnt_d).then_inc(d_pool, 16)
            gp.wait_ge(s_nm, H)
            gp.wait_ge(d_pool, 16)
            for g, w in enumerate(WIN):
                st.on(gp.memset(XP[0][:, :, :], 0.0))
                st.on(gp.memset(RP[0][:, :, :], 0.0))
                st.do(gp.memset(CP[0][:, :], 0.0))
                st.do(gp.tensor_copy(XP[0][:, :, PAD:PAD + GW],
                                     U[:, g, TC:T].rearrange("p (r c) -> p r c", c=GW)))
                n, s, src = GW + 2 * PAD, 1, 0
                while s < w:
                    n -= s
                    st.do(gp.tensor_tensor(XP[1 - src][:, :, 0:n], XP[src][:, :, 0:n],
                                           XP[src][:, :, s:s + n], ALU.add))
                    s, src = 2 * s, 1 - src
                xs = XP[src][:, :, PAD - w // 2:PAD - w // 2 + GW]
                if w // 2 >= GR:
                    st.do(gp.tensor_tensor(RP[0][:, 0:4, :], xs[:, 0:4, :], xs[:, 4:8, :], ALU.add))
                    st.do(gp.tensor_tensor(RP[1][:, 0:2, :], RP[0][:, 0:2, :], RP[0][:, 2:4, :],
                                           ALU.add))
                    st.do(gp.tensor_tensor(RP[0][:, 0:1, :], RP[1][:, 0:1, :], RP[1][:, 1:2, :],
                                           ALU.add))
                    res = RP[0][:, 0:1, :].broadcast_to([P, GR, GW])
                else:
                    st.do(gp.tensor_copy(RP[0][:, w // 2:w // 2 + GR, :], xs))
                    n, s, src = GR + w - 1, 1, 0
                    while s < w:
                        n -= s
                        st.do(gp.tensor_tensor(RP[1 - src][:, 0:n, :], RP[src][:, 0:n, :],
                                               RP[src][:, s:s + n, :], ALU.add))
                        s, src = 2 * s, 1 - src
                    res = RP[src][:, 0:GR, :]
                mean_l = XP[0][:, :, 0:GW]
                st.do(gp.tensor_tensor(mean_l, res, rcnt[:, g, TC:T].rearrange(
                    "p (r c) -> p r c", c=GW), ALU.mult))
                ul = U[:, g, TC:T].rearrange("p (r c) -> p r c", c=GW)
                st.do(gp.tensor_tensor(ul, mean_l, ul, ALU.subtract))
                st.do(gp.tensor_copy(CP[0][:, PAD:PAD + TC], U[:, g, 0:TC]))
                n, s, src = TC + 2 * PAD, 1, 0
                while s < w:
                    n -= s
                    st.do(gp.tensor_tensor(CP[1 - src][:, 0:n], CP[src][:, 0:n],
                                           CP[src][:, s:s + n], ALU.add))
                    s, src = 2 * s, 1 - src
                cs = CP[src][:, PAD - w // 2:PAD - w // 2 + TC]
                st.do(gp.tensor_tensor(CP[1 - src][:, 0:TC], cs, rcnt[:, g, 0:TC], ALU.mult))
                st.do(gp.tensor_tensor(U[:, g, 0:TC], CP[1 - src][:, 0:TC], U[:, g, 0:TC],
                                       ALU.subtract))
            gp.dma_start(wpool[:, :, :], wpool_d).then_inc(d_wp, 16)
            gp.sem_inc(s_pool, 1)
            gp.wait_ge(s_mgl, KT)
            gp.dma_start(xres[:, :, :], x_d).then_inc(d_xr, 16)

        @block.scalar
        def _(act):
            act.dma_start(xT[:, :, :], x_d).then_inc(d_x, 16)
            smalls = [(cst[:, :], cst_d), (col[:, :], col_d), (cin[:, :, :], c_d),
                      (wgr[:, :, :], wg_d), (bg[:, :], bg_d), (m0[:, :], m0_d),
                      (wr[:, :, :], wr_d), (br[:, :], br_d)]
            for dst, src in smalls:
                act.dma_start(dst, src).then_inc(d_const, 16)
            act.sem_inc(blk_free, 4)
            st = Steps(act, a_steps)

            def split_hi(slot, use, p):
                act.wait_ge(raw_full[slot], (use + 1) * 16)
                act.activation(whi[p][:, :], raw[slot][:, :], ACT.Copy).then_inc(hi_ready, 1)

            def inv_rms(out, in_, n, sem_):
                st.do(act.activation(out, in_, ACT.Ln, bias=eps, scale=1.0 / n))
                act.activation(out, out, ACT.Exp, scale=-0.5).then_inc(sem_, 1)

            act.wait_ge(d_const, 16 * len(smalls))
            act.activation(csil[:, :, :], cin[:, :, :], ACT.Tanh, scale=0.5).then_inc(s_csil, 1)
            act.activation(wgh[:, :, :], wgr[:, :, :], ACT.Copy).then_inc(s_wgh, 1)
            act.wait_ge(d_x, 16)
            for k in range(KT):
                act.activation(hn[:, k, :], xT[:, k, :], ACT.Square).then_inc(s_sq, 1)
            act.wait_ge(s_ssq, 1)
            inv_rms(halves(rstd[:, :]), ps[:, 0:2, 0:HALF], D, s_rstd)
            for k in range(KT):
                act.wait_ge(s_hn, k + 1)
                act.activation(hhi[:, k, :], hn[:, k, :], ACT.Copy).then_inc(s_hhi, 1)
            split_hi(AT_QK % NRAW, AT_QK // NRAW, 0)
            act.wait_ge(s_gps, 1)
            act.activation(halves(gI[:, :]), ps[0:R16, 6:8, 0:HALF], ACT.Identity,
                           bias=bg[0:R16, :]).then_inc(s_gate, 1)
            act.activation(halves(gF[:, :]), ps[32:32 + R16, 6:8, 0:HALF], ACT.Identity,
                           bias=bg[32:32 + R16, :]).then_inc(s_gate, 1)
            act.wait_ge(s_lsg, 1)
            st.do(act.activation(gC[:, :], gC[:, :], ACT.Exp, scale=-1.0))
            act.activation(gC[:, :], gC[:, :], ACT.Ln, bias=cst[0:R16, C_ONE:C_ONE + 1])\
               .then_inc(s_gate, 1)

            with act.Fori(0, N_QK // NRAW) as i:
                for j in range(NRAW):
                    split_hi((j + 1) % NRAW, i + AT_QK // NRAW + (j + 1) // NRAW, (j + 1) % 2)
                    for b in range(2):
                        e = 2 * j + b
                        act.wait_ge(blk_ready, i * 8 + e + 1)
                        act.activation(halves(QK[:, i * 8 + e, :]), pair(e), ACT.Identity,
                                       bias=col[:, bass.ds(i * 8 + e + B_IN, 1)])\
                           .then_inc(blk_free, 1)
            def v_rows(v, e):
                act.wait_ge(blk_ready, e + 1)
                st.on(act.activation(Vt[:, 0:3, v, 0:DH], ps[:, 2 * (e % 4), 0:3 * P].rearrange(
                    "p (t n) -> p t n", n=P), ACT.Copy))
                act.activation(Vt[:, 3:5, v, 0:DH], ps[:, 2 * (e % 4) + 1, 0:2 * P].rearrange(
                    "p (t n) -> p t n", n=P), ACT.Copy).then_inc(blk_free, 1)

            e = E_V
            for v in range(H):
                if v % 2 == 0:
                    c = AT_V + v // 2 + 1
                    split_hi(c % NRAW, c // NRAW, (v // 2 + 1) % 2)
                act.wait_ge(blk_ready, e + 1)
                act.activation(halves(vst[v % 2][:, :]), pair(e), ACT.Identity,
                               bias=col[:, 16 + v:17 + v]).then_inc(blk_free, 1)
                e += 1
                if v:
                    v_rows(v - 1, e)
                    e += 1
            v_rows(H - 1, e)
            assert e + 1 == E_G8
            act.wait_ge(blk_ready, E_G8 + 1)
            gps = ps[:, 2 * (E_G8 % 4), :]
            st.on(act.activation(a_tok[:, :, :].rearrange("p t r -> p (t r)"), gps[:, 0:80], ACT.Copy))
            st.on(act.activation(wi_tok[:, 1:NT, :].rearrange("p t r -> p (t r)"), gps[:, 80:144],
                                 ACT.Exp))
            st.on(act.activation(em_tok[:, :, :].rearrange("p t r -> p (t r)"), gps[:, 144:224],
                                 ACT.Exp))
            act.activation(ws_tok[:, :], gps[:, 224:240], ACT.Exp).then_inc(blk_free, 1)
            act.wait_ge(blk_free, 4 + E_U)
            act.activation(ws_tok[:, :], ws_tok[:, :], ACT.Copy, scale=SCALE).then_inc(s_gtok, 1)
            for j in range(N_U):
                if j + 1 < N_U:
                    c = AT_U + j + 1
                    split_hi(c % NRAW, c // NRAW, (j + 1) % 2)
                for b in range(2):
                    e = E_U + 2 * j + b
                    act.wait_ge(blk_ready, e + 1)
                    act.activation(halves(U[:, 2 * j + b, :]), pair(e), ACT.Identity,
                                   bias=col[:, 24 + 2 * j + b:25 + 2 * j + b]).then_inc(blk_free, 1)

            act.wait_ge(s_gtok, 1)
            with act.Fori(0, H // 2) as i:
                for hp in range(2):
                    h = i * 2 + hp
                    act.activation(kst[hp][:, :], QK[:, h + H, :], ACT.Copy).then_inc(s_kst, 1)

                    def off_exp(d, j, o, t0, n):
                        st_h.on(act.activation(OFF[d][:, o:o + n], ps[:, 2 + d, t0:t0 + n], ACT.Exp,
                                               bias=a_tok[:, j + 1, bass.ds(h + d * H, 1)]))

                    def s_out(j):
                        act.wait_ge(s_sc, h * 5 + j + 2)
                        b = (j + 1) % 2
                        o, n = (2048, P) if j < 0 else (j * TL, TL)
                        act.activation(S[:, o:o + n], ps[:, b, 0:n], ACT.Copy, scale=SCALE)\
                           .then_inc(s_sev, 1)

                    st_h = Steps(act, a_head)
                    s_out(-1)
                    s_out(0)
                    act.wait_ge(s_tdg, h * 2 + 1)
                    for j in range(3):
                        off_exp(0, j, OFF_F[j], (j + 1) * P, (3 - j) * P)
                    s_out(1)
                    act.wait_ge(s_tdg, h * 2 + 2)
                    for j in range(1, 4):
                        off_exp(1, j, OFF_B[j - 1], 0, j * P)
                    for d in range(2):
                        act.activation(kw[d][:, :], ps[:, 4, 2 * P:3 * P], ACT.Copy,
                                       scale=ws_tok[:, bass.ds(h + d * H, 1)]).then_inc(s_kw, 1)
                    s_out(2)
                    s_out(3)
                    for d in range(2):
                        act.activation(DG[d][:, :, :], DG[d][:, :, :], ACT.Exp).then_inc(s_exp, 1)
                    act.wait_ge(s_pv, h * 6 + 6)
                    act.activation(stC[:, :, h, :], ps[:, 7, 0:2 * V1].rearrange(
                        "p (d n) -> p d n", n=V1), ACT.Copy).then_inc(pv7_free, 1)

            act.wait_ge(s_nm, H)
            split_hi(AT_O % NRAW, AT_O // NRAW, 0)
            for j in range(N_O):
                c = AT_O + j + 1
                split_hi(c % NRAW, c // NRAW, (j + 1) % 2)
                for b in range(2):
                    e, f = E_O + 2 * j + b, 2 * j + b
                    act.wait_ge(blk_ready, e + 1)
                    act.activation(halves(O[:, f, :]), pair(e), ACT.Tanh, scale=0.5,
                                   bias=col[:, 28 + f:29 + f]).then_inc(blk_free, 1)
                if j == 1:
                    act.wait_ge(s_hd, 1)
                    inv_rms(hss[:, :, :], hss[:, :, :], DH, s_o)
            act.wait_ge(blk_free, 4 + E_TH)
            with act.Fori(0, N_G // NRAW) as i:
                for j in range(NRAW):
                    c = AT_G + j + 1
                    split_hi(c % NRAW, i + c // NRAW, (j + 1) % 2)
                    for b in range(2):
                        f = 2 * j + b
                        act.wait_ge(blk_ready, i * 8 + E_TH + f + 1)
                        act.activation(halves(TH[:, i * 8 + f, :]), pair(E_TH + f), ACT.Tanh,
                                       scale=0.5, bias=col[:, bass.ds(i * 8 + 36 + f, 1)])\
                           .then_inc(blk_free, 1)
            for g in range(NG):
                act.wait_ge(blk_ready, E_PL + g + 1)
                act.activation(halves(ybh[:, g, :]), pair(E_PL + g), ACT.Copy,
                               scale=col[:, P_S + g:P_S + g + 1]).then_inc(s_ybh, 1)
            split_hi((AT_B + 1) % NRAW, (AT_B + 1) // NRAW, 1)
            for k in range(KT):
                act.activation(hhi[:, k, :], Y[:, k, :], ACT.Copy, scale=half_gn[:, k:k + 1])\
                   .then_inc(s_yh, 1)
            done = [E_B + 4, E_B + 8] + [E_A + 2 * j + 2 for j in range(6)]
            for j in range(N_A + N_OUT):
                c = AT_A + j
                act.wait_ge(blk_ready, done[j])
                split_hi(c % NRAW, c // NRAW, j % 2)
                if 2 <= j < 2 + N_A:
                    if j == 2:
                        act.wait_ge(s_yl, KT)
                    for k in (2 * j - 4, 2 * j - 3):
                        act.wait_ge(s_mg, k + 1)
                        act.activation(mgh[:, k, :], TH[:, k, :], ACT.Copy).then_inc(s_mgh, 1)
            for k in range(KT):
                act.wait_ge(s_xr, k + 1)
                act.activation(n2[:, k, :], xres[:, k, :], ACT.Square).then_inc(s_sq2, 1)

            def expert_hi(s, full):
                act.wait_ge(e_full[s], full * 16)
                act.activation(ehi[s][:, :], eraw[s][:, :], ACT.Copy).then_inc(e_hi, 1)

            act.wait_ge(blk_ready, E_END)
            for s in range(3):
                expert_hi(s, 1)
            act.wait_ge(s_ssq2, 1)
            inv_rms(halves(rs2[:, :]), ps[:, 0:2, 0:HALF], D, s_rs2)
            act.wait_ge(s_ex, 1)
            act.activation(t4[:, :, :], t4[:, :, :], ACT.Exp).then_inc(s_lg, 1)
            act.wait_ge(s_ex, 2)
            act.activation(r5[:, 4, :], r5[:, 4, :], ACT.Exp).then_inc(s_lg, 1)
            for t in range(NT):
                act.wait_ge(s_tkp, t + 1)
                act.activation(tkh[:, t, :].rearrange("p (a n) -> p a n", a=2),
                               ps[:, 4 + 2 * (t % 2):6 + 2 * (t % 2), :], ACT.Copy)\
                   .then_inc(s_tk, 1)

            act.wait_ge(e_gat, 1)
            act.activation(xgh[:, :, :].rearrange("p (a k) n -> p a (k n)", a=2), ps[:, 4:6, :],
                           ACT.Copy).then_inc(e_xgh, 1)
            act.wait_ge(s_cnt, 1)
            rounds = act.value_load(rounds_i[0:1, 0:1], min_val=1, max_val=ROUNDS)
            with act.Fori(0, rounds) as r:
                with act.Fori(0, NE) as e:
                    n = r * NE + e
                    for s in range(3):
                        act.wait_ge(e_mm, n * ECH + s + 1)
                        expert_hi(s, n * 2 + 2)
                    act.activation(th[:, :], ps[:, 0, :], ACT.Tanh, scale=0.5).then_inc(e_th, 1)
                    act.wait_ge(e_selp, n + 1)
                    act.wait_ge(e_cmb, n * KT + KT)
                    act.wait_ge(e_yl, n + 1)
                    st_i = Steps(act, a_head)
                    st_i.on(act.activation(selT[:, 0:512], ps[:, 2, :], ACT.Copy))
                    st_i.on(act.activation(selT[:, 512:T], ps[:, 3, 0:P], ACT.Copy))
                    act.activation(wslot[:, :], ps[:, 3, 2 * P:2 * P + 1], ACT.Copy)\
                       .then_inc(e_selT, 1)
                    act.wait_ge(e_mm, n * ECH + 4)
                    expert_hi(0, n * 2 + 3)
                    act.wait_ge(e_gat, n * 2 + 3)
                    act.activation(xgh[:, :, :].rearrange("p (a k) n -> p a (k n)", a=2),
                                   ps[:, 4:6, :], ACT.Copy).then_inc(e_xgh, 1)
                    act.wait_ge(e_aTp, n + 1)
                    act.activation(aTh[:, :, :].rearrange("p f n -> p (f n)"), ps[:, 0, :],
                                   ACT.Copy).then_inc(e_aTh, 1)
                    act.wait_ge(e_mm, n * ECH + 5)
                    expert_hi(1, n * 2 + 3)
                    act.wait_ge(e_mm, n * ECH + 6)
                    expert_hi(2, n * 2 + 3)
                    act.activation(yh[:, :].rearrange("p (a n) -> p a n", a=2), ps[:, 2:4, :],
                                   ACT.Copy, scale=wslot[:, :]).then_inc(e_yh, 1)
            for k in range(KT):
                act.wait_ge(e_add, rounds * (NE * KT) + k + 1)
                act.activation(h2[:, k, :], xres[:, k, :], ACT.Square).then_inc(s_sqf, 1)
            act.wait_ge(s_ssf, 1)
            inv_rms(halves(rs2[:, :]), ps[:, 0:2, 0:HALF], D, s_rsf)

        @block.vector
        def _(dve):
            st = Steps(dve, v_steps)

            def split_lo(slot, p, ci):
                dve.wait_ge(hi_ready, ci + 1)
                dve.tensor_tensor(wlo[p][:, :], raw[slot][:, :], f32(whi[p][:, :]), ALU.subtract)\
                   .then_inc(raw_free[slot], 1)

            def by(ap, shape):
                return ap.broadcast_to(shape)

            dve.sem_inc(m_free, 1)
            dve.sem_inc(qc5_free, 1)
            dve.sem_inc(qc1_free, 1)
            dve.sem_inc(pv6_free, 1)
            dve.sem_inc(pv7_free, 1)
            dve.wait_ge(d_const, 16 * 8)
            dve.wait_ge(s_csil, 1)
            st.do(dve.scalar_tensor_tensor(csil[:, :, :], csil[:, :, :], 1.0, cin[:, :, :],
                                           ALU.add, ALU.mult))
            dve.tensor_scalar(csil[:, :, :], csil[:, :, :], 0.5, None, ALU.mult).then_inc(s_csil, 1)
            st.on(dve.tensor_scalar(col[:, 28:52], col[:, 28:52], 0.5, None, ALU.mult))
            st.on(dve.tensor_scalar(half_gn[:, :], col[:, G_N:G_N + KT], 0.5, None, ALU.mult))
            dve.wait_ge(s_wgh, 1)
            dve.tensor_tensor(wgl[:, :, :], wgr[:, :, :], f32(wgh[:, :, :]), ALU.subtract)\
               .then_inc(s_wgl, 1)
            dve.wait_ge(raw_free[NRAW - 1], 1 + N_MOD1 // NRAW)
            st.do(dve.tensor_tensor(mod[:, 0:16, :], ps[:, 2, 0:32].rearrange("p (j c) -> p j c", c=2),
                                    by(col[:, B_MOD:B_MOD + 16].unsqueeze(2), [P, 16, 2]), ALU.add))
            st.do(dve.scalar_tensor_tensor(gain[:, :, :], mod[:, 8:16, :], 1.0,
                                           by(col[:, G_1:G_1 + KT].unsqueeze(2), [P, KT, 2]),
                                           ALU.add, ALU.mult))

            def modulate(dst, src, k, shift):
                return [dve.tensor_scalar(dst[:, k, a:b], src[:, k, a:b], gain[:, k, c:c + 1],
                                          mod[:, shift + k, c:c + 1], ALU.mult, ALU.add)
                        for c, a, b in ((0, 0, TC), (1, TC, T))]

            dve.wait_ge(s_rstd, 1)
            for k in range(KT):
                st.do(dve.tensor_tensor(hn[:, k, :], xT[:, k, :], rstd[:, :], ALU.mult))
                ctx_part, lat_part = modulate(hn, hn, k, 0)
                st.on(ctx_part)
                lat_part.then_inc(s_hn, 1)
            for k in range(KT):
                dve.wait_ge(s_hhi, k + 1)
                dve.tensor_tensor(hlo[:, k, :], hn[:, k, :], f32(hhi[:, k, :]), ALU.subtract)\
                   .then_inc(s_hlo, 1)
            split_lo(AT_QK % NRAW, 0, 0)
            dve.wait_ge(s_gate, 2)
            st.on(dve.tensor_scalar(gB[:, :], gF[:, :], 0.0, None, ALU.min))
            dve.scalar_tensor_tensor(gC[:, :], gF[:, :], -1.0, gF[:, :], ALU.mult, ALU.max)\
               .then_inc(s_lsg, 1)
            dve.wait_ge(s_gate, 3)
            st.wait()
            st.do(dve.tensor_tensor(gF[:, :], gB[:, :], gC[:, :], ALU.subtract))
            with dve.Fori(0, N_QK // NRAW) as i:
                for j in range(NRAW):
                    split_lo((j + 1) % NRAW, (j + 1) % 2, i * 4 + j + 1)
            split_lo((AT_V + 1) % NRAW, 1, CV + 1)

            mf, mb = cst[0:R16, C_MF:C_MF + 1], cst[0:R16, C_MB:C_MB + 1]
            segs = ((0, TC), (TC, T))

            def scans(dst_f, dst_b, src, initial, op):
                for (a, b), ini in zip(segs, initial):
                    st.on(dve.tensor_tensor_scan(dst_f[:, a:b], gOne[:, a:b], src[:, a:b], ini,
                                                 ALU.mult, op))
                    rev = slice(b - 1, a - 1 if a else None, -1)
                    st.on(dve.tensor_tensor_scan(dst_b[:, rev], gOne[:, rev], src[:, rev], ini,
                                                 ALU.mult, op))
                st.wait()

            def pick(dst, f, b):
                st.do(dve.tensor_scalar(f, f, mf, None, ALU.mult))
                st.do(dve.scalar_tensor_tensor(dst, b, mb, f, ALU.mult, ALU.add))

            dve.wait_ge(s_init, 1)
            scans(gA, gB, gF, (0.0, 0.0), ALU.add)
            pick(gF[:, :], gA[:, :], gB[:, :])
            split_lo((AT_V + 2) % NRAW, 0, CV + 2)
            st.do(dve.tensor_tensor(gA[:, :], gI[:, :], gF[:, :], ALU.subtract))
            scans(gB, gC, gA, (NEG, m0[:, :]), ALU.max)
            pick(gB[:, :], gB[:, :], gC[:, :])
            st.on(dve.tensor_scalar(negM[:, :], gB[:, :], -1.0, None, ALU.mult))
            st.on(dve.scalar_tensor_tensor(gC[:, :], gF[:, :], -1.0, gB[:, :], ALU.mult, ALU.subtract))
            for c, src in ((0, gB), (1, gF)):
                st.on(dve.tensor_scalar(mlast[:, 3:4], src[:, TC - 1:TC], mf, None, ALU.mult))
                st.wait()
                st.do(dve.scalar_tensor_tensor(mlast[:, c:c + 1], src[:, 0:1], mb, mlast[:, 3:4],
                                               ALU.mult, ALU.add))
            st.on(dve.tensor_tensor(mlast[:, 2:3], mlast[:, 0:1], mlast[:, 1:2], ALU.add))
            st.on(dve.tensor_scalar(gI[:, TC:T], negM[:, TC:T], m0[:, :], None, ALU.add))
            dve.tensor_scalar(gF[:, 0:TC], gA[:, 0:TC], mlast[:, 0:1], None, ALU.subtract)\
               .then_inc(s_grow, 1)
            split_lo((AT_V + 3) % NRAW, 1, CV + 3)
            split_lo(AT_U % NRAW, 0, CU)
            split_lo((AT_U + 1) % NRAW, 1, CU + 1)

            with dve.Fori(0, H // 2) as i:
                for hp in range(2):
                    h = i * 2 + hp
                    hs = Steps(dve, v_head)
                    hs.enter(h * HEAD_STEPS)
                    dve.tensor_copy(qst[hp][:, :], QK[:, h, :]).then_inc(s_qst, 1)
                    dve.wait_ge(s_m, h + 1)
                    for d in range(2):
                        neg = cst[:, (C_NEGF, C_NEGB)[d]:(C_NEGF, C_NEGB)[d] + P]
                        for t in range(NT):
                            src = ps[:, 4, d * P:(d + 1) * P] if t == 0 else \
                                ps[:, 2 + d, (t - 1) * P:t * P]
                            ins = dve.scalar_tensor_tensor(
                                DG[d][:, t, :], src, a_tok[:, t, bass.ds(h + d * H, 1)], neg,
                                ALU.add, ALU.min)
                            if t < NT - 1:
                                hs.on(ins)
                        ins.then_inc(s_tdg, 1)
                    c1 = AT_MOD2 + 2 * hp + 1
                    dve.wait_ge(raw_free[c1 % NRAW], i + c1 // NRAW + 2)
                    dve.tensor_tensor(mod[:, bass.ds(h * 4 + 16, 4), :],
                                      ps[:, 5, 0:8].rearrange("p (j c) -> p j c", c=2),
                                      by(col[:, bass.ds(h * 4 + B_MOD + 16, 4)].unsqueeze(2),
                                         [P, 4, 2]), ALU.add).then_inc(qc5_free, 1)
                    dve.wait_ge(s_sev, h * 5 + 5)
                    for d in range(2):
                        dve.wait_ge(s_exp, h * 2 + d + 1)
                        if d == 1:
                            dve.wait_ge(s_kw, h * 2 + 2)
                        dg = DG[d][:, 1:NT, :]
                        ins = dve.tensor_tensor(dg, dg, S[:, :].rearrange(
                            "p (j x) -> p j x", x=TL + P)[:, 0:NL, 0:P], ALU.mult)
                        if d == 1:
                            ins.then_inc(m_free, 1)
                        else:
                            hs.on(ins)
                        hs.on(dve.tensor_tensor(DG[d][:, 0, :], DG[d][:, 0, :], S[:, 2048:2048 + P],
                                                ALU.mult))
                        for j in (range(0, 3), range(1, 4))[d]:
                            o = (OFF_F, OFF_B)[d][j - d]
                            t0, n = ((j + 1) * P, (3 - j) * P) if d == 0 else (0, j * P)
                            ins = dve.tensor_tensor(OFF[d][:, o:o + n], OFF[d][:, o:o + n],
                                                    S[:, j * TL + t0:j * TL + t0 + n], ALU.mult)
                            if (d, j) == (1, 3):
                                ins.then_inc(s_p, 1)
                            else:
                                hs.on(ins)
                    dve.wait_ge(s_pv, h * 6 + 1)
                    dve.tensor_copy(num[:, 0, :, :], ps[:, 6, 0:2 * V1].rearrange(
                        "p (d n) -> p d n", n=V1)).then_inc(pv6_free, 1)
                    for t in range(NL):
                        dve.wait_ge(s_pv, h * 6 + 2 + t)
                        qc, qs = ((5, qc5_free), (1, qc1_free))[t % 2]
                        wi = wi_tok[:, t + 1, :].rearrange("p (d h) -> p d h", d=2)[:, :, bass.ds(h, 1)]
                        dve.tensor_tensor(num[:, t + 1, :, :], ps[:, qc, 0:2 * V1].rearrange(
                            "p (d n) -> p d n", n=V1), by(wi, [P, 2, V1]), ALU.mult).then_inc(qs, 1)
                        dve.wait_ge(qs, (h * 3 + 3 + t // 2) if qc == 5 else (h * 2 + 2 + t // 2))
                        pb, pf = ((7, pv7_free), (6, pv6_free))[t % 2]
                        dve.tensor_tensor(num[:, t + 1, :, :], num[:, t + 1, :, :],
                                          ps[:, pb, 0:2 * V1].rearrange("p (d n) -> p d n", n=V1),
                                          ALU.add).then_inc(pf, 1)
                    dve.wait_ge(pv6_free, h * 3 + 4)
                    dve.wait_ge(pv7_free, h * 3 + 3)
                    em = em_tok[:, :, :].rearrange("p t (d h) -> p t d h", d=2)[:, :, :, bass.ds(h, 1)]
                    den = num[:, :, :, DH:V1]
                    rv = rinv[:, :, :].unsqueeze(3)
                    hs.do(dve.scalar_tensor_tensor(rv, den, -1.0, den, ALU.mult, ALU.max))
                    hs.do(dve.tensor_tensor(rv, rv, em, ALU.max))
                    hs.do(dve.reciprocal(rinv[:, :, :], rinv[:, :, :]))
                    nn = num[:, :, :, 0:DH]
                    hs.do(dve.tensor_tensor(nn, nn, by(rinv[:, :, :].unsqueeze(3), [P, NT, 2, DH]),
                                            ALU.mult))
                    dve.wait_ge(s_pv, h * 6 + 6)
                    dve.tensor_tensor(Vt[:, :, h, 0:DH], num[:, :, 0, 0:DH], num[:, :, 1, 0:DH],
                                      ALU.add).then_inc(s_nm, 1)
                    assert hs.n == HEAD_STEPS, hs.n

            dve.wait_ge(s_nm, H)
            split_lo(AT_O % NRAW, 0, CO)
            split_lo((AT_O + 1) % NRAW, 1, CO + 1)
            tmp = Y[:, 0:2, :].rearrange("p a n -> p (a n)")[:, 0:H * DH].rearrange(
                "p (h n) -> p h n", n=DH)
            for t in range(NT):
                hv = Vt[:, t, :, 0:DH]
                st.do(dve.tensor_tensor(tmp, hv, hv, ALU.mult))
                ins = dve.tensor_reduce(hss[:, t, :], tmp, AX, ALU.add)
                if t < NT - 1:
                    st.do(ins)
                else:
                    ins.then_inc(s_hd, 1)
            split_lo((AT_O + 2) % NRAW, 0, CO + 2)
            split_lo((AT_O + 3) % NRAW, 1, CO + 3)
            dve.wait_ge(s_o, 1)
            for t in range(NT):
                hv = Vt[:, t, :, 0:DH]
                dve.tensor_tensor(hv, hv, by(hss[:, t, :].unsqueeze(2), [P, H, DH]), ALU.mult)\
                   .then_inc(s_hd, 1)
            split_lo(AT_G % NRAW, 0, CTH)
            for k in range(KT):
                e = E_Y + k
                dve.wait_ge(blk_free, 4 + E_Y)
                dve.wait_ge(blk_ready, e + 1)
                st.on(dve.scalar_tensor_tensor(Y[:, k, 0:3 * P], O[:, k, 0:3 * P], 1.0,
                                               ps[:, 2 * (e % 4), 0:3 * P], ALU.add, ALU.mult))
                dve.scalar_tensor_tensor(Y[:, k, 3 * P:T], O[:, k, 3 * P:T], 1.0,
                                         ps[:, 2 * (e % 4) + 1, 0:2 * P], ALU.add, ALU.mult)\
                   .then_inc(blk_free, 1)
            with dve.Fori(0, N_G // NRAW) as i:
                for j in range(NRAW):
                    split_lo((AT_G + j + 1) % NRAW, (j + 1) % 2, i * 4 + CTH + j + 1)
            for g in range(NG):
                dve.wait_ge(s_ybh, g + 1)
                dve.scalar_tensor_tensor(halves(ybl[:, g, :]), pair(E_PL + g),
                                         col[:, P_S + g:P_S + g + 1], halves(f32(ybh[:, g, :])),
                                         ALU.mult, ALU.subtract).then_inc(blk_free, 1)
            split_lo((AT_B + 1) % NRAW, 1, CB + 1)
            for k in range(KT):
                dve.wait_ge(s_yh, k + 1)
                dve.scalar_tensor_tensor(hlo[:, k, :], Y[:, k, :], half_gn[:, k:k + 1],
                                         f32(hhi[:, k, :]), ALU.mult, ALU.subtract).then_inc(s_yl, 1)
                e = E_B + k
                dve.wait_ge(blk_ready, e + 1)
                dve.scalar_tensor_tensor(halves(TH[:, k, :]), halves(TH[:, k, :]), 1.0, pair(e),
                                         ALU.add, ALU.mult).then_inc(blk_free, 1)
                if k in (3, 7):
                    split_lo((CA + k // 4 - CA + AT_A) % NRAW, (k // 4) % 2, CA + k // 4)
            dve.tensor_scalar(half_gate[:, :, :], mod[:, 16:24, :], 0.5, None, ALU.mult)\
               .then_inc(v_steps, 1)
            st.n += 1
            for k in range(KT):
                e = E_A + k
                dve.wait_ge(blk_free, 4 + E_B + k + 1)
                dve.wait_ge(blk_ready, e + 1)
                dve.scalar_tensor_tensor(halves(TH[:, KT + k, :]), halves(TH[:, KT + k, :]), 1.0,
                                         pair(e), ALU.add, ALU.mult).then_inc(blk_free, 1)
                dve.wait_ge(blk_free, 4 + e + 1)
                dve.tensor_tensor(TH[:, k, :], TH[:, k, :], TH[:, KT + k, :], ALU.add)\
                   .then_inc(s_mg, 1)
                if k % 2 == 1:
                    ci = CA + 2 + k // 2
                    split_lo((AT_A + 2 + k // 2) % NRAW, ci % 2, ci)
                    for kk in (k - 1, k):
                        dve.wait_ge(s_mgh, kk + 1)
                        dve.tensor_tensor(mgl[:, kk, :], TH[:, kk, :], f32(mgh[:, kk, :]),
                                          ALU.subtract).then_inc(s_mgl, 1)
            dve.wait_ge(d_xr, 16)
            st.wait()
            for k in range(KT):
                e = E_OUT + k
                dve.wait_ge(blk_ready, e + 1)
                pa, pb = ps[:, 2 * (e % 4), :], ps[:, 2 * (e % 4) + 1, :]
                for j, (c, src, a, b) in enumerate(((0, pa[:, 0:TC], 0, TC),
                                                    (1, pa[:, TC:HALF], TC, HALF),
                                                    (1, pb[:, 0:HALF], HALF, T))):
                    st.on(dve.scalar_tensor_tensor(xres[:, k, a:b], src, half_gate[:, k, c:c + 1],
                                                   xres[:, k, a:b], ALU.mult, ALU.add))
                st.wait()
                dve.sem_inc(blk_free, 1)
                dve.sem_inc(s_xr, 1)
                if k in (0, 2):
                    ci = COUT + 2 + k // 2
                    split_lo((AT_OUT + 2 + k // 2) % NRAW, ci % 2, ci)

            def expert_lo(s, ci):
                dve.wait_ge(e_hi, ci + 1)
                dve.tensor_tensor(elo[s][:, :], eraw[s][:, :], f32(ehi[s][:, :]), ALU.subtract)\
                   .then_inc(e_free[s], 1)

            st.do(dve.scalar_tensor_tensor(gain[:, :, :], mod[:, 32:40, :], 1.0,
                                           by(col[:, G_2:G_2 + KT].unsqueeze(2), [P, KT, 2]),
                                           ALU.add, ALU.mult))
            for s in range(3):
                expert_lo(s, s)
            dve.wait_ge(s_rs2, 1)
            for k in range(KT):
                st.do(dve.tensor_tensor(h2[:, k, :], xres[:, k, :], rs2[:, :], ALU.mult))
                ctx_part, lat_part = modulate(h2, h2, k, 24)
                st.on(ctx_part)
                lat_part.then_inc(s_h2, 1)
            dve.memset(f32(yh[:, :]), 0.0).then_inc(e_yh, 1)
            dve.memset(f32(yl[:, :]), 0.0).then_inc(e_yl, 1)
            dve.memset(f32(selT[:, :]), 0.0).then_inc(e_selT, 1)

            gm, se, v1, v2, ed, pw, wa, wb = (r5[:, i, :] for i in range(8))

            def over(ap, n):
                return by(ap.unsqueeze(2), [P, NT, n])

            def first_max(out, vals, mx):
                st.do(dve.tensor_tensor(t5[:, :, :], vals, over(mx, 4), ALU.is_equal))
                wt = cst[:, C_WT:C_WT + 4 * NT].rearrange("p (t n) -> p t n", n=4)
                st.do(dve.tensor_tensor(t5[:, :, :], t5[:, :, :], wt, ALU.mult))
                st.do(dve.tensor_reduce(r5[:, 8, :], t5[:, :, :], AX, ALU.max))
                st.do(dve.tensor_tensor(out, t5[:, :, :], over(r5[:, 8, :], 4), ALU.is_equal))

            dve.wait_ge(s_rk, 1)
            st.do(dve.tensor_tensor(lg[:, :, :], ps[:, 2, 0:NT * (EG + NE)].rearrange(
                "p (t n) -> p t n", t=NT), by(br[:, :].unsqueeze(1), [P, NT, EG + NE]), ALU.add))
            gl = lg[:, :, 0:EG]
            st.do(dve.tensor_reduce(gm, gl, AX, ALU.max))
            dve.tensor_tensor(t4[:, :, :], gl, over(gm, EG), ALU.subtract).then_inc(s_ex, 1)
            first_max(goh[:, :, :], gl, gm)
            le = lg[:, :, EG:].rearrange("p t (g e) -> p t g e", g=EG)
            st.do(dve.tensor_tensor(t16[:, :, :, :], le, by(goh[:, :, :].unsqueeze(3),
                                                            [P, NT, EG, EE]), ALU.mult))
            st.do(dve.tensor_reduce(les[:, :, :], t16[:, :, :, :].rearrange("p t g e -> p t e g"),
                                    AX, ALU.add))
            st.do(dve.tensor_reduce(v1, les[:, :, :], AX, ALU.max))
            first_max(o1[:, :, :], les[:, :, :], v1)
            st.do(dve.scalar_tensor_tensor(les[:, :, :], o1[:, :, :], NEG, les[:, :, :],
                                           ALU.mult, ALU.add))
            st.do(dve.tensor_reduce(v2, les[:, :, :], AX, ALU.max))
            dve.tensor_tensor(ed, v2, v1, ALU.subtract).then_inc(s_ex, 1)
            first_max(o2[:, :, :], les[:, :, :], v2)
            st.on(dve.tensor_tensor(t5[:, :, :], o1[:, :, :], o2[:, :, :], ALU.add))
            dve.wait_ge(s_lg, 2)
            st.wait()
            am4 = am[:, :, :].rearrange("p t (g e) -> p t g e", g=EG)
            gb = by(goh[:, :, :].unsqueeze(3), [P, NT, EG, EE])
            dve.tensor_tensor(am4, by(t5[:, :, :].unsqueeze(2), [P, NT, EG, EE]), gb, ALU.mult)\
               .then_inc(s_am, 1)
            st.do(dve.tensor_reduce(se, t4[:, :, :], AX, ALU.add))
            st.do(dve.scalar_tensor_tensor(pw, ed, 1.0, se, ALU.add, ALU.mult))
            st.do(dve.reciprocal(wa, pw))
            st.do(dve.tensor_scalar(wa, wa, 0.5, None, ALU.mult))
            st.do(dve.tensor_tensor(wb, wa, ed, ALU.mult))
            st.on(dve.tensor_tensor(o1[:, :, :], o1[:, :, :], over(wa, EE), ALU.mult))
            st.do(dve.tensor_tensor(o2[:, :, :], o2[:, :, :], over(wb, EE), ALU.mult))
            st.do(dve.tensor_tensor(o1[:, :, :], o1[:, :, :], o2[:, :, :], ALU.add))
            st.do(dve.tensor_tensor(wtok[:, :, :].rearrange("p t (g e) -> p t g e", g=EG),
                                    by(o1[:, :, :].unsqueeze(2), [P, NT, EG, EE]), gb, ALU.mult))
            dve.wait_ge(s_rk, 2)
            rk = ps[:, 3, 0:NT * NE].rearrange("p (t n) -> p t n", t=NT)
            st.do(dve.scalar_tensor_tensor(rank[:, :, 0:NE], rk, 1.0, am[:, :, :], ALU.add, ALU.mult))
            st.do(dve.tensor_scalar(rank[:, :, 0:NE], rank[:, :, 0:NE], -1.0, None, ALU.add))
            st.do(dve.tensor_scalar(rank[:, :, NE:NE + 1], rank[:, :, 0:1], -float(SLOTS), None,
                                    ALU.add))
            st.do(dve.tensor_reduce(thr[:, 5:6], ps[:, 3, NT * NE:NT * NE + NE], AX, ALU.max))
            st.do(dve.tensor_scalar(thr[:, 0:5], cst[:, C_THR:C_THR + ROUNDS], thr[:, 5:6], None,
                                    ALU.is_lt))
            st.do(dve.tensor_reduce(thr[:, 6:7], thr[:, 0:5], AX, ALU.add))
            dve.tensor_copy(rounds_i[0:1, 0:1], thr[0:1, 6:7]).then_inc(s_cnt, 1)
            for t in range(NT):
                dve.wait_ge(s_tk, t + 1)
                dve.tensor_tensor(tkl[:, t, :].rearrange("p (a n) -> p a n", a=2),
                                  ps[:, 4 + 2 * (t % 2):6 + 2 * (t % 2), :],
                                  f32(tkh[:, t, :]).rearrange("p (a n) -> p a n", a=2),
                                  ALU.subtract).then_inc(s_tkl, 1)

            def choose(e, steps, done):
                for t in range(NT):
                    ins = dve.tensor_scalar(sel[:, t, :], iota, rank[:, t, bass.ds(e, 1)]
                                            if not isinstance(e, int) else rank[:, t, e:e + 1],
                                            None, ALU.is_equal)
                    if t < NT - 1:
                        steps.on(ins)
                ins.then_inc(done, 1)

            choose(0, st, e_sel)
            dve.wait_ge(e_gat, 2)
            dve.tensor_copy(xgl[:, :, :].rearrange("p (a k) n -> p a (k n)", a=2), ps[:, 6:8, :])\
               .then_inc(e_xgl, 1)

            def add_out(k, count, steps):
                dve.wait_ge(e_cmb, count)
                b = 4 + 2 * (k % 2)
                for c, src, a0, b0 in ((0, ps[:, b, 0:TC], 0, TC), (1, ps[:, b, TC:HALF], TC, HALF)):
                    steps.on(dve.scalar_tensor_tensor(xres[:, k, a0:b0], src,
                                                      mod[:, 40 + k, c:c + 1],
                                                      xres[:, k, a0:b0], ALU.mult, ALU.add))
                dve.scalar_tensor_tensor(xres[:, k, HALF:T], ps[:, b + 1, 0:HALF],
                                         mod[:, 40 + k, 1:2], xres[:, k, HALF:T],
                                         ALU.mult, ALU.add).then_inc(e_add, 1)

            dve.wait_ge(s_cnt, 1)
            rounds = dve.value_load(rounds_i[0:1, 0:1], min_val=1, max_val=ROUNDS)
            with dve.Fori(0, rounds) as r:
                with dve.Fori(0, NE) as e:
                    n = r * NE + e
                    it = Steps(dve, v_item)
                    it.enter(n * ITEM_STEPS)
                    for s in range(3):
                        expert_lo(s, n * ECH + 3 + s)
                    dve.wait_ge(e_th, n + 1)
                    dve.wait_ge(e_mm, n * ECH + 4)
                    it.do(dve.scalar_tensor_tensor(act_[:, :], th[:, :], 1.0, ps[:, 0, :],
                                                   ALU.add, ALU.mult))
                    dve.tensor_tensor(act_[:, :], act_[:, :], ps[:, 1, :], ALU.mult)\
                       .then_inc(e_act, 1)
                    dve.wait_ge(e_selp, n + 1)
                    choose(e + 1, it, e_sel)
                    for k in range(KT):
                        add_out(k, n * KT + k + 1, it)
                    expert_lo(0, n * ECH + 6)
                    dve.wait_ge(e_gat, n * 2 + 4)
                    dve.tensor_copy(xgl[:, :, :].rearrange("p (a k) n -> p a (k n)", a=2),
                                    ps[:, 6:8, :]).then_inc(e_xgl, 1)
                    dve.wait_ge(e_aTh, n + 1)
                    dve.tensor_tensor(aTl[:, :, :].rearrange("p f n -> p (f n)"), ps[:, 0, :],
                                      f32(aTh[:, :, :]).rearrange("p f n -> p (f n)"),
                                      ALU.subtract).then_inc(e_aTl, 1)
                    expert_lo(1, n * ECH + 7)
                    expert_lo(2, n * ECH + 8)
                    dve.wait_ge(e_yh, n + 2)
                    dve.scalar_tensor_tensor(yl[:, :].rearrange("p (a n) -> p a n", a=2),
                                             ps[:, 2:4, :], wslot[:, :],
                                             f32(yh[:, :]).rearrange("p (a n) -> p a n", a=2),
                                             ALU.mult, ALU.subtract).then_inc(e_yl, 1)
                    assert it.n == ITEM_STEPS, it.n
                dve.tensor_scalar(rank[:, :, :], rank[:, :, :], -float(SLOTS), None, ALU.add)\
                   .then_inc(s_round, 1)
                dve.wait_ge(s_round, r + 1)
            for k in range(KT):
                add_out(k, rounds * (NE * KT) + k + 1, st)
            dve.wait_ge(s_rsf, 1)
            for k in range(KT):
                dve.scalar_tensor_tensor(yout[:, k, :], xres[:, k, :], col[:, G_F + k:G_F + k + 1],
                                         rs2[:, :], ALU.mult, ALU.mult).then_inc(s_yo, 1)

        @block.tensor
        def _(pe):
            def mm(out, lhsT, rhs, start, stop):
                return nc.tensor.matmul(out, lhsT, rhs, start=start, stop=stop)

            def three(groups, lh, ll, rh, rl, start, stop):
                for l, r, a, b in ((lh, rh, start, False), (lh, rl, False, False),
                                   (ll, rh, False, stop)):
                    for out, cut in groups:
                        last = mm(out, l, cut(r), a, b)
                return last

            def cut_half(a):
                return lambda r: r[:, a * HALF:(a + 1) * HALF]

            def block_out(e, wh, wl, kt, at_w, rh, rl):
                groups = [(pair(e)[:, a, :], cut_half(a)) for a in range(2)]
                for k in range(kt):
                    o = at_w + k * P
                    last = three(groups, wh[:, o:o + P], wl[:, o:o + P], rh[:, k, :], rl[:, k, :],
                                 k == 0, k == kt - 1)
                return last

            def chunk_split(slot, use):
                pe.wait_ge(raw_free[slot], use + 2)

            def dense(c, p, e0, i=0, rh=hhi, rl=hlo, kt=KT, per_i=0, between=None):
                chunk_split(c % NRAW, i + c // NRAW)
                for b in range(CH // (kt * P)):
                    pe.wait_ge(blk_free, i * per_i + e0 + b + 1)
                    block_out(e0 + b, whi[p], wlo[p], kt, b * kt * P, rh, rl).then_inc(blk_ready, 1)

            pe.wait_ge(d_const, 16 * 8)
            for k in range(KT):
                pe.wait_ge(s_sq, k + 1)
                for a in range(2):
                    last = mm(ps[:, a, 0:HALF], ones, hn[:, k, a * HALF:(a + 1) * HALF],
                              k == 0, k == KT - 1)
            last.then_inc(s_ssq, 1)
            pe.wait_ge(s_csil, 2)

            def mod_chunk(slot, use, bank, j0):
                pe.wait_ge(raw_full[slot], (use + 1) * 16)
                for b in range(2):
                    for k in range(KT):
                        o = (b * KT + k) * P
                        last = mm(ps[:, bank, 2 * (j0 + b):2 * (j0 + b) + 2], raw[slot][:, o:o + P],
                                  csil[:, k, :], k == 0, k == KT - 1)
                last.then_inc(raw_free[slot], 1)

            for c in range(N_MOD1):
                mod_chunk(c % NRAW, c // NRAW, 2, 2 * c)
            pe.wait_ge(s_wgl, 1)
            for k in range(KT):
                pe.wait_ge(s_hlo, k + 1)
                last = three([(ps[0:GP, 6 + a, 0:HALF], cut_half(a)) for a in range(2)],
                             wgh[:, k, :], wgl[:, k, :], hhi[:, k, :], hlo[:, k, :],
                             k == 0, k == KT - 1)
            last.then_inc(s_gps, 1)
            pe.wait_ge(s_gate, 2)
            with pe.Fori(0, N_QK // NRAW) as i:
                for j in range(NRAW):
                    dense(AT_QK + j, j % 2, 2 * j, i, per_i=8)

            def v_rows(v, e):
                pe.wait_ge(blk_free, 4 + E_V + max(2 * v - 1, 0) + 1)
                pe.wait_ge(blk_free, e + 1)
                for t in range(NT):
                    last = nc.tensor.transpose(
                        ps[:, 2 * (e % 4) + t // 3, (t % 3) * P:(t % 3 + 1) * P],
                        vst[v % 2][:, t * P:(t + 1) * P], ident)
                last.then_inc(blk_ready, 1)

            e = E_V
            for v in range(H):
                c, p = AT_V + v // 2, (v // 2) % 2
                if v % 2 == 0:
                    chunk_split(c % NRAW, c // NRAW)
                pe.wait_ge(blk_free, e + 1)
                block_out(e, whi[p], wlo[p], KT, (v % 2) * KT * P, hhi, hlo).then_inc(blk_ready, 1)
                e += 1
                if v:
                    v_rows(v - 1, e)
                    e += 1
            v_rows(H - 1, e)
            pe.wait_ge(s_grow, 1)
            pe.wait_ge(blk_free, E_G8 + 1)
            g0 = 2 * (E_G8 % 4)
            for t in range(NT):
                for src, o in ((gA, 0), (gI, 64), (gC, 144)):
                    if t or src is not gI:
                        nc.tensor.transpose(ps[:, g0, o + t * R16:o + (t + 1) * R16],
                                            src[:, t * P:(t + 1) * P], ident[0:R16, 0:R16])
            nc.tensor.transpose(ps[:, g0, 224:240], gF[:, 0:P], ident[0:R16, 0:R16])\
              .then_inc(blk_ready, 1)
            for j in range(N_U):
                dense(AT_U + j, j % 2, E_U + 2 * j)

            pe.wait_ge(blk_free, 4 + E_O)
            pe.wait_ge(d_st, 16)
            pe.wait_ge(s_init, 2)
            with pe.Fori(0, H // 2) as i:
                for hp in range(2):
                    h = i * 2 + hp
                    pe.wait_ge(s_mrow, h * 2 + 2)
                    pe.wait_ge(m_free, h + 1)
                    for d in range(2):
                        mm(ps[:, 2 + d, :], ones[0:R16, :], mrow[d][:, TC:T], True, True)
                    for d in range(2):
                        mm(ps[:, 4, d * P:(d + 1) * P], ones[0:R16, :], mrow[d][:, 0:TC], True, True)
                    pe.wait_ge(s_kst, h + 1)
                    nc.tensor.transpose(ps[:, 4, 2 * P:3 * P], kst[hp][:, 0:P], ident).then_inc(s_m, 1)
                    pe.wait_ge(s_qst, h + 1)
                    mm(ps[:, 0, 0:P], kst[hp][:, 0:P], qst[hp][:, 0:P], True, True).then_inc(s_sc, 1)
                    pe.wait_ge(qc1_free, h * 2 + 1)
                    for j in range(NL):
                        if j:
                            pe.wait_ge(s_sev, h * 5 + j)
                        mm(ps[:, (j + 1) % 2, :], kst[hp][:, (j + 1) * P:(j + 2) * P],
                           qst[hp][:, TC:T], True, True).then_inc(s_sc, 1)
                    pe.wait_ge(qc5_free, h * 3 + 1)
                    for c2 in range(2):
                        c = AT_MOD2 + 2 * hp + c2
                        mod_chunk(c % NRAW, i + c // NRAW, 5, 2 * c2)
                    def pv(t, bank, free):
                        pe.wait_ge(*free)
                        for d in range(2):
                            tiles = [t] if t == 0 else (range(1, t + 1), range(t, NT))[d]
                            for s in tiles:
                                if s == t:
                                    w = DG[d][:, t, :]
                                elif d == 0:
                                    o = OFF_F[s - 1] + (t - s - 1) * P
                                    w = OFF[0][:, o:o + P]
                                else:
                                    o = OFF_B[s - 2] + (t - 1) * P
                                    w = OFF[1][:, o:o + P]
                                last = mm(ps[:, bank, d * V1:(d + 1) * V1], w, Vt[:, s, h, :],
                                          s == tiles[0], s == tiles[-1])
                        last.then_inc(s_pv, 1)

                    pe.wait_ge(s_p, h + 1)
                    pv(0, 6, (pv6_free, h * 3 + 1))
                    for t in range(NL):
                        if t % 2 == 0:
                            pe.wait_ge(qc5_free, h * 3 + 2 + t // 2)
                        else:
                            pe.wait_ge(qc1_free, h * 2 + 1 + t // 2)
                        mm(ps[:, (5, 1)[t % 2], 0:2 * V1].rearrange("p (d n) -> p d n", n=V1),
                           qst[hp][:, (t + 1) * P:(t + 2) * P], stC[:, :, h, :], True, True)
                        pv(t + 1, (7, 6)[t % 2],
                           (pv7_free, h * 3 + 1 + t // 2) if t % 2 == 0
                           else (pv6_free, h * 3 + 2 + t // 2))
                    pe.wait_ge(s_kw, h * 2 + 2)
                    pe.wait_ge(pv7_free, h * 3 + 3)
                    for d in range(2):
                        last = mm(ps[:, 7, d * V1:(d + 1) * V1], kw[d][:, :], Vt[:, 0, h, :],
                                  True, True)
                    last.then_inc(s_pv, 1)

            for s_, v_ in ((pv6_free, 1 + 3 * H), (pv7_free, 1 + 3 * H), (qc1_free, 1 + 2 * H),
                           (qc5_free, 1 + 3 * H), (m_free, 1 + H), (s_sev, 5 * H)):
                pe.wait_ge(s_, v_)
            for j in range(N_O):
                dense(AT_O + j, j % 2, E_O + 2 * j)
            for k in range(H):
                e = E_Y + k
                pe.wait_ge(s_hd, 1 + NT)
                pe.wait_ge(blk_free, e + 1)
                for t in range(NT):
                    last = nc.tensor.transpose(
                        ps[:, 2 * (e % 4) + t // 3, (t % 3) * P:(t % 3 + 1) * P],
                        Vt[:, t, k, 0:DH], ident)
                last.then_inc(blk_ready, 1)
            with pe.Fori(0, N_G // NRAW) as i:
                for j in range(NRAW):
                    dense(AT_G + j, j % 2, E_TH + 2 * j, i, per_i=8)
            pe.wait_ge(s_pool, 1)
            pe.wait_ge(d_wp, 16)
            for g in range(NG):
                e = E_PL + g
                pe.wait_ge(blk_free, e + 1)
                for a in range(2):
                    last = mm(pair(e)[:, a, :], wpool[:, g, :], U[:, g, a * HALF:(a + 1) * HALF],
                              True, True)
                last.then_inc(blk_ready, 1)
            pe.wait_ge(blk_free, 4 + E_B)
            for j in range(N_B):
                dense(AT_B + j, j % 2, E_B + 4 * j, rh=ybh, rl=ybl, kt=NG)
            pe.wait_ge(s_yl, KT)
            for j in range(N_A):
                dense(AT_A + j, j % 2, E_A + 2 * j)
            pe.wait_ge(s_mgl, KT)
            for j in range(N_OUT):
                dense(AT_OUT + j, j % 2, E_OUT + 2 * j, rh=mgh, rl=mgl)
            pe.wait_ge(blk_free, 4 + E_END)
            for k in range(KT):
                pe.wait_ge(s_sq2, k + 1)
                for a in range(2):
                    last = mm(ps[:, a, 0:HALF], ones, n2[:, k, a * HALF:(a + 1) * HALF],
                              k == 0, k == KT - 1)
            last.then_inc(s_ssq2, 1)
            pe.wait_ge(s_h2, KT)
            for t in range(NT):
                for k in range(KT):
                    last = mm(ps[:, 2, t * (EG + NE):(t + 1) * (EG + NE)],
                              h2[:, k, t * P:(t + 1) * P], wr[:, k, :], k == 0, k == KT - 1)
            last.then_inc(s_rk, 1)
            def token_major(t):
                if t >= 2:
                    pe.wait_ge(s_tkl, t - 1)
                for k in range(KT):
                    last = nc.tensor.transpose(ps[:, 4 + 2 * (t % 2) + k // 4, (k % 4) * P:
                                                  (k % 4 + 1) * P], h2[:, k, t * P:(t + 1) * P], ident)
                last.then_inc(s_tkp, 1)

            for t in range(2):
                token_major(t)
            pe.wait_ge(s_am, 1)
            for t in range(NT + 1):
                out = ps[:, 3, t * NE:(t + 1) * NE]
                for u in range(min(t + 1, NT)):
                    last = mm(out, ones if u < t else cst[:, C_STRICT:C_STRICT + P], am[:, u, :],
                              u == 0, u == min(t, NT - 1))
            last.then_inc(s_rk, 1)
            for t in range(2, NT):
                token_major(t)

            def gather():
                for src, bank in ((tkh, 4), (tkl, 6)):
                    for k in range(KT):
                        for t in range(NT):
                            last = mm(ps[:, bank + k // 4, (k % 4) * P:(k % 4 + 1) * P],
                                      src[:, t, k * P:(k + 1) * P], sel[:, t, :],
                                      t == 0, t == NT - 1)
                    last.then_inc(e_gat, 1)

            def combine(adds):
                for k in range(KT):
                    if k >= 2:
                        pe.wait_ge(e_add, adds + k - 1)
                    b = 4 + 2 * (k % 2)
                    for src in (yh, yl):
                        for a in range(2):
                            last = mm(ps[:, b + a, 0:HALF], src[:, k * P:(k + 1) * P],
                                      selT[:, a * HALF:(a + 1) * HALF], src is yh, src is yl)
                    last.then_inc(e_cmb, 1)

            pe.wait_ge(s_tkl, NT)
            pe.wait_ge(e_sel, 1)
            gather()
            pe.wait_ge(s_cnt, 1)
            rounds = pe.value_load(rounds_i[0:1, 0:1], min_val=1, max_val=ROUNDS)
            with pe.Fori(0, rounds) as r:
                with pe.Fori(0, NE) as e:
                    n = r * NE + e
                    pe.wait_ge(e_xgh, n + 1)
                    pe.wait_ge(e_xgl, n + 1)
                    for c in range(4):
                        s = c % 3
                        pe.wait_ge(e_free[s], n * 2 + 2 + c // 3)
                        for k in range(4):
                            kk = (c % 2) * 4 + k
                            last = three([(ps[:, c // 2, :],
                                           lambda w, k=k: w[:, k * DE:(k + 1) * DE])],
                                         xgh[:, kk, :], xgl[:, kk, :], ehi[s], elo[s],
                                         kk == 0, kk == KT - 1)
                        last.then_inc(e_mm, 1)
                    pe.wait_ge(e_yh, n + 1)
                    pe.wait_ge(e_yl, n + 1)
                    for t in range(NT):
                        nc.tensor.transpose(ps[:, 2 + t // 4, (t % 4) * P:(t % 4 + 1) * P],
                                            f32(sel[:, t, :]), ident)
                    for t in range(NT):
                        last = mm(ps[:, 3, 2 * P:2 * P + 1], f32(sel[:, t, :]),
                                  wtok[:, t, bass.ds(e, 1)], t == 0, t == NT - 1)
                    last.then_inc(e_selp, 1)
                    pe.wait_ge(e_selT, n + 1)
                    combine(n * KT)
                    pe.wait_ge(e_sel, n + 2)
                    pe.wait_ge(e_add, n * KT + KT)
                    gather()
                    pe.wait_ge(e_act, n + 1)
                    for f in range(FT):
                        last = nc.tensor.transpose(ps[:, 0, f * P:(f + 1) * P],
                                                   act_[:, f * P:(f + 1) * P], ident)
                    last.then_inc(e_aTp, 1)
                    pe.wait_ge(e_aTh, n + 1)
                    pe.wait_ge(e_aTl, n + 1)
                    pe.wait_ge(e_selT, n + 2)
                    for c in (4, 5):
                        s = c % 3
                        pe.wait_ge(e_free[s], n * 2 + 3)
                        for f2 in range(2):
                            f = (c - 4) * 2 + f2
                            groups = [(ps[:, 2 + a, :], lambda w, a=a, f2=f2:
                                       w[:, (2 * f2 + a) * 512:(2 * f2 + a + 1) * 512])
                                      for a in range(2)]
                            last = three(groups, aTh[:, f, :], aTl[:, f, :], ehi[s], elo[s],
                                         f == 0, f == FT - 1)
                        last.then_inc(e_mm, 1)
            pe.wait_ge(e_xgh, rounds * NE + 1)
            pe.wait_ge(e_xgl, rounds * NE + 1)
            pe.wait_ge(e_yh, rounds * NE + 1)
            pe.wait_ge(e_yl, rounds * NE + 1)
            pe.wait_ge(e_selT, rounds * NE + 1)
            combine(rounds * (NE * KT))
            for k in range(KT):
                pe.wait_ge(s_sqf, k + 1)
                for a in range(2):
                    last = mm(ps[:, a, 0:HALF], ones, h2[:, k, a * HALF:(a + 1) * HALF],
                              k == 0, k == KT - 1)
            last.then_inc(s_ssf, 1)


def _constants():
    c = np.zeros((P, C_END), np.float32)
    r, q = np.arange(P)[:, None], np.arange(P)[None, :]
    c[:, C_ID:C_ID + P] = r == q
    c[:, C_ONE:C_ONE + P] = 1
    c[:, C_STRICT:C_STRICT + P] = r < q
    c[:, C_IOTA:C_IOTA + P] = q
    c[:, C_NEGF:C_NEGF + P] = np.where(r <= q, 0, NEG)
    c[:, C_NEGB:C_NEGB + P] = np.where(r >= q, 0, NEG)
    c[:H, C_MF] = 1
    c[H:R16, C_MB] = 1
    c[:, C_WT:C_WT + 4 * NT] = np.tile([8, 4, 2, 1], NT)
    c[:, C_THR:C_THR + ROUNDS] = np.arange(ROUNDS) * SLOTS
    c[:, C_EPS] = EPS
    cnt = np.zeros((NG, T), np.float32)

    def width(n, w):
        i = np.arange(n)
        return np.clip(i - w // 2 + w, 0, n) - np.clip(i - w // 2, 0, n)

    for g, w in enumerate(WIN):
        cnt[g, :TC] = width(TC, w)
        cnt[g, TC:] = np.outer(width(GR, w), width(GW, w)).ravel()
    return c, np.ascontiguousarray(np.broadcast_to(1 / cnt, (P, NG, T)), dtype=np.float32)


def _layout(i):
    i = {k: np.asarray(v) for k, v in i.items()}
    fm = lambda a: a.T.reshape(KT, P, -1).transpose(1, 0, 2)
    cols = lambda v: v.reshape(-1, P).T

    def chunks(w, kt):
        nb, per = w.shape[1] // P, CH // (kt * P)
        return w.reshape(kt, P, nb, P).transpose(2, 1, 0, 3).reshape(
            nb // per, per, P, kt * P).transpose(0, 2, 1, 3).reshape(nb // per, P, CH)

    w, b = i["w_in"][0], i["b_in"][0]
    g0 = 4 * D
    pool, ga, gb = g0 + 4 * H, g0 + 4 * H + NG * P, g0 + 4 * H + NG * P + D
    qkvu = np.r_[0:3 * D, pool:pool + NG * P]
    late = np.r_[3 * D:4 * D, gb:gb + D, ga:ga + D]
    wm = chunks(i["w_mod"][0], KT)
    wst = np.concatenate([wm[:N_MOD1], chunks(w[:, qkvu], KT), wm[N_MOD1:], chunks(w[:, late], KT),
                          chunks(i["w_proj_b"][0], NG), chunks(i["w_proj_a"][0], KT),
                          chunks(i["w_out"][0], KT)])
    wg = np.zeros((P, KT, GP), np.float32)
    bg = np.zeros((GP, 1), np.float32)
    for dst, src in ((0, 0), (8, 16), (32, 8), (40, 24)):
        wg[:, :, dst:dst + H] = w[:, g0 + src:g0 + src + H].reshape(KT, P, H).transpose(1, 0, 2)
        bg[dst:dst + H, 0] = b[g0 + src:g0 + src + H]
    col = np.concatenate([cols(b[qkvu]), cols(b[late]), cols(i["b_mod"][0]), cols(i["g_norm1"][0]),
                          cols(i["g_norm2"][0]), cols(i["g_final"]), cols(i["gn_gain"][0]),
                          cols(i["pool_scale"][0])], axis=1)
    wr = np.concatenate([i["w_router_grp"][0], i["w_router_exp"][0].reshape(D, NE)], 1)
    br = np.concatenate([i["b_router_grp"][0], i["b_router_exp"][0].reshape(NE)])
    st = np.concatenate([i["state_C"][0, 0], i["state_n"][0, 0][..., None]], -1)
    up = lambda a: a.reshape(NE, 2, 4, P, DE).transpose(0, 1, 3, 2, 4).reshape(NE, 2, P, CH)
    down = i["w_exp_down"][0].reshape(NE, 2, 2, P, D).transpose(0, 1, 3, 2, 4).reshape(NE, 2, P, CH)
    ex = np.concatenate([up(i["w_exp_gate"][0]), up(i["w_exp_up"][0]), down], 1)
    cst, rcnt = _constants()
    return dict(
        x=fm(np.concatenate([i["x_prompt"][0], i["x_sample"][0]])),
        c=fm(np.stack([i["c_ctx"], i["c"][0]])), wst=wst, wg=wg, bg=bg, col=col,
        wpool=i["w_pool_grp"][0].transpose(1, 0, 2), wr=wr.reshape(KT, P, -1).transpose(1, 0, 2),
        br=np.broadcast_to(br, (P, EG + NE)), st=st.transpose(2, 0, 1, 3),
        m0=i["state_m"][0, 0].reshape(R16, 1), cst=cst, rcnt=rcnt,
        wexp=np.concatenate([ex, ex[:1]]))


_OUTS = (("y", (P, KT, T)), ("so", (P, 2, H, V1)), ("mo", (R16, 1)))


def kernel(**inputs):
    import concourse.bacc as bacc
    from concourse.bass_utils import run_bass_kernel_spmd

    nc = bacc.Bacc("TRN2", target_bir_lowering=False, num_devices=1)
    arrays, args = {}, []
    for name, a in _layout(inputs).items():
        arrays["in_" + name] = a = np.ascontiguousarray(a)
        args.append(nc.dram_tensor("in_" + name, a.shape, mybir.dt.from_np(a.dtype),
                                   kind="ExternalInput").ap())
    for name, shape in _OUTS:
        args.append(nc.dram_tensor("out_" + name, shape, F32, kind="ExternalOutput").ap())
    layer_kernel(nc, *args)
    got = run_bass_kernel_spmd(nc, [arrays], core_ids=[0]).results[0]
    y = got["out_y"].transpose(2, 1, 0).reshape(T, D)
    so = got["out_so"].transpose(1, 2, 0, 3)
    return (np.ascontiguousarray(y[:TC])[None], np.ascontiguousarray(y[TC:])[None],
            np.ascontiguousarray(so[..., :DH])[None, None],
            np.ascontiguousarray(so[..., DH])[None, None],
            np.ascontiguousarray(got["out_mo"].reshape(1, 1, 2, H)))
```

```python
import concourse.bass as bass
from concourse import mybir
from contextlib import ExitStack
import numpy as np

F32 = mybir.dt.float32
F32R = mybir.dt.float32r
I32 = mybir.dt.int32
ALU = mybir.AluOpType
ACT = mybir.ActivationFunctionType
AX = mybir.AxisListType.X

P = 128
D = 1024
KT = D // P
TC, TL = 128, 512
T = TC + TL
NT = T // P
NL = TL // P
HALF = T // 2
H = 8
DH = 128
V1 = DH + 1
R16 = 2 * H
GP = 48
WIN = (2, 4, 8, 16)
NG = len(WIN)
GW, GR = 64, TL // 64
PAD = 8
CH = 2048
NRAW = 4
EG, EE = 4, 4
NE = EG * EE
DE = 512
FT = DE // P
SLOTS = 128
ROUNDS = -(-T // SLOTS)
NPAIR = NE // 2
ECH = 12
ERAW, ESPL = 4, 3
EPS = 1e-6
NEG = -1e30
SCALE = DH ** -0.5

N_MOD1 = 8
N_QK, N_V, N_U = 8, 4, 2
N_MOD2 = 16
N_O, N_G, N_B, N_A, N_OUT = 4, 8, 2, 4, 4
N_DENSE = N_MOD1 + N_QK + N_V + N_U + N_MOD2 + N_O + N_G + N_B + N_A + N_OUT
AT_QK = N_MOD1
AT_V = AT_QK + N_QK
AT_U = AT_V + N_V
AT_MOD2 = AT_U + N_U
AT_O = AT_MOD2 + N_MOD2
AT_G = AT_O + N_O
AT_B = AT_G + N_G
AT_A = AT_B + N_B
AT_OUT = AT_A + N_A

C_ID, C_ONE, C_FWD, C_BWD, C_STRICT, C_IOTA, C_NEGF, C_NEGB = (P * i for i in range(8))
C_MF = 8 * P
C_MB = C_MF + 1
C_WT = C_MF + 2
C_THR = C_WT + 4 * NT
C_EPS = C_THR + ROUNDS
C_END = C_EPS + 1

B_IN, B_MOD, G_1, G_2, G_F, G_N, P_S, W_END = 0, 52, 100, 108, 116, 124, 132, 136


class Steps:

    def __init__(self, eng, sem):
        self.eng, self.sem, self.base, self.n = eng, sem, 0, 0

    def on(self, ins):
        ins.then_inc(self.sem, 1)
        self.n += 1

    def wait(self):
        self.eng.wait_ge(self.sem, self.base + self.n)

    def do(self, ins):
        self.on(ins)
        self.wait()

    def enter(self, base):
        self.base, self.n = base, 0


def layer_kernel(nc, x_d, c_d, wst_d, wg_d, bg_d, col_d, wpool_d, wr_d, br_d, st_d, m0_d, cst_d,
                 rcnt_d, wexp_d, y_d, so_d, mo_d):
    ctx = ExitStack()
    with ctx:
        base = -(-nc.sbuf_base // 32) * 32
        ctx.enter_context(nc.sbuf_tensor("arena", [P, 207 * 256], F32))

        def at(name, kib, shape, dt=F32):
            return nc.alloc_sbuf_tensor_at(name, shape, dt, offset=base + int(kib * 1024))

        def sem(name):
            return ctx.enter_context(nc.semaphore(name))

        cst = at("cst", 0, [P, C_END])
        ident, ones = cst[:, C_ID:C_ID + P], cst[:, C_ONE:C_ONE + P]
        iota = cst[:, C_IOTA:C_IOTA + P]
        eps = cst[:, C_EPS:C_EPS + 1]
        col = at("col", 4.25, [P, W_END])
        mod = at("mod", 4.875, [P, 48, 2])
        gain = at("gain", 5.25, [P, KT, 2])
        cin = at("cin", 5.375, [P, KT, 2])
        csil = at("csil", 5.5, [P, KT, 2])
        half_gate = at("half_gate", 5.625, [P, KT, 2])
        half_gn = at("half_gn", 5.6875, [P, KT])
        a_tok = at("a_tok", 5.75, [P, NT, R16])
        wi_tok = at("wi_tok", 6.0625, [P, NT, R16])
        em_tok = at("em_tok", 6.375, [P, NT, R16])
        ws_tok = at("ws_tok", 6.6875, [P, R16])
        hss = at("hss", 6.75, [P, NT, H])
        rinv = at("rinv", 6.9375, [P, NT, 2])
        bg = at("bg", 7.0, [GP, 1])
        m0 = at("m0", 7.0625, [R16, 1])
        mlast = at("mlast", 7.125, [R16, 4])
        rounds_i = at("rounds_i", 7.1875, [1, 1], I32)
        wslot = at("wslot", 7.21875, [P, 2])
        wr = at("wr", 7.25, [P, KT, EG + NE])
        br = at("br", 7.875, [P, EG + NE])

        raw = [at(f"raw{s}", 8 + 8 * s, [P, CH]) for s in range(NRAW)]
        whi = [at(f"whi{s}", 40 + 16 * s, [P, CH], F32R) for s in range(2)]
        wlo = [at(f"wlo{s}", 48 + 16 * s, [P, CH], F32R) for s in range(2)]
        hhi = at("hhi", 72, [P, KT, T], F32R)
        hlo = at("hlo", 92, [P, KT, T], F32R)
        hn = at("hn", 112, [P, KT, T])
        xT = at("xT", 132, [P, KT, T])
        rstd = at("rstd", 172.5, [P, T])
        QK = at("QK", 112, [P, 2 * H, T])
        Vt = at("Vt", 152, [P, NT, H, V1])
        U = at("U", 172.75, [P, NG, T])
        TMP = 182.75
        wgr = at("wgr", TMP, [P, KT, GP])
        wgh = at("wgh", TMP + 1.5, [P, KT, GP], F32R)
        wgl = at("wgl", TMP + 3, [P, KT, GP], F32R)
        vst = [at(f"vst{s}", TMP + 2.5 * s, [P, T]) for s in range(2)]
        gI, gF, gA, gB, gC, gOne = (at(n, TMP + 5 + 2.5 * i, [R16, T])
                                    for i, n in enumerate(("gI", "gF", "gA", "gB", "gC", "gOne")))
        negM = at("negM", TMP + 22.5, [R16, T])
        DG = [at(f"DG{d}", 40 + 2.5 * d, [P, NT, P]) for d in range(2)]
        OFF = [at(f"OFF{d}", 45 + 3 * d, [P, 6 * P]) for d in range(2)]
        S = at("S", 51, [P, 20 * P])
        num = at("num", 61, [P, NT, 2, V1])
        mrow = [at(f"mrow{d}", 66.25 + 2.5 * d, [R16, T]) for d in range(2)]
        qst = [at(f"qst{s}", TMP + 5 * s, [P, T]) for s in range(2)]
        kst = [at(f"kst{s}", TMP + 2.5 + 5 * s, [P, T]) for s in range(2)]
        stC = at("stC", TMP + 10, [P, 2, H, V1])
        qcw = at("qcw", TMP + 18.125, [P, 2, V1])
        kw = [at(f"kw{d}", TMP + 19.25 + 0.5 * d, [P, P]) for d in range(2)]
        O = at("O", 132, [P, KT, T])
        Y = at("Y", 112, [P, KT, T])
        TH = at("TH", 132, [P, 2 * KT, T])
        XP = [at(f"XP{i}", TMP + 2.5 * i, [P, GR, GW + 2 * PAD]) for i in range(2)]
        RP = [at(f"RP{i}", TMP + 5 + 3.75 * i, [P, 2 * GR - 1, GW]) for i in range(2)]
        rcnt = at("rcnt", TMP + 12.5, [P, NG, T])
        CP = [at(f"CP{i}", TMP + 22.5 + 0.625 * i, [P, TC + 2 * PAD]) for i in range(2)]
        ybh = at("ybh", TMP, [P, NG, T], F32R)
        ybl = at("ybl", TMP + 10, [P, NG, T], F32R)
        wpool = at("wpool", TMP + 22.5, [P, NG, P])
        mgh = at("mgh", 112, [P, KT, T], F32R)
        mgl = at("mgl", TMP, [P, KT, T], F32R)
        xres = at("xres", 132, [P, KT, T])
        n2 = at("n2", 152, [P, KT, T])
        h2 = at("h2", 112, [P, KT, T])
        rs2 = at("rs2", 192.5, [P, T])
        eraw = [at(f"eraw{s}", o, [P, CH]) for s, o in enumerate((72, 80, 88, 199))]
        ehi = [at(f"ehi{s}", 8 + 16 * s, [P, CH], F32R) for s in range(ESPL)]
        elo = [at(f"elo{s}", 16 + 16 * s, [P, CH], F32R) for s in range(ESPL)]
        sel = at("sel", 56, [P, NT, 2 * SLOTS], F32R)
        selT = at("selT", 61, [P, 2, T], F32R)
        th = at("th", 66, [P, DE])
        act_ = at("act", 68, [P, DE])
        aTh = at("aTh", 70, [P, FT, SLOTS], F32R)
        aTl = at("aTl", 128, [P, FT, SLOTS], F32R)
        xgh = at("xgh", 112, [P, KT, 2 * SLOTS], F32R)
        xgl = at("xgl", 120, [P, KT, 2 * SLOTS], F32R)
        yh = at("yh", 96, [P, 2, D], F32R)
        yl = at("yl", 104, [P, 2, D], F32R)
        tkh = at("tkh", 152, [P, NT, D], F32R)
        tkl = at("tkl", 172, [P, NT, D], F32R)
        wtok = at("wtok", 195, [P, NT, NE])
        rank = at("rank", 195.5, [P, NT, NE + 2])
        RT = 196
        lg = at("lg", RT, [P, NT, EG + NE])
        r5 = at("r5", RT + 0.5, [P, 12, NT])
        goh = at("goh", RT + 1, [P, NT, EG])
        les = at("les", RT + 1.125, [P, NT, EE])
        o1 = at("o1", RT + 1.25, [P, NT, EE])
        o2 = at("o2", RT + 1.375, [P, NT, EE])
        t4 = at("t4", RT + 1.5, [P, NT, EE])
        t5 = at("t5", RT + 1.625, [P, NT, EE])
        t16 = at("t16", RT + 1.75, [P, NT, EG, EE])
        am = at("am", RT + 2.25, [P, NT, NE])
        thr = at("thr", RT + 2.75, [P, 8])
        yout = at("yout", 152, [P, KT, T])

        ps = ctx.enter_context(nc.psum_tensor("ps", [P, 8, 512], F32))

        def pair(e):
            return ps[:, 2 * (e % 4):2 * (e % 4) + 2, 0:HALF]

        def halves(ap):
            return ap.rearrange("p (a n) -> p a n", a=2)

        def f32(t):
            return t.bitcast(F32)

        d_const, d_x, d_st, d_pool, d_wp, d_xr = (sem(n) for n in (
            "d_const", "d_x", "d_st", "d_pool", "d_wp", "d_xr"))
        raw_full = [sem(f"raw_full{s}") for s in range(NRAW)]
        raw_free = [sem(f"raw_free{s}") for s in range(NRAW)]
        hi_ready = sem("hi_ready")
        blk_ready, blk_free = sem("blk_ready"), sem("blk_free")
        s_csil, s_sq, s_ssq, s_rstd, s_hn, s_hhi, s_hlo = (sem(n) for n in (
            "s_csil", "s_sq", "s_ssq", "s_rstd", "s_hn", "s_hhi", "s_hlo"))
        s_wgh, s_wgl, s_gps, s_gate, s_lsg, s_grow, s_gtok = (sem(n) for n in (
            "s_wgh", "s_wgl", "s_gps", "s_gate", "s_lsg", "s_grow", "s_gtok"))
        s_init = sem("s_init")
        s_mrow, s_qst, s_kst, s_m, s_kw, s_sc, s_sev, s_tdg, s_exp, s_p, s_pv, s_nm = (
            sem(n) for n in ("s_mrow", "s_qst", "s_kst", "s_m", "s_kw", "s_sc", "s_sev", "s_tdg",
                             "s_exp", "s_p", "s_pv", "s_nm"))
        m_free, qc5_free, qc1_free, pv6_free, pv7_free = (sem(n) for n in (
            "m_free", "qc5_free", "qc1_free", "pv6_free", "pv7_free"))
        s_o, s_hd, s_yh, s_yl = (sem(n) for n in ("s_o", "s_hd", "s_yh", "s_yl"))
        s_pool, s_ybh, s_mg, s_mgh, s_mgl, s_xr = (sem(n) for n in (
            "s_pool", "s_ybh", "s_mg", "s_mgh", "s_mgl", "s_xr"))
        s_sq2, s_ssq2, s_rs2, s_h2, s_lg, s_ex, s_am, s_rk, s_tkp, s_tk, s_tkl, s_cnt = (sem(n) for n in (
            "s_sq2", "s_ssq2", "s_rs2", "s_h2", "s_lg", "s_ex", "s_am", "s_rk", "s_tkp", "s_tk",
            "s_tkl", "s_cnt"))
        e_full = [sem(f"e_full{s}") for s in range(ERAW)]
        e_free = [sem(f"e_free{s}") for s in range(ERAW)]
        e_hi, e_mm = sem("e_hi"), sem("e_mm")
        e_th, e_act, e_sel, e_selp, e_selT, e_cmb, e_add, e_gat, e_aTp = (sem(n) for n in (
            "e_th", "e_act", "e_sel", "e_selp", "e_selT", "e_cmb", "e_add", "e_gat", "e_aTp"))
        e_xgh, e_xgl, e_aTh, e_aTl, e_yh, e_yl = (sem(n) for n in (
            "e_xgh", "e_xgl", "e_aTh", "e_aTl", "e_yh", "e_yl"))
        s_round = sem("s_round")
        s_sqf, s_ssf, s_rsf, s_out = sem("s_sqf"), sem("s_ssf"), sem("s_rsf"), sem("s_out")
        s_yo, s_sto = sem("s_yo"), sem("s_sto")
        a_steps, v_steps, g_steps = sem("act_steps"), sem("dve_steps"), sem("pool_steps")
        v_head, v_item, a_head = sem("dve_head_steps"), sem("dve_item_steps"), sem("act_loop_steps")

        block = ctx.enter_context(nc.Block())
        E_V, E_G8, E_U, E_O, E_Y, E_TH, E_PL, E_B, E_A, E_OUT, E_END = (
            16, 32, 33, 37, 45, 53, 69, 73, 81, 89, 97)
        CV, CU, CO, CTH, CB, CA, COUT = 8, 12, 14, 18, 26, 28, 32
        OFF_F, OFF_B = (0, 3 * P, 5 * P), (0, P, 3 * P)
        HEAD_STEPS, PAIR_STEPS = 20, 18

        @block.sync
        def _(sp):
            for s in range(NRAW):
                sp.sem_inc(raw_free[s], 1)
            for s in range(ERAW):
                sp.sem_inc(e_free[s], 1)
            with sp.Fori(0, N_DENSE // NRAW) as i:
                for s in range(NRAW):
                    sp.wait_ge(raw_free[s], i + 1)
                    sp.dma_start(raw[s][:, :], wst_d[i * NRAW + s, :, :]).then_inc(raw_full[s], 16)
            sp.wait_ge(blk_ready, E_OUT)
            for s in range(ERAW):
                if s == ERAW - 1:
                    sp.wait_ge(blk_ready, E_END)
                sp.dma_start(eraw[s][:, :], wexp_d[0, s, :, :]).then_inc(e_full[s], 16)
            sp.wait_ge(s_cnt, 1)
            rounds = sp.value_load(rounds_i[0:1, 0:1], min_val=1, max_val=ROUNDS)
            with sp.Fori(0, rounds) as r:
                with sp.Fori(0, NPAIR) as q:
                    n = r * NPAIR + q
                    for c in range(ERAW, ECH + ERAW):
                        sp.wait_ge(e_free[c % ERAW], n * (ECH // ERAW) + c // ERAW + 1)
                        sp.dma_start(eraw[c % ERAW][:, :], wexp_d[q + c // ECH, c % ECH, :, :])\
                          .then_inc(e_full[c % ERAW], 16)
            for k in range(KT):
                sp.wait_ge(s_yo, k + 1)
                sp.dma_start(y_d[:, k, :], yout[:, k, :]).then_inc(s_out, 16)
            sp.wait_ge(s_out, 16 * KT)
            sp.wait_ge(s_sto, 32)

        @block.gpsimd
        def _(gp):
            st = Steps(gp, g_steps)
            gp.memset(gOne[:, :], 1.0).then_inc(s_init, 1)
            gp.memset(Vt[:, :, :, DH:V1], 1.0).then_inc(s_init, 1)
            gp.wait_ge(s_gtok, 1)
            gp.dma_start(stC[:, :, :, :], st_d).then_inc(d_st, 16)
            gp.wait_ge(blk_ready, E_O)
            with gp.Fori(0, H) as h:
                gp.wait_ge(m_free, h + 1)
                for d in range(2):
                    gp.tensor_tensor(mrow[d][:, :], negM[:, :],
                                     cst[0:R16, bass.ds(h + (C_ID + d * H), 1)].broadcast_to([R16, T]),
                                     ALU.mult).then_inc(s_mrow, 1)
            gp.wait_ge(pv7_free, 1 + 3 * H)
            gp.dma_start(so_d, stC[:, :, :, :]).then_inc(s_sto, 16)
            gp.dma_start(mo_d, mlast[:, 2:3]).then_inc(s_sto, 16)
            gp.wait_ge(s_sto, 32)
            gp.dma_start(rcnt[:, :, :], rcnt_d).then_inc(d_pool, 16)
            gp.wait_ge(s_nm, H)
            gp.wait_ge(d_pool, 16)
            for g, w in enumerate(WIN):
                st.on(gp.memset(XP[0][:, :, :], 0.0))
                st.on(gp.memset(RP[0][:, :, :], 0.0))
                st.do(gp.memset(CP[0][:, :], 0.0))
                st.do(gp.tensor_copy(XP[0][:, :, PAD:PAD + GW],
                                     U[:, g, TC:T].rearrange("p (r c) -> p r c", c=GW)))
                n, s, src = GW + 2 * PAD, 1, 0
                while s < w:
                    n -= s
                    st.do(gp.tensor_tensor(XP[1 - src][:, :, 0:n], XP[src][:, :, 0:n],
                                           XP[src][:, :, s:s + n], ALU.add))
                    s, src = 2 * s, 1 - src
                xs = XP[src][:, :, PAD - w // 2:PAD - w // 2 + GW]
                if w // 2 >= GR:
                    st.do(gp.tensor_tensor(RP[0][:, 0:4, :], xs[:, 0:4, :], xs[:, 4:8, :], ALU.add))
                    st.do(gp.tensor_tensor(RP[1][:, 0:2, :], RP[0][:, 0:2, :], RP[0][:, 2:4, :],
                                           ALU.add))
                    st.do(gp.tensor_tensor(RP[0][:, 0:1, :], RP[1][:, 0:1, :], RP[1][:, 1:2, :],
                                           ALU.add))
                    res = RP[0][:, 0:1, :].broadcast_to([P, GR, GW])
                else:
                    st.do(gp.tensor_copy(RP[0][:, w // 2:w // 2 + GR, :], xs))
                    n, s, src = GR + w - 1, 1, 0
                    while s < w:
                        n -= s
                        st.do(gp.tensor_tensor(RP[1 - src][:, 0:n, :], RP[src][:, 0:n, :],
                                               RP[src][:, s:s + n, :], ALU.add))
                        s, src = 2 * s, 1 - src
                    res = RP[src][:, 0:GR, :]
                mean_l = XP[0][:, :, 0:GW]
                st.do(gp.tensor_tensor(mean_l, res, rcnt[:, g, TC:T].rearrange(
                    "p (r c) -> p r c", c=GW), ALU.mult))
                ul = U[:, g, TC:T].rearrange("p (r c) -> p r c", c=GW)
                st.do(gp.tensor_tensor(ul, mean_l, ul, ALU.subtract))
                st.do(gp.tensor_copy(CP[0][:, PAD:PAD + TC], U[:, g, 0:TC]))
                n, s, src = TC + 2 * PAD, 1, 0
                while s < w:
                    n -= s
                    st.do(gp.tensor_tensor(CP[1 - src][:, 0:n], CP[src][:, 0:n],
                                           CP[src][:, s:s + n], ALU.add))
                    s, src = 2 * s, 1 - src
                cs = CP[src][:, PAD - w // 2:PAD - w // 2 + TC]
                st.do(gp.tensor_tensor(CP[1 - src][:, 0:TC], cs, rcnt[:, g, 0:TC], ALU.mult))
                st.do(gp.tensor_tensor(U[:, g, 0:TC], CP[1 - src][:, 0:TC], U[:, g, 0:TC],
                                       ALU.subtract))
            gp.dma_start(wpool[:, :, :], wpool_d).then_inc(d_wp, 16)
            gp.sem_inc(s_pool, 1)
            gp.wait_ge(s_mgl, KT)
            gp.dma_start(xres[:, :, :], x_d).then_inc(d_xr, 16)
            gp.wait_ge(s_rs2, 1)
            for x in range(2):
                gp.memset(f32(yh[:, x, :]), 0.0).then_inc(e_yh, 1)
                gp.memset(f32(yl[:, x, :]), 0.0).then_inc(e_yl, 1)
            gp.memset(f32(selT[:, :, :]), 0.0).then_inc(e_selT, 1)

        @block.scalar
        def _(act):
            act.dma_start(xT[:, :, :], x_d).then_inc(d_x, 16)
            smalls = [(cst[:, :], cst_d), (col[:, :], col_d), (cin[:, :, :], c_d),
                      (wgr[:, :, :], wg_d), (bg[:, :], bg_d), (m0[:, :], m0_d),
                      (wr[:, :, :], wr_d), (br[:, :], br_d)]
            for dst, src in smalls:
                act.dma_start(dst, src).then_inc(d_const, 16)
            act.sem_inc(blk_free, 4)
            st = Steps(act, a_steps)

            def split_hi(slot, use, p):
                act.wait_ge(raw_full[slot], (use + 1) * 16)
                act.activation(whi[p][:, :], raw[slot][:, :], ACT.Copy).then_inc(hi_ready, 1)

            def inv_rms(out, in_, n, sem_):
                st.do(act.activation(out, in_, ACT.Ln, bias=eps, scale=1.0 / n))
                act.activation(out, out, ACT.Exp, scale=-0.5).then_inc(sem_, 1)

            act.wait_ge(d_const, 16 * len(smalls))
            act.activation(csil[:, :, :], cin[:, :, :], ACT.Tanh, scale=0.5).then_inc(s_csil, 1)
            act.activation(wgh[:, :, :], wgr[:, :, :], ACT.Copy).then_inc(s_wgh, 1)
            act.wait_ge(d_x, 16)
            for k in range(KT):
                act.activation(hn[:, k, :], xT[:, k, :], ACT.Square).then_inc(s_sq, 1)
            act.wait_ge(s_ssq, 1)
            inv_rms(halves(rstd[:, :]), ps[:, 0:2, 0:HALF], D, s_rstd)
            for k in range(KT):
                act.wait_ge(s_hn, k + 1)
                act.activation(hhi[:, k, :], hn[:, k, :], ACT.Copy).then_inc(s_hhi, 1)
            split_hi(AT_QK % NRAW, AT_QK // NRAW, 0)
            act.wait_ge(s_gps, 1)
            act.activation(halves(gI[:, :]), ps[0:R16, 6:8, 0:HALF], ACT.Identity,
                           bias=bg[0:R16, :]).then_inc(s_gate, 1)
            act.activation(halves(gF[:, :]), ps[32:32 + R16, 6:8, 0:HALF], ACT.Identity,
                           bias=bg[32:32 + R16, :]).then_inc(s_gate, 1)
            act.wait_ge(s_lsg, 1)
            st.do(act.activation(gC[:, :], gC[:, :], ACT.Exp, scale=-1.0))
            act.activation(gC[:, :], gC[:, :], ACT.Ln, bias=cst[0:R16, C_ONE:C_ONE + 1])\
               .then_inc(s_gate, 1)

            with act.Fori(0, N_QK // NRAW) as i:
                for j in range(NRAW):
                    split_hi((j + 1) % NRAW, i + AT_QK // NRAW + (j + 1) // NRAW, (j + 1) % 2)
                    for b in range(2):
                        e = 2 * j + b
                        act.wait_ge(blk_ready, i * 8 + e + 1)
                        act.activation(halves(QK[:, i * 8 + e, :]), pair(e), ACT.Identity,
                                       bias=col[:, bass.ds(i * 8 + e + B_IN, 1)])\
                           .then_inc(blk_free, 1)
            def v_rows(v, e):
                act.wait_ge(blk_ready, e + 1)
                st.on(act.activation(Vt[:, 0:3, v, 0:DH], ps[:, 2 * (e % 4), 0:3 * P].rearrange(
                    "p (t n) -> p t n", n=P), ACT.Copy))
                act.activation(Vt[:, 3:5, v, 0:DH], ps[:, 2 * (e % 4) + 1, 0:2 * P].rearrange(
                    "p (t n) -> p t n", n=P), ACT.Copy).then_inc(blk_free, 1)

            e = E_V
            for v in range(H):
                if v % 2 == 0:
                    c = AT_V + v // 2 + 1
                    split_hi(c % NRAW, c // NRAW, (v // 2 + 1) % 2)
                act.wait_ge(blk_ready, e + 1)
                act.activation(halves(vst[v % 2][:, :]), pair(e), ACT.Identity,
                               bias=col[:, 16 + v:17 + v]).then_inc(blk_free, 1)
                e += 1
                if v:
                    v_rows(v - 1, e)
                    e += 1
            v_rows(H - 1, e)
            assert e + 1 == E_G8
            act.wait_ge(blk_ready, E_G8 + 1)
            gps = ps[:, 2 * (E_G8 % 4), :]
            st.on(act.activation(a_tok[:, :, :].rearrange("p t r -> p (t r)"), gps[:, 0:80], ACT.Copy))
            st.on(act.activation(wi_tok[:, 1:NT, :].rearrange("p t r -> p (t r)"), gps[:, 80:144],
                                 ACT.Exp))
            st.on(act.activation(em_tok[:, :, :].rearrange("p t r -> p (t r)"), gps[:, 144:224],
                                 ACT.Exp))
            act.activation(ws_tok[:, :], gps[:, 224:240], ACT.Exp).then_inc(blk_free, 1)
            act.wait_ge(blk_free, 4 + E_U)
            act.activation(ws_tok[:, :], ws_tok[:, :], ACT.Copy, scale=SCALE).then_inc(s_gtok, 1)
            for j in range(N_U):
                if j + 1 < N_U:
                    c = AT_U + j + 1
                    split_hi(c % NRAW, c // NRAW, (j + 1) % 2)
                for b in range(2):
                    e = E_U + 2 * j + b
                    act.wait_ge(blk_ready, e + 1)
                    act.activation(halves(U[:, 2 * j + b, :]), pair(e), ACT.Identity,
                                   bias=col[:, 24 + 2 * j + b:25 + 2 * j + b]).then_inc(blk_free, 1)

            act.wait_ge(s_gtok, 1)
            with act.Fori(0, H // 2) as i:
                for hp in range(2):
                    h = i * 2 + hp
                    act.activation(kst[hp][:, :], QK[:, h + H, :], ACT.Copy).then_inc(s_kst, 1)

                    def off_exp(d, j, o, t0, n):
                        st_h.on(act.activation(OFF[d][:, o:o + n], ps[:, 2 + d, t0:t0 + n], ACT.Exp,
                                               bias=a_tok[:, j + 1, bass.ds(h + d * H, 1)]))

                    def s_out(j):
                        act.wait_ge(s_sc, h * 5 + j + 2)
                        b = (j + 1) % 2
                        o, n = (2048, P) if j < 0 else (j * TL, TL)
                        act.activation(S[:, o:o + n], ps[:, b, 0:n], ACT.Copy, scale=SCALE)\
                           .then_inc(s_sev, 1)

                    st_h = Steps(act, a_head)
                    s_out(-1)
                    s_out(0)
                    act.wait_ge(s_tdg, h * 2 + 1)
                    for j in range(3):
                        off_exp(0, j, OFF_F[j], (j + 1) * P, (3 - j) * P)
                    s_out(1)
                    act.wait_ge(s_tdg, h * 2 + 2)
                    for j in range(1, 4):
                        off_exp(1, j, OFF_B[j - 1], 0, j * P)
                    for d in range(2):
                        act.activation(kw[d][:, :], ps[:, 4, 2 * P:3 * P], ACT.Copy,
                                       scale=ws_tok[:, bass.ds(h + d * H, 1)]).then_inc(s_kw, 1)
                    s_out(2)
                    s_out(3)
                    for d in range(2):
                        act.activation(DG[d][:, :, :], DG[d][:, :, :], ACT.Exp).then_inc(s_exp, 1)
                    act.wait_ge(s_pv, h * 6 + 6)
                    act.activation(stC[:, :, h, :], ps[:, 7, 0:2 * V1].rearrange(
                        "p (d n) -> p d n", n=V1), ACT.Copy).then_inc(pv7_free, 1)

            act.wait_ge(s_nm, H)
            split_hi(AT_O % NRAW, AT_O // NRAW, 0)
            for j in range(N_O):
                c = AT_O + j + 1
                split_hi(c % NRAW, c // NRAW, (j + 1) % 2)
                for b in range(2):
                    e, f = E_O + 2 * j + b, 2 * j + b
                    act.wait_ge(blk_ready, e + 1)
                    act.activation(halves(O[:, f, :]), pair(e), ACT.Tanh, scale=0.5,
                                   bias=col[:, 28 + f:29 + f]).then_inc(blk_free, 1)
                if j == 1:
                    act.wait_ge(s_hd, 1)
                    inv_rms(hss[:, :, :], hss[:, :, :], DH, s_o)
            act.wait_ge(blk_free, 4 + E_TH)
            with act.Fori(0, N_G // NRAW) as i:
                for j in range(NRAW):
                    c = AT_G + j + 1
                    split_hi(c % NRAW, i + c // NRAW, (j + 1) % 2)
                    for b in range(2):
                        f = 2 * j + b
                        act.wait_ge(blk_ready, i * 8 + E_TH + f + 1)
                        act.activation(halves(TH[:, i * 8 + f, :]), pair(E_TH + f), ACT.Tanh,
                                       scale=0.5, bias=col[:, bass.ds(i * 8 + 36 + f, 1)])\
                           .then_inc(blk_free, 1)
            for g in range(NG):
                act.wait_ge(blk_ready, E_PL + g + 1)
                act.activation(halves(ybh[:, g, :]), pair(E_PL + g), ACT.Copy,
                               scale=col[:, P_S + g:P_S + g + 1]).then_inc(s_ybh, 1)
            split_hi((AT_B + 1) % NRAW, (AT_B + 1) // NRAW, 1)
            for k in range(KT):
                act.activation(hhi[:, k, :], Y[:, k, :], ACT.Copy, scale=half_gn[:, k:k + 1])\
                   .then_inc(s_yh, 1)
            done = [E_B + 4, E_B + 8] + [E_A + 2 * j + 2 for j in range(6)]
            for j in range(N_A + N_OUT):
                c = AT_A + j
                act.wait_ge(blk_ready, done[j])
                split_hi(c % NRAW, c // NRAW, j % 2)
                if 2 <= j < 2 + N_A:
                    if j == 2:
                        act.wait_ge(s_yl, KT)
                    for k in (2 * j - 4, 2 * j - 3):
                        act.wait_ge(s_mg, k + 1)
                        act.activation(mgh[:, k, :], TH[:, k, :], ACT.Copy).then_inc(s_mgh, 1)
            for k in range(KT):
                act.wait_ge(s_xr, k + 1)
                act.activation(n2[:, k, :], xres[:, k, :], ACT.Square).then_inc(s_sq2, 1)

            def expert_hi(c, n=0, used=True):
                act.wait_ge(e_full[c % ERAW], (n * (ECH // ERAW) + c // ERAW + 1) * 16)
                if used:
                    act.wait_ge(e_mm, n * ECH + c - ESPL + 1)
                act.activation(ehi[c % ESPL][:, :], eraw[c % ERAW][:, :], ACT.Copy)\
                   .then_inc(e_hi, 1)

            act.wait_ge(blk_ready, E_END)
            for c in range(ESPL):
                expert_hi(c, used=False)
            act.wait_ge(s_ssq2, 1)
            inv_rms(halves(rs2[:, :]), ps[:, 0:2, 0:HALF], D, s_rs2)
            act.wait_ge(s_ex, 1)
            act.activation(t4[:, :, :], t4[:, :, :], ACT.Exp).then_inc(s_lg, 1)
            act.wait_ge(s_ex, 2)
            act.activation(r5[:, 4, :], r5[:, 4, :], ACT.Exp).then_inc(s_lg, 1)
            for t in range(NT):
                act.wait_ge(s_tkp, t + 1)
                act.activation(tkh[:, t, :].rearrange("p (a n) -> p a n", a=2),
                               ps[:, 4 + 2 * (t % 2):6 + 2 * (t % 2), :], ACT.Copy)\
                   .then_inc(s_tk, 1)

            def tokens_hi(a, count):
                act.wait_ge(e_gat, count)
                act.activation(xgh[:, 4 * a:4 * a + 4, :].rearrange("p (b k) n -> p b (k n)", b=2),
                               ps[:, 4 + 2 * a:6 + 2 * a, :], ACT.Copy).then_inc(e_xgh, 1)

            def tanh_gate(x, n):
                act.wait_ge(e_mm, n * ECH + 4 * x + 4)
                act.activation(th[:, :], ps[:, 0, :], ACT.Tanh, scale=0.5).then_inc(e_th, 1)

            def act_hi(x, n):
                act.wait_ge(e_aTp, n * 2 + x + 1)
                act.activation(aTh[:, :, :].rearrange("p f n -> p (f n)"), ps[:, 0, :],
                               ACT.Copy).then_inc(e_aTh, 1)

            def out_hi(x, n):
                act.wait_ge(e_mm, n * ECH + 10 + 2 * x)
                if x == 0:
                    act.wait_ge(e_selT, n + 2)
                act.activation(yh[:, x, :].rearrange("p (a n) -> p a n", a=2), ps[:, 2:4, :],
                               ACT.Copy, scale=wslot[:, x:x + 1]).then_inc(e_yh, 1)

            for a in range(2):
                tokens_hi(a, a + 1)
            act.wait_ge(s_cnt, 1)
            rounds = act.value_load(rounds_i[0:1, 0:1], min_val=1, max_val=ROUNDS)
            with act.Fori(0, rounds) as r:
                with act.Fori(0, NPAIR) as q:
                    n = r * NPAIR + q
                    for c in (3, 4, 5):
                        expert_hi(c, n)
                    tanh_gate(0, n)
                    expert_hi(6, n)
                    act_hi(0, n)
                    for c in (7, 8, 9):
                        expert_hi(c, n)
                    tanh_gate(1, n)
                    expert_hi(10, n)
                    act.wait_ge(e_selp, n + 1)
                    st_i = Steps(act, a_head)
                    flat = selT[:, :, :].rearrange("p x n -> p (x n)")
                    st_i.on(act.activation(flat[:, 0:1024].rearrange("p (a n) -> p a n", a=2),
                                           ps[:, 4:6, :], ACT.Copy))
                    st_i.on(act.activation(flat[:, 1024:2 * T], ps[:, 6, 0:2 * P], ACT.Copy))
                    act.activation(wslot[:, :], ps[:, 7, 0:2], ACT.Copy).then_inc(e_selT, 1)
                    expert_hi(11, n)
                    out_hi(0, n)
                    expert_hi(12, n)
                    act_hi(1, n)
                    for a in range(2):
                        tokens_hi(a, n * 2 + 3 + a)
                    expert_hi(13, n)
                    expert_hi(14, n)
                    out_hi(1, n)
            for k in range(KT):
                act.wait_ge(e_add, rounds * (NPAIR * KT) + k + 1)
                act.activation(h2[:, k, :], xres[:, k, :], ACT.Square).then_inc(s_sqf, 1)
            act.wait_ge(s_ssf, 1)
            inv_rms(halves(rs2[:, :]), ps[:, 0:2, 0:HALF], D, s_rsf)

        @block.vector
        def _(dve):
            st = Steps(dve, v_steps)

            def split_lo(slot, p, ci):
                dve.wait_ge(hi_ready, ci + 1)
                dve.tensor_tensor(wlo[p][:, :], raw[slot][:, :], f32(whi[p][:, :]), ALU.subtract)\
                   .then_inc(raw_free[slot], 1)

            def by(ap, shape):
                return ap.broadcast_to(shape)

            dve.sem_inc(m_free, 1)
            dve.sem_inc(qc5_free, 1)
            dve.sem_inc(qc1_free, 1)
            dve.sem_inc(pv6_free, 1)
            dve.sem_inc(pv7_free, 1)
            dve.wait_ge(d_const, 16 * 8)
            dve.wait_ge(s_csil, 1)
            st.do(dve.scalar_tensor_tensor(csil[:, :, :], csil[:, :, :], 1.0, cin[:, :, :],
                                           ALU.add, ALU.mult))
            dve.tensor_scalar(csil[:, :, :], csil[:, :, :], 0.5, None, ALU.mult).then_inc(s_csil, 1)
            st.on(dve.tensor_scalar(col[:, 28:52], col[:, 28:52], 0.5, None, ALU.mult))
            st.on(dve.tensor_scalar(half_gn[:, :], col[:, G_N:G_N + KT], 0.5, None, ALU.mult))
            dve.wait_ge(s_wgh, 1)
            dve.tensor_tensor(wgl[:, :, :], wgr[:, :, :], f32(wgh[:, :, :]), ALU.subtract)\
               .then_inc(s_wgl, 1)
            dve.wait_ge(raw_free[NRAW - 1], 1 + N_MOD1 // NRAW)
            st.do(dve.tensor_tensor(mod[:, 0:16, :], ps[:, 2, 0:32].rearrange("p (j c) -> p j c", c=2),
                                    by(col[:, B_MOD:B_MOD + 16].unsqueeze(2), [P, 16, 2]), ALU.add))
            st.do(dve.scalar_tensor_tensor(gain[:, :, :], mod[:, 8:16, :], 1.0,
                                           by(col[:, G_1:G_1 + KT].unsqueeze(2), [P, KT, 2]),
                                           ALU.add, ALU.mult))

            def modulate(dst, src, k, shift):
                return [dve.tensor_scalar(dst[:, k, a:b], src[:, k, a:b], gain[:, k, c:c + 1],
                                          mod[:, shift + k, c:c + 1], ALU.mult, ALU.add)
                        for c, a, b in ((0, 0, TC), (1, TC, T))]

            dve.wait_ge(s_rstd, 1)
            for k in range(KT):
                st.do(dve.tensor_tensor(hn[:, k, :], xT[:, k, :], rstd[:, :], ALU.mult))
                ctx_part, lat_part = modulate(hn, hn, k, 0)
                st.on(ctx_part)
                lat_part.then_inc(s_hn, 1)
            for k in range(KT):
                dve.wait_ge(s_hhi, k + 1)
                dve.tensor_tensor(hlo[:, k, :], hn[:, k, :], f32(hhi[:, k, :]), ALU.subtract)\
                   .then_inc(s_hlo, 1)
            split_lo(AT_QK % NRAW, 0, 0)
            dve.wait_ge(s_gate, 2)
            st.on(dve.tensor_scalar(gB[:, :], gF[:, :], 0.0, None, ALU.min))
            dve.scalar_tensor_tensor(gC[:, :], gF[:, :], -1.0, gF[:, :], ALU.mult, ALU.max)\
               .then_inc(s_lsg, 1)
            dve.wait_ge(s_gate, 3)
            st.wait()
            st.do(dve.tensor_tensor(gF[:, :], gB[:, :], gC[:, :], ALU.subtract))
            with dve.Fori(0, N_QK // NRAW) as i:
                for j in range(NRAW):
                    split_lo((j + 1) % NRAW, (j + 1) % 2, i * 4 + j + 1)
            split_lo((AT_V + 1) % NRAW, 1, CV + 1)

            mf, mb = cst[0:R16, C_MF:C_MF + 1], cst[0:R16, C_MB:C_MB + 1]
            segs = ((0, TC), (TC, T))

            def scans(dst_f, dst_b, src, initial, op):
                for (a, b), ini in zip(segs, initial):
                    st.on(dve.tensor_tensor_scan(dst_f[:, a:b], gOne[:, a:b], src[:, a:b], ini,
                                                 ALU.mult, op))
                    rev = slice(b - 1, a - 1 if a else None, -1)
                    st.on(dve.tensor_tensor_scan(dst_b[:, rev], gOne[:, rev], src[:, rev], ini,
                                                 ALU.mult, op))
                st.wait()

            def pick(dst, f, b):
                st.do(dve.tensor_scalar(f, f, mf, None, ALU.mult))
                st.do(dve.scalar_tensor_tensor(dst, b, mb, f, ALU.mult, ALU.add))

            dve.wait_ge(s_init, 1)
            scans(gA, gB, gF, (0.0, 0.0), ALU.add)
            pick(gF[:, :], gA[:, :], gB[:, :])
            split_lo((AT_V + 2) % NRAW, 0, CV + 2)
            st.do(dve.tensor_tensor(gA[:, :], gI[:, :], gF[:, :], ALU.subtract))
            scans(gB, gC, gA, (NEG, m0[:, :]), ALU.max)
            pick(gB[:, :], gB[:, :], gC[:, :])
            st.on(dve.tensor_scalar(negM[:, :], gB[:, :], -1.0, None, ALU.mult))
            st.on(dve.scalar_tensor_tensor(gC[:, :], gF[:, :], -1.0, gB[:, :], ALU.mult, ALU.subtract))
            for c, src in ((0, gB), (1, gF)):
                st.on(dve.tensor_scalar(mlast[:, 3:4], src[:, TC - 1:TC], mf, None, ALU.mult))
                st.wait()
                st.do(dve.scalar_tensor_tensor(mlast[:, c:c + 1], src[:, 0:1], mb, mlast[:, 3:4],
                                               ALU.mult, ALU.add))
            st.on(dve.tensor_tensor(mlast[:, 2:3], mlast[:, 0:1], mlast[:, 1:2], ALU.add))
            st.on(dve.tensor_scalar(gI[:, TC:T], negM[:, TC:T], m0[:, :], None, ALU.add))
            dve.tensor_scalar(gF[:, 0:TC], gA[:, 0:TC], mlast[:, 0:1], None, ALU.subtract)\
               .then_inc(s_grow, 1)
            split_lo((AT_V + 3) % NRAW, 1, CV + 3)
            split_lo(AT_U % NRAW, 0, CU)
            split_lo((AT_U + 1) % NRAW, 1, CU + 1)

            with dve.Fori(0, H // 2) as i:
                for hp in range(2):
                    h = i * 2 + hp
                    hs = Steps(dve, v_head)
                    hs.enter(h * HEAD_STEPS)
                    dve.tensor_copy(qst[hp][:, :], QK[:, h, :]).then_inc(s_qst, 1)
                    dve.wait_ge(s_m, h + 1)
                    for d in range(2):
                        neg = cst[:, (C_NEGF, C_NEGB)[d]:(C_NEGF, C_NEGB)[d] + P]
                        for t in range(NT):
                            src = ps[:, 4, d * P:(d + 1) * P] if t == 0 else \
                                ps[:, 2 + d, (t - 1) * P:t * P]
                            ins = dve.scalar_tensor_tensor(
                                DG[d][:, t, :], src, a_tok[:, t, bass.ds(h + d * H, 1)], neg,
                                ALU.add, ALU.min)
                            if t < NT - 1:
                                hs.on(ins)
                        ins.then_inc(s_tdg, 1)
                    c1 = AT_MOD2 + 2 * hp + 1
                    dve.wait_ge(raw_free[c1 % NRAW], i + c1 // NRAW + 2)
                    dve.tensor_tensor(mod[:, bass.ds(h * 4 + 16, 4), :],
                                      ps[:, 5, 0:8].rearrange("p (j c) -> p j c", c=2),
                                      by(col[:, bass.ds(h * 4 + B_MOD + 16, 4)].unsqueeze(2),
                                         [P, 4, 2]), ALU.add).then_inc(qc5_free, 1)
                    dve.wait_ge(s_sev, h * 5 + 5)
                    for d in range(2):
                        dve.wait_ge(s_exp, h * 2 + d + 1)
                        if d == 1:
                            dve.wait_ge(s_kw, h * 2 + 2)
                        dg = DG[d][:, 1:NT, :]
                        ins = dve.tensor_tensor(dg, dg, S[:, :].rearrange(
                            "p (j x) -> p j x", x=TL + P)[:, 0:NL, 0:P], ALU.mult)
                        if d == 1:
                            ins.then_inc(m_free, 1)
                        else:
                            hs.on(ins)
                        hs.on(dve.tensor_tensor(DG[d][:, 0, :], DG[d][:, 0, :], S[:, 2048:2048 + P],
                                                ALU.mult))
                        for j in (range(0, 3), range(1, 4))[d]:
                            o = (OFF_F, OFF_B)[d][j - d]
                            t0, n = ((j + 1) * P, (3 - j) * P) if d == 0 else (0, j * P)
                            ins = dve.tensor_tensor(OFF[d][:, o:o + n], OFF[d][:, o:o + n],
                                                    S[:, j * TL + t0:j * TL + t0 + n], ALU.mult)
                            if (d, j) == (1, 3):
                                ins.then_inc(s_p, 1)
                            else:
                                hs.on(ins)
                    dve.wait_ge(s_pv, h * 6 + 1)
                    dve.tensor_copy(num[:, 0, :, :], ps[:, 6, 0:2 * V1].rearrange(
                        "p (d n) -> p d n", n=V1)).then_inc(pv6_free, 1)
                    for t in range(NL):
                        dve.wait_ge(s_pv, h * 6 + 2 + t)
                        qc, qs = ((5, qc5_free), (1, qc1_free))[t % 2]
                        wi = wi_tok[:, t + 1, :].rearrange("p (d h) -> p d h", d=2)[:, :, bass.ds(h, 1)]
                        dve.tensor_tensor(num[:, t + 1, :, :], ps[:, qc, 0:2 * V1].rearrange(
                            "p (d n) -> p d n", n=V1), by(wi, [P, 2, V1]), ALU.mult).then_inc(qs, 1)
                        dve.wait_ge(qs, (h * 3 + 3 + t // 2) if qc == 5 else (h * 2 + 2 + t // 2))
                        pb, pf = ((7, pv7_free), (6, pv6_free))[t % 2]
                        dve.tensor_tensor(num[:, t + 1, :, :], num[:, t + 1, :, :],
                                          ps[:, pb, 0:2 * V1].rearrange("p (d n) -> p d n", n=V1),
                                          ALU.add).then_inc(pf, 1)
                    dve.wait_ge(pv6_free, h * 3 + 4)
                    dve.wait_ge(pv7_free, h * 3 + 3)
                    em = em_tok[:, :, :].rearrange("p t (d h) -> p t d h", d=2)[:, :, :, bass.ds(h, 1)]
                    den = num[:, :, :, DH:V1]
                    rv = rinv[:, :, :].unsqueeze(3)
                    hs.do(dve.scalar_tensor_tensor(rv, den, -1.0, den, ALU.mult, ALU.max))
                    hs.do(dve.tensor_tensor(rv, rv, em, ALU.max))
                    hs.do(dve.reciprocal(rinv[:, :, :], rinv[:, :, :]))
                    nn = num[:, :, :, 0:DH]
                    hs.do(dve.tensor_tensor(nn, nn, by(rinv[:, :, :].unsqueeze(3), [P, NT, 2, DH]),
                                            ALU.mult))
                    dve.wait_ge(s_pv, h * 6 + 6)
                    dve.tensor_tensor(Vt[:, :, h, 0:DH], num[:, :, 0, 0:DH], num[:, :, 1, 0:DH],
                                      ALU.add).then_inc(s_nm, 1)
                    assert hs.n == HEAD_STEPS, hs.n

            dve.wait_ge(s_nm, H)
            split_lo(AT_O % NRAW, 0, CO)
            split_lo((AT_O + 1) % NRAW, 1, CO + 1)
            tmp = Y[:, 0:2, :].rearrange("p a n -> p (a n)")[:, 0:H * DH].rearrange(
                "p (h n) -> p h n", n=DH)
            for t in range(NT):
                hv = Vt[:, t, :, 0:DH]
                st.do(dve.tensor_tensor(tmp, hv, hv, ALU.mult))
                ins = dve.tensor_reduce(hss[:, t, :], tmp, AX, ALU.add)
                if t < NT - 1:
                    st.do(ins)
                else:
                    ins.then_inc(s_hd, 1)
            split_lo((AT_O + 2) % NRAW, 0, CO + 2)
            split_lo((AT_O + 3) % NRAW, 1, CO + 3)
            dve.wait_ge(s_o, 1)
            for t in range(NT):
                hv = Vt[:, t, :, 0:DH]
                dve.tensor_tensor(hv, hv, by(hss[:, t, :].unsqueeze(2), [P, H, DH]), ALU.mult)\
                   .then_inc(s_hd, 1)
            split_lo(AT_G % NRAW, 0, CTH)
            for k in range(KT):
                e = E_Y + k
                dve.wait_ge(blk_free, 4 + E_Y)
                dve.wait_ge(blk_ready, e + 1)
                st.on(dve.scalar_tensor_tensor(Y[:, k, 0:3 * P], O[:, k, 0:3 * P], 1.0,
                                               ps[:, 2 * (e % 4), 0:3 * P], ALU.add, ALU.mult))
                dve.scalar_tensor_tensor(Y[:, k, 3 * P:T], O[:, k, 3 * P:T], 1.0,
                                         ps[:, 2 * (e % 4) + 1, 0:2 * P], ALU.add, ALU.mult)\
                   .then_inc(blk_free, 1)
            with dve.Fori(0, N_G // NRAW) as i:
                for j in range(NRAW):
                    split_lo((AT_G + j + 1) % NRAW, (j + 1) % 2, i * 4 + CTH + j + 1)
            for g in range(NG):
                dve.wait_ge(s_ybh, g + 1)
                dve.scalar_tensor_tensor(halves(ybl[:, g, :]), pair(E_PL + g),
                                         col[:, P_S + g:P_S + g + 1], halves(f32(ybh[:, g, :])),
                                         ALU.mult, ALU.subtract).then_inc(blk_free, 1)
            split_lo((AT_B + 1) % NRAW, 1, CB + 1)
            for k in range(KT):
                dve.wait_ge(s_yh, k + 1)
                dve.scalar_tensor_tensor(hlo[:, k, :], Y[:, k, :], half_gn[:, k:k + 1],
                                         f32(hhi[:, k, :]), ALU.mult, ALU.subtract).then_inc(s_yl, 1)
                e = E_B + k
                dve.wait_ge(blk_ready, e + 1)
                dve.scalar_tensor_tensor(halves(TH[:, k, :]), halves(TH[:, k, :]), 1.0, pair(e),
                                         ALU.add, ALU.mult).then_inc(blk_free, 1)
                if k in (3, 7):
                    split_lo((CA + k // 4 - CA + AT_A) % NRAW, (k // 4) % 2, CA + k // 4)
            dve.tensor_scalar(half_gate[:, :, :], mod[:, 16:24, :], 0.5, None, ALU.mult)\
               .then_inc(v_steps, 1)
            st.n += 1
            for k in range(KT):
                e = E_A + k
                dve.wait_ge(blk_free, 4 + E_B + k + 1)
                dve.wait_ge(blk_ready, e + 1)
                dve.scalar_tensor_tensor(halves(TH[:, KT + k, :]), halves(TH[:, KT + k, :]), 1.0,
                                         pair(e), ALU.add, ALU.mult).then_inc(blk_free, 1)
                dve.wait_ge(blk_free, 4 + e + 1)
                dve.tensor_tensor(TH[:, k, :], TH[:, k, :], TH[:, KT + k, :], ALU.add)\
                   .then_inc(s_mg, 1)
                if k % 2 == 1:
                    ci = CA + 2 + k // 2
                    split_lo((AT_A + 2 + k // 2) % NRAW, ci % 2, ci)
                    for kk in (k - 1, k):
                        dve.wait_ge(s_mgh, kk + 1)
                        dve.tensor_tensor(mgl[:, kk, :], TH[:, kk, :], f32(mgh[:, kk, :]),
                                          ALU.subtract).then_inc(s_mgl, 1)
            dve.wait_ge(d_xr, 16)
            st.wait()
            for k in range(KT):
                e = E_OUT + k
                dve.wait_ge(blk_ready, e + 1)
                pa, pb = ps[:, 2 * (e % 4), :], ps[:, 2 * (e % 4) + 1, :]
                for j, (c, src, a, b) in enumerate(((0, pa[:, 0:TC], 0, TC),
                                                    (1, pa[:, TC:HALF], TC, HALF),
                                                    (1, pb[:, 0:HALF], HALF, T))):
                    st.on(dve.scalar_tensor_tensor(xres[:, k, a:b], src, half_gate[:, k, c:c + 1],
                                                   xres[:, k, a:b], ALU.mult, ALU.add))
                st.wait()
                dve.sem_inc(blk_free, 1)
                dve.sem_inc(s_xr, 1)
                if k in (0, 2):
                    ci = COUT + 2 + k // 2
                    split_lo((AT_OUT + 2 + k // 2) % NRAW, ci % 2, ci)

            def expert_lo(c, n=0):
                dve.wait_ge(e_hi, n * ECH + c + 1)
                dve.tensor_tensor(elo[c % ESPL][:, :], eraw[c % ERAW][:, :],
                                  f32(ehi[c % ESPL][:, :]), ALU.subtract)\
                   .then_inc(e_free[c % ERAW], 1)

            st.do(dve.scalar_tensor_tensor(gain[:, :, :], mod[:, 32:40, :], 1.0,
                                           by(col[:, G_2:G_2 + KT].unsqueeze(2), [P, KT, 2]),
                                           ALU.add, ALU.mult))
            for c in range(ESPL):
                expert_lo(c)
            dve.wait_ge(s_rs2, 1)
            for k in range(KT):
                st.do(dve.tensor_tensor(h2[:, k, :], xres[:, k, :], rs2[:, :], ALU.mult))
                ctx_part, lat_part = modulate(h2, h2, k, 24)
                st.on(ctx_part)
                lat_part.then_inc(s_h2, 1)
            gm, se, v1, v2, ed, pw, wa, wb = (r5[:, i, :] for i in range(8))

            def over(ap, n):
                return by(ap.unsqueeze(2), [P, NT, n])

            def first_max(out, vals, mx):
                st.do(dve.tensor_tensor(t5[:, :, :], vals, over(mx, 4), ALU.is_equal))
                wt = cst[:, C_WT:C_WT + 4 * NT].rearrange("p (t n) -> p t n", n=4)
                st.do(dve.tensor_tensor(t5[:, :, :], t5[:, :, :], wt, ALU.mult))
                st.do(dve.tensor_reduce(r5[:, 8, :], t5[:, :, :], AX, ALU.max))
                st.do(dve.tensor_tensor(out, t5[:, :, :], over(r5[:, 8, :], 4), ALU.is_equal))

            dve.wait_ge(s_rk, 1)
            st.do(dve.tensor_tensor(lg[:, :, :], ps[:, 2, 0:NT * (EG + NE)].rearrange(
                "p (t n) -> p t n", t=NT), by(br[:, :].unsqueeze(1), [P, NT, EG + NE]), ALU.add))
            gl = lg[:, :, 0:EG]
            st.do(dve.tensor_reduce(gm, gl, AX, ALU.max))
            dve.tensor_tensor(t4[:, :, :], gl, over(gm, EG), ALU.subtract).then_inc(s_ex, 1)
            first_max(goh[:, :, :], gl, gm)
            le = lg[:, :, EG:].rearrange("p t (g e) -> p t g e", g=EG)
            st.do(dve.tensor_tensor(t16[:, :, :, :], le, by(goh[:, :, :].unsqueeze(3),
                                                            [P, NT, EG, EE]), ALU.mult))
            st.do(dve.tensor_reduce(les[:, :, :], t16[:, :, :, :].rearrange("p t g e -> p t e g"),
                                    AX, ALU.add))
            st.do(dve.tensor_reduce(v1, les[:, :, :], AX, ALU.max))
            first_max(o1[:, :, :], les[:, :, :], v1)
            st.do(dve.scalar_tensor_tensor(les[:, :, :], o1[:, :, :], NEG, les[:, :, :],
                                           ALU.mult, ALU.add))
            st.do(dve.tensor_reduce(v2, les[:, :, :], AX, ALU.max))
            dve.tensor_tensor(ed, v2, v1, ALU.subtract).then_inc(s_ex, 1)
            first_max(o2[:, :, :], les[:, :, :], v2)
            st.on(dve.tensor_tensor(t5[:, :, :], o1[:, :, :], o2[:, :, :], ALU.add))
            dve.wait_ge(s_lg, 2)
            st.wait()
            am4 = am[:, :, :].rearrange("p t (g e) -> p t g e", g=EG)
            gb = by(goh[:, :, :].unsqueeze(3), [P, NT, EG, EE])
            dve.tensor_tensor(am4, by(t5[:, :, :].unsqueeze(2), [P, NT, EG, EE]), gb, ALU.mult)\
               .then_inc(s_am, 1)
            st.do(dve.tensor_reduce(se, t4[:, :, :], AX, ALU.add))
            st.do(dve.scalar_tensor_tensor(pw, ed, 1.0, se, ALU.add, ALU.mult))
            st.do(dve.reciprocal(wa, pw))
            st.do(dve.tensor_scalar(wa, wa, 0.5, None, ALU.mult))
            st.do(dve.tensor_tensor(wb, wa, ed, ALU.mult))
            st.on(dve.tensor_tensor(o1[:, :, :], o1[:, :, :], over(wa, EE), ALU.mult))
            st.do(dve.tensor_tensor(o2[:, :, :], o2[:, :, :], over(wb, EE), ALU.mult))
            st.do(dve.tensor_tensor(o1[:, :, :], o1[:, :, :], o2[:, :, :], ALU.add))
            st.do(dve.tensor_tensor(wtok[:, :, :].rearrange("p t (g e) -> p t g e", g=EG),
                                    by(o1[:, :, :].unsqueeze(2), [P, NT, EG, EE]), gb, ALU.mult))
            dve.wait_ge(s_rk, 2)
            rk = ps[:, 3, 0:NT * NE].rearrange("p (t n) -> p t n", t=NT)
            st.do(dve.scalar_tensor_tensor(rank[:, :, 0:NE], rk, 1.0, am[:, :, :], ALU.add, ALU.mult))
            st.do(dve.tensor_scalar(rank[:, :, 0:NE], rank[:, :, 0:NE], -1.0, None, ALU.add))
            st.do(dve.tensor_scalar(rank[:, :, NE:NE + 2], rank[:, :, 0:2], -float(SLOTS), None,
                                    ALU.add))
            st.do(dve.tensor_reduce(thr[:, 5:6], ps[:, 3, NT * NE:NT * NE + NE], AX, ALU.max))
            st.do(dve.tensor_scalar(thr[:, 0:5], cst[:, C_THR:C_THR + ROUNDS], thr[:, 5:6], None,
                                    ALU.is_lt))
            st.do(dve.tensor_reduce(thr[:, 6:7], thr[:, 0:5], AX, ALU.add))
            dve.tensor_copy(rounds_i[0:1, 0:1], thr[0:1, 6:7]).then_inc(s_cnt, 1)
            for t in range(NT):
                dve.wait_ge(s_tk, t + 1)
                dve.tensor_tensor(tkl[:, t, :].rearrange("p (a n) -> p a n", a=2),
                                  ps[:, 4 + 2 * (t % 2):6 + 2 * (t % 2), :],
                                  f32(tkh[:, t, :]).rearrange("p (a n) -> p a n", a=2),
                                  ALU.subtract).then_inc(s_tkl, 1)

            def choose(q):
                at_ = slice(0, 2) if q is None else bass.ds(q * 2 + 2, 2)
                shape = [P, NT, 2, SLOTS]
                dve.tensor_tensor(sel[:, :, :].rearrange("p t (x n) -> p t x n", x=2),
                                  by(iota.unsqueeze(1).unsqueeze(1), shape),
                                  by(rank[:, :, at_].unsqueeze(3), shape), ALU.is_equal)\
                   .then_inc(e_sel, 1)

            def tokens_lo(a, count):
                dve.wait_ge(e_xgh, count)
                hi, lo = (x[:, 4 * a:4 * a + 4, :].rearrange("p (b k) n -> p b (k n)", b=2)
                          for x in (xgh, xgl))
                dve.tensor_tensor(lo, ps[:, 4 + 2 * a:6 + 2 * a, :], f32(hi), ALU.subtract)\
                   .then_inc(e_xgl, 1)

            def add_out(k, count, steps):
                dve.wait_ge(e_cmb, count)
                b = 2 + 2 * (k % 3)
                for c, src, a0, b0 in ((0, ps[:, b, 0:TC], 0, TC), (1, ps[:, b, TC:HALF], TC, HALF)):
                    steps.on(dve.scalar_tensor_tensor(xres[:, k, a0:b0], src,
                                                      mod[:, 40 + k, c:c + 1],
                                                      xres[:, k, a0:b0], ALU.mult, ALU.add))
                dve.scalar_tensor_tensor(xres[:, k, HALF:T], ps[:, b + 1, 0:HALF],
                                         mod[:, 40 + k, 1:2], xres[:, k, HALF:T],
                                         ALU.mult, ALU.add).then_inc(e_add, 1)

            def inner(x, n, steps):
                dve.wait_ge(e_th, n * 2 + x + 1)
                steps.do(dve.scalar_tensor_tensor(act_[:, :], th[:, :], 1.0, ps[:, 0, :],
                                                  ALU.add, ALU.mult))
                dve.tensor_tensor(act_[:, :], act_[:, :], ps[:, 1, :], ALU.mult)\
                   .then_inc(e_act, 1)

            def act_lo(x, n):
                dve.wait_ge(e_aTh, n * 2 + x + 1)
                dve.tensor_tensor(aTl[:, :, :].rearrange("p f n -> p (f n)"), ps[:, 0, :],
                                  f32(aTh[:, :, :]).rearrange("p f n -> p (f n)"),
                                  ALU.subtract).then_inc(e_aTl, 1)

            def out_lo(x, n):
                dve.wait_ge(e_yh, n * 2 + 3 + x)
                dve.scalar_tensor_tensor(yl[:, x, :].rearrange("p (a n) -> p a n", a=2),
                                         ps[:, 2:4, :], wslot[:, x:x + 1],
                                         f32(yh[:, x, :]).rearrange("p (a n) -> p a n", a=2),
                                         ALU.mult, ALU.subtract).then_inc(e_yl, 1)

            choose(None)
            for a in range(2):
                tokens_lo(a, a + 1)
            dve.wait_ge(s_cnt, 1)
            rounds = dve.value_load(rounds_i[0:1, 0:1], min_val=1, max_val=ROUNDS)
            with dve.Fori(0, rounds) as r:
                with dve.Fori(0, NPAIR) as q:
                    n = r * NPAIR + q
                    it = Steps(dve, v_item)
                    it.enter(n * PAIR_STEPS)
                    for c in (3, 4, 5):
                        expert_lo(c, n)
                    inner(0, n, it)
                    for k in range(4):
                        add_out(k, n * KT + k + 1, it)
                    act_lo(0, n)
                    for k in range(4, KT):
                        add_out(k, n * KT + k + 1, it)
                    for c in (6, 7, 8, 9):
                        expert_lo(c, n)
                    inner(1, n, it)
                    dve.wait_ge(e_selp, n + 1)
                    choose(q)
                    expert_lo(10, n)
                    expert_lo(11, n)
                    out_lo(0, n)
                    act_lo(1, n)
                    expert_lo(12, n)
                    for a in range(2):
                        tokens_lo(a, n * 2 + 3 + a)
                    expert_lo(13, n)
                    expert_lo(14, n)
                    out_lo(1, n)
                    assert it.n == PAIR_STEPS, it.n
                dve.tensor_scalar(rank[:, :, :], rank[:, :, :], -float(SLOTS), None, ALU.add)\
                   .then_inc(s_round, 1)
                dve.wait_ge(s_round, r + 1)
            for k in range(KT):
                add_out(k, rounds * (NPAIR * KT) + k + 1, st)
            dve.wait_ge(s_rsf, 1)
            for k in range(KT):
                dve.scalar_tensor_tensor(yout[:, k, :], xres[:, k, :], col[:, G_F + k:G_F + k + 1],
                                         rs2[:, :], ALU.mult, ALU.mult).then_inc(s_yo, 1)

        @block.tensor
        def _(pe):
            def mm(out, lhsT, rhs, start, stop):
                return nc.tensor.matmul(out, lhsT, rhs, start=start, stop=stop)

            def three(groups, lh, ll, rh, rl, start, stop):
                for l, r, a, b in ((lh, rh, start, False), (lh, rl, False, False),
                                   (ll, rh, False, stop)):
                    for out, cut in groups:
                        last = mm(out, l, cut(r), a, b)
                return last

            def cut_half(a):
                return lambda r: r[:, a * HALF:(a + 1) * HALF]

            def block_out(e, wh, wl, kt, at_w, rh, rl):
                groups = [(pair(e)[:, a, :], cut_half(a)) for a in range(2)]
                for k in range(kt):
                    o = at_w + k * P
                    last = three(groups, wh[:, o:o + P], wl[:, o:o + P], rh[:, k, :], rl[:, k, :],
                                 k == 0, k == kt - 1)
                return last

            def chunk_split(slot, use):
                pe.wait_ge(raw_free[slot], use + 2)

            def dense(c, p, e0, i=0, rh=hhi, rl=hlo, kt=KT, per_i=0, between=None):
                chunk_split(c % NRAW, i + c // NRAW)
                for b in range(CH // (kt * P)):
                    pe.wait_ge(blk_free, i * per_i + e0 + b + 1)
                    block_out(e0 + b, whi[p], wlo[p], kt, b * kt * P, rh, rl).then_inc(blk_ready, 1)

            pe.wait_ge(d_const, 16 * 8)
            for k in range(KT):
                pe.wait_ge(s_sq, k + 1)
                for a in range(2):
                    last = mm(ps[:, a, 0:HALF], ones, hn[:, k, a * HALF:(a + 1) * HALF],
                              k == 0, k == KT - 1)
            last.then_inc(s_ssq, 1)
            pe.wait_ge(s_csil, 2)

            def mod_chunk(slot, use, bank, j0):
                pe.wait_ge(raw_full[slot], (use + 1) * 16)
                for b in range(2):
                    for k in range(KT):
                        o = (b * KT + k) * P
                        last = mm(ps[:, bank, 2 * (j0 + b):2 * (j0 + b) + 2], raw[slot][:, o:o + P],
                                  csil[:, k, :], k == 0, k == KT - 1)
                last.then_inc(raw_free[slot], 1)

            for c in range(N_MOD1):
                mod_chunk(c % NRAW, c // NRAW, 2, 2 * c)
            pe.wait_ge(s_wgl, 1)
            for k in range(KT):
                pe.wait_ge(s_hlo, k + 1)
                last = three([(ps[0:GP, 6 + a, 0:HALF], cut_half(a)) for a in range(2)],
                             wgh[:, k, :], wgl[:, k, :], hhi[:, k, :], hlo[:, k, :],
                             k == 0, k == KT - 1)
            last.then_inc(s_gps, 1)
            pe.wait_ge(s_gate, 2)
            with pe.Fori(0, N_QK // NRAW) as i:
                for j in range(NRAW):
                    dense(AT_QK + j, j % 2, 2 * j, i, per_i=8)

            def v_rows(v, e):
                pe.wait_ge(blk_free, 4 + E_V + max(2 * v - 1, 0) + 1)
                pe.wait_ge(blk_free, e + 1)
                for t in range(NT):
                    last = nc.tensor.transpose(
                        ps[:, 2 * (e % 4) + t // 3, (t % 3) * P:(t % 3 + 1) * P],
                        vst[v % 2][:, t * P:(t + 1) * P], ident)
                last.then_inc(blk_ready, 1)

            e = E_V
            for v in range(H):
                c, p = AT_V + v // 2, (v // 2) % 2
                if v % 2 == 0:
                    chunk_split(c % NRAW, c // NRAW)
                pe.wait_ge(blk_free, e + 1)
                block_out(e, whi[p], wlo[p], KT, (v % 2) * KT * P, hhi, hlo).then_inc(blk_ready, 1)
                e += 1
                if v:
                    v_rows(v - 1, e)
                    e += 1
            v_rows(H - 1, e)
            pe.wait_ge(s_grow, 1)
            pe.wait_ge(blk_free, E_G8 + 1)
            g0 = 2 * (E_G8 % 4)
            for t in range(NT):
                for src, o in ((gA, 0), (gI, 64), (gC, 144)):
                    if t or src is not gI:
                        nc.tensor.transpose(ps[:, g0, o + t * R16:o + (t + 1) * R16],
                                            src[:, t * P:(t + 1) * P], ident[0:R16, 0:R16])
            nc.tensor.transpose(ps[:, g0, 224:240], gF[:, 0:P], ident[0:R16, 0:R16])\
              .then_inc(blk_ready, 1)
            for j in range(N_U):
                dense(AT_U + j, j % 2, E_U + 2 * j)

            pe.wait_ge(blk_free, 4 + E_O)
            pe.wait_ge(d_st, 16)
            pe.wait_ge(s_init, 2)
            with pe.Fori(0, H // 2) as i:
                for hp in range(2):
                    h = i * 2 + hp
                    pe.wait_ge(s_mrow, h * 2 + 2)
                    pe.wait_ge(m_free, h + 1)
                    for d in range(2):
                        mm(ps[:, 2 + d, :], ones[0:R16, :], mrow[d][:, TC:T], True, True)
                    for d in range(2):
                        mm(ps[:, 4, d * P:(d + 1) * P], ones[0:R16, :], mrow[d][:, 0:TC], True, True)
                    pe.wait_ge(s_kst, h + 1)
                    nc.tensor.transpose(ps[:, 4, 2 * P:3 * P], kst[hp][:, 0:P], ident).then_inc(s_m, 1)
                    pe.wait_ge(s_qst, h + 1)
                    mm(ps[:, 0, 0:P], kst[hp][:, 0:P], qst[hp][:, 0:P], True, True).then_inc(s_sc, 1)
                    pe.wait_ge(qc1_free, h * 2 + 1)
                    for j in range(NL):
                        if j:
                            pe.wait_ge(s_sev, h * 5 + j)
                        mm(ps[:, (j + 1) % 2, :], kst[hp][:, (j + 1) * P:(j + 2) * P],
                           qst[hp][:, TC:T], True, True).then_inc(s_sc, 1)
                    pe.wait_ge(qc5_free, h * 3 + 1)
                    for c2 in range(2):
                        c = AT_MOD2 + 2 * hp + c2
                        mod_chunk(c % NRAW, i + c // NRAW, 5, 2 * c2)
                    def pv(t, bank, free):
                        pe.wait_ge(*free)
                        for d in range(2):
                            tiles = [t] if t == 0 else (range(1, t + 1), range(t, NT))[d]
                            for s in tiles:
                                if s == t:
                                    w = DG[d][:, t, :]
                                elif d == 0:
                                    o = OFF_F[s - 1] + (t - s - 1) * P
                                    w = OFF[0][:, o:o + P]
                                else:
                                    o = OFF_B[s - 2] + (t - 1) * P
                                    w = OFF[1][:, o:o + P]
                                last = mm(ps[:, bank, d * V1:(d + 1) * V1], w, Vt[:, s, h, :],
                                          s == tiles[0], s == tiles[-1])
                        last.then_inc(s_pv, 1)

                    pe.wait_ge(s_p, h + 1)
                    pv(0, 6, (pv6_free, h * 3 + 1))
                    for t in range(NL):
                        if t % 2 == 0:
                            pe.wait_ge(qc5_free, h * 3 + 2 + t // 2)
                        else:
                            pe.wait_ge(qc1_free, h * 2 + 1 + t // 2)
                        mm(ps[:, (5, 1)[t % 2], 0:2 * V1].rearrange("p (d n) -> p d n", n=V1),
                           qst[hp][:, (t + 1) * P:(t + 2) * P], stC[:, :, h, :], True, True)
                        pv(t + 1, (7, 6)[t % 2],
                           (pv7_free, h * 3 + 1 + t // 2) if t % 2 == 0
                           else (pv6_free, h * 3 + 2 + t // 2))
                    pe.wait_ge(s_kw, h * 2 + 2)
                    pe.wait_ge(pv7_free, h * 3 + 3)
                    for d in range(2):
                        last = mm(ps[:, 7, d * V1:(d + 1) * V1], kw[d][:, :], Vt[:, 0, h, :],
                                  True, True)
                    last.then_inc(s_pv, 1)

            for s_, v_ in ((pv6_free, 1 + 3 * H), (pv7_free, 1 + 3 * H), (qc1_free, 1 + 2 * H),
                           (qc5_free, 1 + 3 * H), (m_free, 1 + H), (s_sev, 5 * H)):
                pe.wait_ge(s_, v_)
            for j in range(N_O):
                dense(AT_O + j, j % 2, E_O + 2 * j)
            for k in range(H):
                e = E_Y + k
                pe.wait_ge(s_hd, 1 + NT)
                pe.wait_ge(blk_free, e + 1)
                for t in range(NT):
                    last = nc.tensor.transpose(
                        ps[:, 2 * (e % 4) + t // 3, (t % 3) * P:(t % 3 + 1) * P],
                        Vt[:, t, k, 0:DH], ident)
                last.then_inc(blk_ready, 1)
            with pe.Fori(0, N_G // NRAW) as i:
                for j in range(NRAW):
                    dense(AT_G + j, j % 2, E_TH + 2 * j, i, per_i=8)
            pe.wait_ge(s_pool, 1)
            pe.wait_ge(d_wp, 16)
            for g in range(NG):
                e = E_PL + g
                pe.wait_ge(blk_free, e + 1)
                for a in range(2):
                    last = mm(pair(e)[:, a, :], wpool[:, g, :], U[:, g, a * HALF:(a + 1) * HALF],
                              True, True)
                last.then_inc(blk_ready, 1)
            pe.wait_ge(blk_free, 4 + E_B)
            for j in range(N_B):
                dense(AT_B + j, j % 2, E_B + 4 * j, rh=ybh, rl=ybl, kt=NG)
            pe.wait_ge(s_yl, KT)
            for j in range(N_A):
                dense(AT_A + j, j % 2, E_A + 2 * j)
            pe.wait_ge(s_mgl, KT)
            for j in range(N_OUT):
                dense(AT_OUT + j, j % 2, E_OUT + 2 * j, rh=mgh, rl=mgl)
            pe.wait_ge(blk_free, 4 + E_END)
            for k in range(KT):
                pe.wait_ge(s_sq2, k + 1)
                for a in range(2):
                    last = mm(ps[:, a, 0:HALF], ones, n2[:, k, a * HALF:(a + 1) * HALF],
                              k == 0, k == KT - 1)
            last.then_inc(s_ssq2, 1)
            pe.wait_ge(s_h2, KT)
            for t in range(NT):
                for k in range(KT):
                    last = mm(ps[:, 2, t * (EG + NE):(t + 1) * (EG + NE)],
                              h2[:, k, t * P:(t + 1) * P], wr[:, k, :], k == 0, k == KT - 1)
            last.then_inc(s_rk, 1)
            def token_major(t):
                if t >= 2:
                    pe.wait_ge(s_tkl, t - 1)
                for k in range(KT):
                    last = nc.tensor.transpose(ps[:, 4 + 2 * (t % 2) + k // 4, (k % 4) * P:
                                                  (k % 4 + 1) * P], h2[:, k, t * P:(t + 1) * P], ident)
                last.then_inc(s_tkp, 1)

            for t in range(2):
                token_major(t)
            pe.wait_ge(s_am, 1)
            for t in range(NT + 1):
                out = ps[:, 3, t * NE:(t + 1) * NE]
                for u in range(min(t + 1, NT)):
                    last = mm(out, ones if u < t else cst[:, C_STRICT:C_STRICT + P], am[:, u, :],
                              u == 0, u == min(t, NT - 1))
            last.then_inc(s_rk, 1)
            for t in range(2, NT):
                token_major(t)

            def gather():
                for k in range(KT):
                    out = ps[:, 4 + k // 2, (k % 2) * 2 * SLOTS:(k % 2 + 1) * 2 * SLOTS]
                    for t in range(NT):
                        for src in (tkh, tkl):
                            last = mm(out, src[:, t, k * P:(k + 1) * P], sel[:, t, :],
                                      t == 0 and src is tkh, t == NT - 1 and src is tkl)
                    if k % 4 == 3:
                        last.then_inc(e_gat, 1)

            def combine(adds, k):
                if k >= 3:
                    pe.wait_ge(e_add, adds + k - 2)
                b = 2 + 2 * (k % 3)
                parts = [(x, src) for x in range(2) for src in (yh, yl)]
                for x, src in parts:
                    for a in range(2):
                        last = mm(ps[:, b + a, 0:HALF], src[:, x, k * P:(k + 1) * P],
                                  selT[:, x, a * HALF:(a + 1) * HALF],
                                  (x, src) == parts[0], (x, src) == parts[-1])
                last.then_inc(e_cmb, 1)

            def outputs_split(n):
                pe.wait_ge(e_yh, n * 2 + 2)
                pe.wait_ge(e_yl, n * 2 + 2)
                pe.wait_ge(e_selT, n + 1)

            def chunk(c, n):
                pe.wait_ge(e_free[c % ERAW], n * (ECH // ERAW) + c // ERAW + 2)
                return ehi[c % ESPL], elo[c % ESPL]

            def gate_up(x, n):
                for c in range(4):
                    hi, lo = chunk(4 * x + c, n)
                    for k in range(4):
                        kk = (c % 2) * 4 + k
                        last = three([(ps[:, c // 2, :], lambda w, k=k: w[:, k * DE:(k + 1) * DE])],
                                     xgh[:, kk, x * SLOTS:(x + 1) * SLOTS],
                                     xgl[:, kk, x * SLOTS:(x + 1) * SLOTS], hi, lo,
                                     kk == 0, kk == KT - 1)
                    last.then_inc(e_mm, 1)

            def inner_T(x, n):
                pe.wait_ge(e_act, n * 2 + x + 1)
                for f in range(FT):
                    last = nc.tensor.transpose(ps[:, 0, f * P:(f + 1) * P],
                                               act_[:, f * P:(f + 1) * P], ident)
                last.then_inc(e_aTp, 1)

            def down(x, n):
                for c in range(2):
                    hi, lo = chunk(8 + 2 * x + c, n)
                    for f2 in range(2):
                        f = 2 * c + f2
                        groups = [(ps[:, 2 + a, :], lambda w, a=a, f2=f2:
                                   w[:, (2 * f2 + a) * 512:(2 * f2 + a + 1) * 512])
                                  for a in range(2)]
                        last = three(groups, aTh[:, f, :], aTl[:, f, :], hi, lo,
                                     f == 0, f == FT - 1)
                    last.then_inc(e_mm, 1)

            pe.wait_ge(s_tkl, NT)
            pe.wait_ge(e_sel, 1)
            gather()
            pe.wait_ge(s_cnt, 1)
            rounds = pe.value_load(rounds_i[0:1, 0:1], min_val=1, max_val=ROUNDS)
            with pe.Fori(0, rounds) as r:
                with pe.Fori(0, NPAIR) as q:
                    n = r * NPAIR + q
                    pe.wait_ge(e_xgl, n * 2 + 2)
                    gate_up(0, n)
                    outputs_split(n)
                    for k in range(4):
                        combine(n * KT, k)
                    inner_T(0, n)
                    for k in range(4, KT):
                        combine(n * KT, k)
                    pe.wait_ge(e_aTl, n * 2 + 1)
                    gate_up(1, n)
                    pe.wait_ge(e_add, n * KT + KT)
                    for x in range(2):
                        for t in range(NT):
                            o = x * NT + t
                            nc.tensor.transpose(ps[:, 4 + o // 4, (o % 4) * P:(o % 4 + 1) * P],
                                                f32(sel[:, t, x * SLOTS:(x + 1) * SLOTS]), ident)
                        for t in range(NT):
                            last = mm(ps[:, 7, x:x + 1], f32(sel[:, t, x * SLOTS:(x + 1) * SLOTS]),
                                      wtok[:, t, bass.ds(q * 2 + x, 1)], t == 0, t == NT - 1)
                    last.then_inc(e_selp, 1)
                    down(0, n)
                    inner_T(1, n)
                    pe.wait_ge(e_sel, n + 2)
                    pe.wait_ge(e_selT, n + 2)
                    gather()
                    pe.wait_ge(e_aTl, n * 2 + 2)
                    pe.wait_ge(e_yl, n * 2 + 3)
                    down(1, n)
            pe.wait_ge(e_xgl, rounds * (NPAIR * 2) + 2)
            outputs_split(rounds * NPAIR)
            for k in range(KT):
                combine(rounds * (NPAIR * KT), k)
            for k in range(KT):
                pe.wait_ge(s_sqf, k + 1)
                for a in range(2):
                    last = mm(ps[:, a, 0:HALF], ones, h2[:, k, a * HALF:(a + 1) * HALF],
                              k == 0, k == KT - 1)
            last.then_inc(s_ssf, 1)


def _constants():
    c = np.zeros((P, C_END), np.float32)
    r, q = np.arange(P)[:, None], np.arange(P)[None, :]
    c[:, C_ID:C_ID + P] = r == q
    c[:, C_ONE:C_ONE + P] = 1
    c[:, C_STRICT:C_STRICT + P] = r < q
    c[:, C_IOTA:C_IOTA + P] = q
    c[:, C_NEGF:C_NEGF + P] = np.where(r <= q, 0, NEG)
    c[:, C_NEGB:C_NEGB + P] = np.where(r >= q, 0, NEG)
    c[:H, C_MF] = 1
    c[H:R16, C_MB] = 1
    c[:, C_WT:C_WT + 4 * NT] = np.tile([8, 4, 2, 1], NT)
    c[:, C_THR:C_THR + ROUNDS] = np.arange(ROUNDS) * SLOTS
    c[:, C_EPS] = EPS
    cnt = np.zeros((NG, T), np.float32)

    def width(n, w):
        i = np.arange(n)
        return np.clip(i - w // 2 + w, 0, n) - np.clip(i - w // 2, 0, n)

    for g, w in enumerate(WIN):
        cnt[g, :TC] = width(TC, w)
        cnt[g, TC:] = np.outer(width(GR, w), width(GW, w)).ravel()
    return c, np.ascontiguousarray(np.broadcast_to(1 / cnt, (P, NG, T)), dtype=np.float32)


def _layout(i):
    i = {k: np.asarray(v) for k, v in i.items()}
    fm = lambda a: a.T.reshape(KT, P, -1).transpose(1, 0, 2)
    cols = lambda v: v.reshape(-1, P).T

    def chunks(w, kt):
        nb, per = w.shape[1] // P, CH // (kt * P)
        return w.reshape(kt, P, nb, P).transpose(2, 1, 0, 3).reshape(
            nb // per, per, P, kt * P).transpose(0, 2, 1, 3).reshape(nb // per, P, CH)

    w, b = i["w_in"][0], i["b_in"][0]
    g0 = 4 * D
    pool, ga, gb = g0 + 4 * H, g0 + 4 * H + NG * P, g0 + 4 * H + NG * P + D
    qkvu = np.r_[0:3 * D, pool:pool + NG * P]
    late = np.r_[3 * D:4 * D, gb:gb + D, ga:ga + D]
    wm = chunks(i["w_mod"][0], KT)
    wst = np.concatenate([wm[:N_MOD1], chunks(w[:, qkvu], KT), wm[N_MOD1:], chunks(w[:, late], KT),
                          chunks(i["w_proj_b"][0], NG), chunks(i["w_proj_a"][0], KT),
                          chunks(i["w_out"][0], KT)])
    wg = np.zeros((P, KT, GP), np.float32)
    bg = np.zeros((GP, 1), np.float32)
    for dst, src in ((0, 0), (8, 16), (32, 8), (40, 24)):
        wg[:, :, dst:dst + H] = w[:, g0 + src:g0 + src + H].reshape(KT, P, H).transpose(1, 0, 2)
        bg[dst:dst + H, 0] = b[g0 + src:g0 + src + H]
    col = np.concatenate([cols(b[qkvu]), cols(b[late]), cols(i["b_mod"][0]), cols(i["g_norm1"][0]),
                          cols(i["g_norm2"][0]), cols(i["g_final"]), cols(i["gn_gain"][0]),
                          cols(i["pool_scale"][0])], axis=1)
    wr = np.concatenate([i["w_router_grp"][0], i["w_router_exp"][0].reshape(D, NE)], 1)
    br = np.concatenate([i["b_router_grp"][0], i["b_router_exp"][0].reshape(NE)])
    st = np.concatenate([i["state_C"][0, 0], i["state_n"][0, 0][..., None]], -1)
    up = lambda a: a.reshape(NPAIR, 2, 2, 4, P, DE).transpose(0, 1, 2, 4, 3, 5).reshape(
        NPAIR, 2, 2, P, CH)
    down = i["w_exp_down"][0].reshape(NPAIR, 4, 2, P, D).transpose(0, 1, 3, 2, 4).reshape(
        NPAIR, 4, P, CH)
    gu = np.stack([up(i["w_exp_gate"][0]), up(i["w_exp_up"][0])], 2).reshape(NPAIR, 8, P, CH)
    ex = np.concatenate([gu, down], 1)
    cst, rcnt = _constants()
    return dict(
        x=fm(np.concatenate([i["x_prompt"][0], i["x_sample"][0]])),
        c=fm(np.stack([i["c_ctx"], i["c"][0]])), wst=wst, wg=wg, bg=bg, col=col,
        wpool=i["w_pool_grp"][0].transpose(1, 0, 2), wr=wr.reshape(KT, P, -1).transpose(1, 0, 2),
        br=np.broadcast_to(br, (P, EG + NE)), st=st.transpose(2, 0, 1, 3),
        m0=i["state_m"][0, 0].reshape(R16, 1), cst=cst, rcnt=rcnt,
        wexp=np.concatenate([ex, ex[:1]]))


_OUTS = (("y", (P, KT, T)), ("so", (P, 2, H, V1)), ("mo", (R16, 1)))


def kernel(**inputs):
    import concourse.bacc as bacc
    from concourse.bass_utils import run_bass_kernel_spmd

    nc = bacc.Bacc("TRN2", target_bir_lowering=False, num_devices=1)
    arrays, args = {}, []
    for name, a in _layout(inputs).items():
        arrays["in_" + name] = a = np.ascontiguousarray(a)
        args.append(nc.dram_tensor("in_" + name, a.shape, mybir.dt.from_np(a.dtype),
                                   kind="ExternalInput").ap())
    for name, shape in _OUTS:
        args.append(nc.dram_tensor("out_" + name, shape, F32, kind="ExternalOutput").ap())
    layer_kernel(nc, *args)
    got = run_bass_kernel_spmd(nc, [arrays], core_ids=[0]).results[0]
    y = got["out_y"].transpose(2, 1, 0).reshape(T, D)
    so = got["out_so"].transpose(1, 2, 0, 3)
    return (np.ascontiguousarray(y[:TC])[None], np.ascontiguousarray(y[TC:])[None],
            np.ascontiguousarray(so[..., :DH])[None, None],
            np.ascontiguousarray(so[..., DH])[None, None],
            np.ascontiguousarray(got["out_mo"].reshape(1, 1, 2, H)))
```

```python
import concourse.bass as bass
from concourse import mybir
from contextlib import ExitStack
import numpy as np

F32 = mybir.dt.float32
F32R = mybir.dt.float32r
I32 = mybir.dt.int32
ALU = mybir.AluOpType
ACT = mybir.ActivationFunctionType
AX = mybir.AxisListType.X

P = 128
D = 1024
KT = D // P
TC, TL = 128, 512
T = TC + TL
NT = T // P
NL = TL // P
HALF = T // 2
H = 8
DH = 128
V1 = DH + 1
R16 = 2 * H
GP = 48
WIN = (2, 4, 8, 16)
NG = len(WIN)
GW, GR = 64, TL // 64
PAD = 8
CH = 2048
NRAW = 4
EG, EE = 4, 4
NE = EG * EE
DE = 512
FT = DE // P
N_YD = 5
SLOTS = 128
ROUNDS = -(-T // SLOTS)
NPAIR = NE // 2
ECH = 12
ERAW, ESPL = 4, 3
EPS = 1e-6
NEG = -1e30
SCALE = DH ** -0.5

N_MOD1 = 8
N_QK, N_V, N_U = 8, 4, 2
N_MOD2 = 16
N_O, N_G, N_B, N_A, N_OUT = 4, 8, 2, 4, 4
N_DENSE = N_MOD1 + N_QK + N_V + N_U + N_MOD2 + N_O + N_G + N_B + N_A + N_OUT
AT_QK = N_MOD1
AT_V = AT_QK + N_QK
AT_U = AT_V + N_V
AT_MOD2 = AT_U + N_U
AT_O = AT_MOD2 + N_MOD2
AT_G = AT_O + N_O
AT_B = AT_G + N_G
AT_A = AT_B + N_B
AT_OUT = AT_A + N_A

C_ID, C_ONE, C_FWD, C_BWD, C_STRICT, C_IOTA, C_NEGF, C_NEGB = (P * i for i in range(8))
C_MF = 8 * P
C_MB = C_MF + 1
C_WT = C_MF + 2
C_THR = C_WT + 4 * NT
C_EPS = C_THR + ROUNDS
C_END = C_EPS + 1

B_IN, B_MOD, G_1, G_2, G_F, G_N, P_S, W_END = 0, 52, 100, 108, 116, 124, 132, 136


class Steps:

    def __init__(self, eng, sem):
        self.eng, self.sem, self.base, self.n = eng, sem, 0, 0

    def on(self, ins):
        ins.then_inc(self.sem, 1)
        self.n += 1

    def wait(self):
        self.eng.wait_ge(self.sem, self.base + self.n)

    def do(self, ins):
        self.on(ins)
        self.wait()

    def enter(self, base):
        self.base, self.n = base, 0


def layer_kernel(nc, x_d, c_d, wst_d, wg_d, bg_d, col_d, wpool_d, wr_d, br_d, st_d, m0_d, cst_d,
                 rcnt_d, wexp_d, y_d, so_d, mo_d):
    ctx = ExitStack()
    with ctx:
        base = -(-nc.sbuf_base // 32) * 32
        ctx.enter_context(nc.sbuf_tensor("arena", [P, 207 * 256], F32))

        def at(name, kib, shape, dt=F32):
            return nc.alloc_sbuf_tensor_at(name, shape, dt, offset=base + int(kib * 1024))

        def sem(name):
            return ctx.enter_context(nc.semaphore(name))

        cst = at("cst", 0, [P, C_END])
        ident, ones = cst[:, C_ID:C_ID + P], cst[:, C_ONE:C_ONE + P]
        iota = cst[:, C_IOTA:C_IOTA + P]
        eps = cst[:, C_EPS:C_EPS + 1]
        col = at("col", 4.25, [P, W_END])
        mod = at("mod", 4.875, [P, 48, 2])
        gain = at("gain", 5.25, [P, KT, 2])
        cin = at("cin", 5.3125, [P, KT, 2])
        csil = at("csil", 5.375, [P, KT, 6])
        half_gate = at("half_gate", 5.625, [P, KT, 2])
        half_gn = at("half_gn", 5.6875, [P, KT])
        a_tok = at("a_tok", 5.75, [P, NT, R16])
        wi_tok = at("wi_tok", 6.0625, [P, NT, R16])
        em_tok = at("em_tok", 6.375, [P, NT, R16])
        ws_tok = at("ws_tok", 6.6875, [P, R16])
        hss = at("hss", 6.75, [P, NT, H])
        rinv = at("rinv", 6.9375, [P, NT, 2])
        bg = at("bg", 7.0, [GP, 1])
        m0 = at("m0", 7.0625, [R16, 1])
        mlast = at("mlast", 7.125, [R16, 4])
        rounds_i = at("rounds_i", 7.1875, [1, 1], I32)
        wslot = at("wslot", 7.21875, [P, 2])
        wr = at("wr", 7.25, [P, KT, EG + NE])
        br = at("br", 7.875, [P, EG + NE])

        raw = [at(f"raw{s}", 8 + 8 * s, [P, CH]) for s in range(NRAW)]
        whi = [at(f"whi{s}", 40 + 16 * s, [P, CH], F32R) for s in range(2)]
        wlo = [at(f"wlo{s}", 48 + 16 * s, [P, CH], F32R) for s in range(2)]
        hhi = at("hhi", 72, [P, KT, T], F32R)
        hlo = at("hlo", 92, [P, KT, T], F32R)
        hn = at("hn", 112, [P, KT, T])
        xT = at("xT", 132, [P, KT, T])
        rstd = at("rstd", 172.5, [P, T])
        QK = at("QK", 112, [P, 2 * H, T])
        Vt = at("Vt", 152, [P, NT, H, V1])
        U = at("U", 172.75, [P, NG, T])
        TMP = 182.75
        mrow1 = at("mrow1", 92, [4, 8 * P])
        wgr = at("wgr", TMP, [P, KT, GP])
        wgh = at("wgh", TMP + 1.5, [P, KT, GP], F32R)
        wgl = at("wgl", TMP + 3, [P, KT, GP], F32R)
        vst = [at(f"vst{s}", TMP + 2.5 * s, [P, T]) for s in range(2)]
        gI, gF, gA, gB, gC, gOne = (at(n, TMP + 5 + 2.5 * i, [R16, T])
                                    for i, n in enumerate(("gI", "gF", "gA", "gB", "gC", "gOne")))
        negM = at("negM", TMP + 22.5, [R16, T])
        DG = [[at(f"DG{p}{d}", (40, 66.25)[p] + 2.5 * d, [P, NT, P]) for d in range(2)]
              for p in range(2)]
        OFF = [[at(f"OFF{p}{d}", (45, TMP + 5)[p] + 3 * d, [P, 6 * P]) for d in range(2)]
               for p in range(2)]
        S = at("S", 51, [P, 20 * P])
        num = at("num", 61, [P, NT, 2, V1])
        qst = at("qst", TMP, [P, TL])
        kst = at("kst", TMP + 2.5, [P, T])
        stC = at("stC", TMP + 11.5, [P, 2, H, V1])
        kw = [[at(f"kw{p}{d}", o, [P, P]) for d, o in enumerate(((172.25, TMP + 2),
                                                                 (202.3125, 202.8125))[p])]
              for p in range(2)]
        pick = [at("pick0", 71.25, [R16, P]), at("pick1", 193.75, [R16, P])]
        mrow = at("mrow", 203.3125, [4, 2 * P])
        O = at("O", 132, [P, KT, T])
        Y = at("Y", 112, [P, KT, T])
        TH = at("TH", 132, [P, 2 * KT, T])
        XP = [at(f"XP{i}", TMP + 2.5 * i, [P, GR, GW + 2 * PAD]) for i in range(2)]
        RP = [at(f"RP{i}", TMP + 5 + 3.75 * i, [P, 2 * GR - 1, GW]) for i in range(2)]
        rcnt = at("rcnt", TMP + 12.5, [P, NG, T])
        CP = [at(f"CP{i}", TMP + 22.5 + 0.625 * i, [P, TC + 2 * PAD]) for i in range(2)]
        ybh = at("ybh", TMP, [P, NG, T], F32R)
        ybl = at("ybl", TMP + 10, [P, NG, T], F32R)
        wpool = at("wpool", TMP + 22.5, [P, NG, P])
        mgh = at("mgh", 112, [P, KT, T], F32R)
        mgl = at("mgl", TMP, [P, KT, T], F32R)
        xres = at("xres", 132, [P, KT, T])
        n2 = at("n2", 152, [P, KT, T])
        h2 = at("h2", 112, [P, KT, T])
        rs2 = at("rs2", 192.625, [P, T])
        eraw = [at(f"eraw{s}", o, [P, CH]) for s, o in enumerate((72, 80, 88, 199.25))]
        ehi = [at(f"ehi{s}", 8 + 16 * s, [P, CH], F32R) for s in range(ESPL)]
        elo = [at(f"elo{s}", 16 + 16 * s, [P, CH], F32R) for s in range(ESPL)]
        sel = at("sel", 56, [P, NT, 2 * SLOTS], F32R)
        selT = at("selT", 61, [P, 2, T], F32R)
        th = at("th", 66, [P, DE])
        act_ = at("act", 68, [P, DE])
        aTh = at("aTh", 70, [P, FT, SLOTS], F32R)
        aTl = at("aTl", 128, [P, FT, SLOTS], F32R)
        xgh = at("xgh", 112, [P, KT, 2 * SLOTS], F32R)
        xgl = at("xgl", 120, [P, KT, 2 * SLOTS], F32R)
        yh = at("yh", 96, [P, 2, D], F32R)
        yl = at("yl", 104, [P, 2, D], F32R)
        tkh = at("tkh", 152, [P, NT, D], F32R)
        tkl = at("tkl", 172, [P, NT, D], F32R)
        wtr = at("wtr", 192, [P, NT, NE, 2], F32R)
        wtok = at("wtok", 195.125, [P, NT, NE])
        rank = at("rank", 195.5, [P, NT, NE + 2])
        RT = 196
        lg = at("lg", RT, [P, NT, EG + NE])
        r5 = at("r5", RT + 0.5, [P, 12, NT])
        goh = at("goh", RT + 1, [P, NT, EG])
        les = at("les", RT + 1.125, [P, NT, EE])
        o1 = at("o1", RT + 1.25, [P, NT, EE])
        o2 = at("o2", RT + 1.375, [P, NT, EE])
        t4 = at("t4", RT + 1.5, [P, NT, EE])
        t5 = at("t5", RT + 1.625, [P, NT, EE])
        t16 = at("t16", RT + 1.75, [P, NT, EG, EE])
        am = at("am", RT + 2.25, [P, NT + 1, NE])
        thr = at("thr", RT + 2.625, [P, 8])
        cum = at("cum", RT + 2.65625, [P, NT + 1, NE])
        lgT = at("lgT", 52, [EG + NE, T])
        yout = at("yout", 152, [P, KT, T])

        ps = ctx.enter_context(nc.psum_tensor("ps", [P, 8, 512], F32))

        def pair(e):
            return ps[:, 2 * (e % 4):2 * (e % 4) + 2, 0:HALF]

        def halves(ap):
            return ap.rearrange("p (a n) -> p a n", a=2)

        def f32(t):
            return t.bitcast(F32)

        d_const, d_st, d_pool, d_wp, d_xr = (sem(n) for n in (
            "d_const", "d_st", "d_pool", "d_wp", "d_xr"))
        d_x = [sem(f"d_x{k}") for k in range(KT // 2)]
        raw_full = [sem(f"raw_full{s}") for s in range(NRAW)]
        raw_free = [sem(f"raw_free{s}") for s in range(NRAW)]
        hi_ready = sem("hi_ready")
        blk_ready, blk_free = sem("blk_ready"), sem("blk_free")
        s_csil, s_sq, s_ssq, s_rstd, s_hn, s_hhi, s_hlo = (sem(n) for n in (
            "s_csil", "s_sq", "s_ssq", "s_rstd", "s_hn", "s_hhi", "s_hlo"))
        s_wgh, s_wgl, s_gps, s_gate, s_lsg, s_grow, s_gtok = (sem(n) for n in (
            "s_wgh", "s_wgl", "s_gps", "s_gate", "s_lsg", "s_grow", "s_gtok"))
        s_init, s_mrow, s_modT = sem("s_init"), sem("s_mrow"), sem("s_modT")
        s_pick, s_qst, s_kst, s_m, s_kw, s_sc, s_sev, s_tdg, s_exp, s_p, s_pv, s_nm = (
            sem(n) for n in ("s_pick", "s_qst", "s_kst", "s_m", "s_kw", "s_sc", "s_sev", "s_tdg",
                             "s_exp", "s_p", "s_pv", "s_nm"))
        m_free, qc5_free, qc1_free, pv6_free, pv7_free = (sem(n) for n in (
            "m_free", "qc5_free", "qc1_free", "pv6_free", "pv7_free"))
        s_o, s_hd, s_yh, s_yl = (sem(n) for n in ("s_o", "s_hd", "s_yh", "s_yl"))
        s_pool, s_ybh, s_mg, s_mgh, s_mgl, s_xr = (sem(n) for n in (
            "s_pool", "s_ybh", "s_mg", "s_mgh", "s_mgl", "s_xr"))
        s_sq2, s_ssq2, s_rs2, s_h2, s_lg, s_ex, s_am, s_rk, s_tkp, s_tk, s_tkl, s_cnt = (sem(n) for n in (
            "s_sq2", "s_ssq2", "s_rs2", "s_h2", "s_lg", "s_ex", "s_am", "s_rk", "s_tkp", "s_tk",
            "s_tkl", "s_cnt"))
        e_full = [sem(f"e_full{s}") for s in range(ERAW)]
        e_free = [sem(f"e_free{s}") for s in range(ERAW)]
        e_hi, e_mm = sem("e_hi"), sem("e_mm")
        e_th, e_act, e_ws, e_sel, e_selp, e_selT, e_cmb, e_add, e_gat, e_aTp = (sem(n) for n in (
            "e_th", "e_act", "e_ws", "e_sel", "e_selp", "e_selT", "e_cmb", "e_add", "e_gat", "e_aTp"))
        e_xgh, e_xgl, e_aTh, e_aTl, e_yh, e_yl = (sem(n) for n in (
            "e_xgh", "e_xgl", "e_aTh", "e_aTl", "e_yh", "e_yl"))
        s_round = sem("s_round")
        s_wtr, s_hn2, s_sum, s_lgp, s_lgT, s_sumf, s_sum1 = (sem(n) for n in (
            "s_wtr", "s_hn2", "s_sum", "s_lgp", "s_lgT", "s_sumf", "s_sum1"))
        s_sqf, s_ssf, s_rsf, s_out = sem("s_sqf"), sem("s_ssf"), sem("s_rsf"), sem("s_out")
        s_yo, s_yp, s_yg, s_sto = (sem(n) for n in ("s_yo", "s_yp", "s_yg", "s_sto"))
        a_steps, v_steps, g_steps = sem("act_steps"), sem("dve_steps"), sem("pool_steps")
        v_head, v_item, a_head = sem("dve_head_steps"), sem("dve_item_steps"), sem("act_loop_steps")

        block = ctx.enter_context(nc.Block())
        E_V, E_G8, E_U, E_O, E_Y, E_TH, E_PL, E_B, E_A, E_OUT, E_END = (
            16, 32, 33, 37, 45, 53, 69, 73, 81, 89, 97)
        CV, CU, CO, CTH, CB, CA, COUT = 8, 12, 14, 18, 26, 28, 32
        OFF_F, OFF_B = (0, 3 * P, 5 * P), (0, P, 3 * P)
        N_SMALL = 8
        HEAD_STEPS, PAIR_STEPS = 4, 18

        @block.sync
        def _(sp):
            smalls = [(cst[:, :], cst_d), (cin[:, :, :], c_d), (col[:, :], col_d),
                      (wgr[:, :, :], wg_d), (bg[:, :], bg_d), (m0[:, :], m0_d),
                      (wr[:, :, :], wr_d), (br[:, :], br_d)]
            assert len(smalls) == N_SMALL
            for dst, src in smalls:
                sp.dma_start(dst, src).then_inc(d_const, 16)
            for s in range(NRAW):
                sp.sem_inc(raw_free[s], 1)
            for s in range(ERAW):
                sp.sem_inc(e_free[s], 1)

            def load_raw(i, s):
                sp.wait_ge(raw_free[s], i + 1)
                sp.dma_start(raw[s][:, :], wst_d[i * NRAW + s, :, :]).then_inc(raw_full[s], 16)

            for c in range(N_MOD1):
                load_raw(c // NRAW, c % NRAW)
                if c < 4:
                    sp.dma_start(xT[:, 2 * c:2 * c + 2, :], x_d[:, 2 * c:2 * c + 2, :])\
                      .then_inc(d_x[c], 16)
            with sp.Fori(N_MOD1 // NRAW, N_DENSE // NRAW) as i:
                for s in range(NRAW):
                    load_raw(i, s)
            sp.wait_ge(blk_ready, E_OUT)
            for s in range(ERAW):
                if s == ERAW - 1:
                    sp.wait_ge(blk_ready, E_END)
                sp.dma_start(eraw[s][:, :], wexp_d[0, s, :, :]).then_inc(e_full[s], 16)
            sp.wait_ge(s_cnt, 1)
            rounds = sp.value_load(rounds_i[0:1, 0:1], min_val=1, max_val=ROUNDS)
            with sp.Fori(0, rounds) as r:
                with sp.Fori(0, NPAIR) as q:
                    n = r * NPAIR + q
                    for c in range(ERAW, ECH + ERAW):
                        sp.wait_ge(e_free[c % ERAW], n * (ECH // ERAW) + c // ERAW + 1)
                        sp.dma_start(eraw[c % ERAW][:, :], wexp_d[q + c // ECH, c % ECH, :, :])\
                          .then_inc(e_full[c % ERAW], 16)
            first, last = list(range(N_YD)), list(range(N_YD, KT))
            order = sorted(first + last, key=lambda k: k * 3 if k < N_YD else (k - N_YD) * 5 + 4)
            for k in order:
                if k < N_YD:
                    sp.wait_ge(s_yo, k + 1)
                else:
                    sp.wait_ge(s_yp, k - N_YD + 1)
                sp.dma_start(y_d[:, k, :], yout[:, k, :]).then_inc(s_out, 16)
            sp.wait_ge(s_out, 16 * KT)
            sp.wait_ge(s_sto, 32)

        @block.gpsimd
        def _(gp):
            st = Steps(gp, g_steps)
            gp.memset(gOne[:, :], 1.0).then_inc(s_init, 1)
            gp.memset(Vt[:, :, :, DH:V1], 1.0).then_inc(s_init, 1)

            def sum_squares(sq, done, n=KT):
                gp.wait_ge(done[0], 1)
                for k in range(1, n):
                    gp.wait_ge(done[0], k + 1)
                    if k > 1:
                        gp.wait_ge(done[1], k - 1)
                    gp.tensor_tensor(sq[:, 0, :], sq[:, 0, :], sq[:, k, :], ALU.add)\
                      .then_inc(done[1], 1)

            sum_squares(hn, (s_sq, s_sum1))
            gp.wait_ge(s_gtok, 1)
            gp.dma_start(stC[:, :, :, :], st_d).then_inc(d_st, 16)
            gp.wait_ge(blk_ready, E_O)

            def pick_rows(h):
                for d in range(2):
                    row = cst[0:R16, bass.ds(h + (C_ID + d * H), 1)]
                    gp.tensor_tensor(pick[d][:, :], ones[0:R16, :], row.broadcast_to([R16, P]),
                                     ALU.mult).then_inc(s_pick, 1)

            pick_rows(0)
            with gp.Fori(1, H) as h:
                gp.wait_ge(s_m, h)
                pick_rows(h)
            gp.wait_ge(pv7_free, 1 + 3 * H)
            gp.dma_start(so_d, stC[:, :, :, :]).then_inc(s_sto, 16)
            gp.dma_start(mo_d, mlast[:, 2:3]).then_inc(s_sto, 16)
            gp.wait_ge(s_sto, 32)
            gp.dma_start(rcnt[:, :, :], rcnt_d).then_inc(d_pool, 16)
            gp.wait_ge(s_nm, 1 + H)
            gp.wait_ge(d_pool, 16)
            for g, w in enumerate(WIN):
                st.on(gp.memset(XP[0][:, :, :], 0.0))
                st.on(gp.memset(RP[0][:, :, :], 0.0))
                st.do(gp.memset(CP[0][:, :], 0.0))
                st.do(gp.tensor_copy(XP[0][:, :, PAD:PAD + GW],
                                     U[:, g, TC:T].rearrange("p (r c) -> p r c", c=GW)))
                n, s, src = GW + 2 * PAD, 1, 0
                while s < w:
                    n -= s
                    st.do(gp.tensor_tensor(XP[1 - src][:, :, 0:n], XP[src][:, :, 0:n],
                                           XP[src][:, :, s:s + n], ALU.add))
                    s, src = 2 * s, 1 - src
                xs = XP[src][:, :, PAD - w // 2:PAD - w // 2 + GW]
                if w // 2 >= GR:
                    st.do(gp.tensor_tensor(RP[0][:, 0:4, :], xs[:, 0:4, :], xs[:, 4:8, :], ALU.add))
                    st.do(gp.tensor_tensor(RP[1][:, 0:2, :], RP[0][:, 0:2, :], RP[0][:, 2:4, :],
                                           ALU.add))
                    st.do(gp.tensor_tensor(RP[0][:, 0:1, :], RP[1][:, 0:1, :], RP[1][:, 1:2, :],
                                           ALU.add))
                    res = RP[0][:, 0:1, :].broadcast_to([P, GR, GW])
                else:
                    st.do(gp.tensor_copy(RP[0][:, w // 2:w // 2 + GR, :], xs))
                    n, s, src = GR + w - 1, 1, 0
                    while s < w:
                        n -= s
                        st.do(gp.tensor_tensor(RP[1 - src][:, 0:n, :], RP[src][:, 0:n, :],
                                               RP[src][:, s:s + n, :], ALU.add))
                        s, src = 2 * s, 1 - src
                    res = RP[src][:, 0:GR, :]
                mean_l = XP[0][:, :, 0:GW]
                st.do(gp.tensor_tensor(mean_l, res, rcnt[:, g, TC:T].rearrange(
                    "p (r c) -> p r c", c=GW), ALU.mult))
                ul = U[:, g, TC:T].rearrange("p (r c) -> p r c", c=GW)
                st.do(gp.tensor_tensor(ul, mean_l, ul, ALU.subtract))
                st.do(gp.tensor_copy(CP[0][:, PAD:PAD + TC], U[:, g, 0:TC]))
                n, s, src = TC + 2 * PAD, 1, 0
                while s < w:
                    n -= s
                    st.do(gp.tensor_tensor(CP[1 - src][:, 0:n], CP[src][:, 0:n],
                                           CP[src][:, s:s + n], ALU.add))
                    s, src = 2 * s, 1 - src
                cs = CP[src][:, PAD - w // 2:PAD - w // 2 + TC]
                st.do(gp.tensor_tensor(CP[1 - src][:, 0:TC], cs, rcnt[:, g, 0:TC], ALU.mult))
                st.do(gp.tensor_tensor(U[:, g, 0:TC], CP[1 - src][:, 0:TC], U[:, g, 0:TC],
                                       ALU.subtract))
            gp.dma_start(wpool[:, :, :], wpool_d).then_inc(d_wp, 16)
            gp.sem_inc(s_pool, 1)
            gp.wait_ge(s_mgl, KT)
            gp.dma_start(xres[:, :, :], x_d).then_inc(d_xr, 16)
            sum_squares(n2, (s_sq2, s_sum))
            gp.wait_ge(s_rs2, 1)
            for x in range(2):
                gp.memset(f32(yh[:, x, :]), 0.0).then_inc(e_yh, 1)
                gp.memset(f32(yl[:, x, :]), 0.0).then_inc(e_yl, 1)
            gp.memset(f32(selT[:, :, :]), 0.0).then_inc(e_selT, 1)
            sum_squares(h2, (s_sqf, s_sumf), KT // 2)
            gp.wait_ge(s_yg, KT)
            gp.wait_ge(s_rsf, 1)
            for k in range(N_YD, KT):
                gp.tensor_tensor(yout[:, k, :], yout[:, k, :], rs2[:, :], ALU.mult)\
                  .then_inc(s_yp, 1)

        @block.scalar
        def _(act):
            act.sem_inc(blk_free, 4)
            st = Steps(act, a_steps)

            def split_hi(slot, use, p):
                act.wait_ge(raw_full[slot], (use + 1) * 16)
                act.activation(whi[p][:, :], raw[slot][:, :], ACT.Copy).then_inc(hi_ready, 1)

            def inv_rms(out, in_, n, sem_):
                st.do(act.activation(out, in_, ACT.Ln, bias=eps, scale=1.0 / n))
                act.activation(out, out, ACT.Exp, scale=-0.5).then_inc(sem_, 1)

            act.wait_ge(d_const, 16 * N_SMALL)
            act.activation(csil[:, :, 2:4], cin[:, :, :], ACT.Tanh, scale=0.5).then_inc(s_csil, 1)
            act.activation(wgh[:, :, :], wgr[:, :, :], ACT.Copy).then_inc(s_wgh, 1)
            for k in range(KT):
                if k % 2 == 0:
                    act.wait_ge(d_x[k // 2], 16)
                act.activation(hn[:, k, :], xT[:, k, :], ACT.Square).then_inc(s_sq, 1)

            def mod_row1(b):
                act.wait_ge(raw_free[NRAW - 1], b + 2)
                act.activation(mrow1[:, b * 512:(b + 1) * 512], ps[0:4, 2 + b, :], ACT.Copy)\
                   .then_inc(s_mrow, 1)

            mod_row1(0)
            act.wait_ge(s_ssq, 1)
            inv_rms(halves(rstd[:, :]), ps[:, 0:2, 0:HALF], D, s_rstd)
            split_hi(AT_QK % NRAW, AT_QK // NRAW, 0)
            mod_row1(1)
            for k in range(KT):
                act.wait_ge(s_hn, k + 1)
                act.activation(hhi[:, k, :], hn[:, k, :], ACT.Copy).then_inc(s_hhi, 1)
            act.wait_ge(s_gps, 1)
            act.activation(halves(gI[:, :]), ps[0:R16, 6:8, 0:HALF], ACT.Identity,
                           bias=bg[0:R16, :]).then_inc(s_gate, 1)
            act.activation(halves(gF[:, :]), ps[32:32 + R16, 6:8, 0:HALF], ACT.Identity,
                           bias=bg[32:32 + R16, :]).then_inc(s_gate, 1)
            act.wait_ge(s_lsg, 1)
            st.do(act.activation(gC[:, :], gC[:, :], ACT.Exp, scale=-1.0))
            act.activation(gC[:, :], gC[:, :], ACT.Ln, bias=cst[0:R16, C_ONE:C_ONE + 1])\
               .then_inc(s_gate, 1)

            with act.Fori(0, N_QK // NRAW) as i:
                for j in range(NRAW):
                    split_hi((j + 1) % NRAW, i + AT_QK // NRAW + (j + 1) // NRAW, (j + 1) % 2)
                    for b in range(2):
                        e = 2 * j + b
                        act.wait_ge(blk_ready, i * 8 + e + 1)
                        act.activation(halves(QK[:, i * 8 + e, :]), pair(e), ACT.Identity,
                                       bias=col[:, bass.ds(i * 8 + e + B_IN, 1)])\
                           .then_inc(blk_free, 1)
            def v_rows(v, e):
                act.wait_ge(blk_ready, e + 1)
                st.on(act.activation(Vt[:, 0:3, v, 0:DH], ps[:, 2 * (e % 4), 0:3 * P].rearrange(
                    "p (t n) -> p t n", n=P), ACT.Copy))
                act.activation(Vt[:, 3:5, v, 0:DH], ps[:, 2 * (e % 4) + 1, 0:2 * P].rearrange(
                    "p (t n) -> p t n", n=P), ACT.Copy).then_inc(blk_free, 1)

            e = E_V
            for v in range(H):
                if v % 2 == 0:
                    c = AT_V + v // 2 + 1
                    split_hi(c % NRAW, c // NRAW, (v // 2 + 1) % 2)
                act.wait_ge(blk_ready, e + 1)
                act.activation(halves(vst[v % 2][:, :]), pair(e), ACT.Identity,
                               bias=col[:, 16 + v:17 + v]).then_inc(blk_free, 1)
                e += 1
                if v:
                    v_rows(v - 1, e)
                    e += 1
            v_rows(H - 1, e)
            assert e + 1 == E_G8
            act.wait_ge(blk_ready, E_G8 + 1)
            gps = ps[:, 2 * (E_G8 % 4), :]
            st.on(act.activation(a_tok[:, :, :].rearrange("p t r -> p (t r)"), gps[:, 0:80], ACT.Copy))
            st.on(act.activation(wi_tok[:, 1:NT, :].rearrange("p t r -> p (t r)"), gps[:, 80:144],
                                 ACT.Exp))
            st.on(act.activation(em_tok[:, :, :].rearrange("p t r -> p (t r)"), gps[:, 144:224],
                                 ACT.Exp))
            act.activation(ws_tok[:, :], gps[:, 224:240], ACT.Exp).then_inc(blk_free, 1)
            act.wait_ge(blk_free, 4 + E_U)
            act.activation(ws_tok[:, :], ws_tok[:, :], ACT.Copy, scale=SCALE).then_inc(s_gtok, 1)
            for j in range(N_U):
                if j + 1 < N_U:
                    c = AT_U + j + 1
                    split_hi(c % NRAW, c // NRAW, (j + 1) % 2)
                for b in range(2):
                    e = E_U + 2 * j + b
                    act.wait_ge(blk_ready, e + 1)
                    act.activation(halves(U[:, 2 * j + b, :]), pair(e), ACT.Identity,
                                   bias=col[:, 24 + 2 * j + b:25 + 2 * j + b]).then_inc(blk_free, 1)

            act.wait_ge(s_gtok, 1)

            def scores_weights(i, hp, last=False):
                h, dg, off = i * 2 + hp, DG[hp], OFF[hp]

                def off_exp(d, j, o, t0, n):
                    act.activation(off[d][:, o:o + n], ps[:, 2 + d, t0:t0 + n], ACT.Exp,
                                   bias=a_tok[:, j + 1, bass.ds(h + d * H, 1)])

                def s_out(j):
                    act.wait_ge(s_sc, h * 5 + j + 2)
                    b = (j + 1) % 2
                    o, n = (2048, P) if j < 0 else (j * TL, TL)
                    act.activation(S[:, o:o + n], ps[:, b, 0:n], ACT.Copy, scale=SCALE)\
                       .then_inc(s_sev, 1)

                if not isinstance(h, int) or h:
                    act.wait_ge(s_p, h)
                for j in range(-1, NL):
                    s_out(j)
                act.wait_ge(s_tdg, h * 2 + 1)
                for j in range(3):
                    off_exp(0, j, OFF_F[j], (j + 1) * P, (3 - j) * P)
                act.wait_ge(s_tdg, h * 2 + 2)
                for j in range(1, 4):
                    off_exp(1, j, OFF_B[j - 1], 0, j * P)
                for d in range(2):
                    act.activation(kw[hp][d][:, :], ps[:, 4, 2 * P:3 * P], ACT.Copy,
                                   scale=ws_tok[:, bass.ds(h + d * H, 1)]).then_inc(s_kw, 1)
                for d in range(2):
                    act.activation(dg[d][:, :, :], dg[d][:, :, :], ACT.Exp).then_inc(s_exp, 1)
                if not last:
                    act.activation(kst[:, :], QK[:, h + (H + 1), :], ACT.Copy).then_inc(s_kst, 1)

            def final_state(i, hp):
                h = i * 2 + hp
                act.wait_ge(s_pv, h * 6 + 6)
                act.activation(stC[:, :, h, :], ps[:, 7, 0:2 * V1].rearrange(
                    "p (d n) -> p d n", n=V1), ACT.Copy).then_inc(pv7_free, 1)

            def mod_row(i, hp):
                c1 = AT_MOD2 + 2 * hp + 1
                act.wait_ge(raw_free[c1 % NRAW], i + c1 // NRAW + 2)
                act.activation(mrow[:, :], ps[0:4, 0, 0:2 * P], ACT.Copy).then_inc(s_mrow, 1)

            act.activation(kst[:, :], QK[:, H, :], ACT.Copy).then_inc(s_kst, 1)
            scores_weights(0, 0)
            mod_row(0, 0)
            with act.Fori(0, H // 2 - 1) as i:
                scores_weights(i, 1)
                final_state(i, 0)
                mod_row(i, 1)
                scores_weights(i + 1, 0)
                final_state(i, 1)
                mod_row(i + 1, 0)
            i = H // 2 - 1
            scores_weights(i, 1, last=True)
            final_state(i, 0)
            mod_row(i, 1)
            act.wait_ge(s_p, H)
            split_hi(AT_O % NRAW, AT_O // NRAW, 0)
            final_state(i, 1)

            act.wait_ge(s_nm, 1 + H)
            for j in range(N_O):
                c = AT_O + j + 1
                split_hi(c % NRAW, c // NRAW, (j + 1) % 2)
                for b in range(2):
                    e, f = E_O + 2 * j + b, 2 * j + b
                    act.wait_ge(blk_ready, e + 1)
                    act.activation(halves(O[:, f, :]), pair(e), ACT.Tanh, scale=0.5,
                                   bias=col[:, 28 + f:29 + f]).then_inc(blk_free, 1)
                if j == 1:
                    act.wait_ge(s_hd, 1)
                    inv_rms(hss[:, :, :], hss[:, :, :], DH, s_o)
            act.wait_ge(blk_free, 4 + E_TH)
            with act.Fori(0, N_G // NRAW) as i:
                for j in range(NRAW):
                    c = AT_G + j + 1
                    split_hi(c % NRAW, i + c // NRAW, (j + 1) % 2)
                    for b in range(2):
                        f = 2 * j + b
                        act.wait_ge(blk_ready, i * 8 + E_TH + f + 1)
                        act.activation(halves(TH[:, i * 8 + f, :]), pair(E_TH + f), ACT.Tanh,
                                       scale=0.5, bias=col[:, bass.ds(i * 8 + 36 + f, 1)])\
                           .then_inc(blk_free, 1)
            for g in range(NG):
                act.wait_ge(blk_ready, E_PL + g + 1)
                act.activation(halves(ybh[:, g, :]), pair(E_PL + g), ACT.Copy,
                               scale=col[:, P_S + g:P_S + g + 1]).then_inc(s_ybh, 1)
            split_hi((AT_B + 1) % NRAW, (AT_B + 1) // NRAW, 1)
            for k in range(KT):
                act.activation(hhi[:, k, :], Y[:, k, :], ACT.Copy, scale=half_gn[:, k:k + 1])\
                   .then_inc(s_yh, 1)
            done = [E_B + 4, E_B + 8] + [E_A + 2 * j + 2 for j in range(6)]
            for j in range(N_A + N_OUT):
                c = AT_A + j
                if j == 2:
                    act.wait_ge(s_yl, KT)
                ks = range(max(2 * j - 4, 0), 2 * j - 2) if j < 2 + N_A else ()
                if j < 1 + N_A:
                    act.wait_ge(blk_ready, done[j])
                    split_hi(c % NRAW, c // NRAW, j % 2)
                for k in ks:
                    act.wait_ge(s_mg, k + 1)
                    act.activation(mgh[:, k, :], TH[:, k, :], ACT.Copy).then_inc(s_mgh, 1)
                if j >= 1 + N_A:
                    act.wait_ge(blk_ready, done[j])
                    split_hi(c % NRAW, c // NRAW, j % 2)
            for k in range(KT):
                act.wait_ge(s_xr, k + 1)
                act.activation(n2[:, k, :], xres[:, k, :], ACT.Square).then_inc(s_sq2, 1)

            def expert_hi(c, n=0, used=True):
                act.wait_ge(e_full[c % ERAW], (n * (ECH // ERAW) + c // ERAW + 1) * 16)
                if used:
                    act.wait_ge(e_mm, n * ECH + c - ESPL + 1)
                act.activation(ehi[c % ESPL][:, :], eraw[c % ERAW][:, :], ACT.Copy)\
                   .then_inc(e_hi, 1)

            act.wait_ge(s_ssq2, 1)
            inv_rms(halves(rs2[:, :]), ps[:, 0:2, 0:HALF], D, s_rs2)
            for k in range(KT):
                act.wait_ge(s_hn2, k + 1)
                for c, a, b in ((0, 0, TC), (1, TC, T)):
                    ins = act.activation(h2[:, k, a:b], h2[:, k, a:b], ACT.Identity,
                                         bias=mod[:, 24 + k, c:c + 1], scale=gain[:, k, c:c + 1])
                ins.then_inc(s_h2, 1)
            act.wait_ge(s_lgp, 1)
            act.activation(halves(lgT[:, :]), ps[0:EG + NE, 2:4, 0:HALF], ACT.Copy)\
               .then_inc(s_lgT, 1)

            def token_hi(t):
                act.wait_ge(s_tkp, t + 1)
                act.activation(tkh[:, t, :].rearrange("p (a n) -> p a n", a=2),
                               ps[:, 4 + 2 * (t % 2):6 + 2 * (t % 2), :], ACT.Copy)\
                   .then_inc(s_tk, 1)

            for t in range(2):
                token_hi(t)
            act.wait_ge(s_ex, 1)
            act.activation(t4[:, :, :], t4[:, :, :], ACT.Exp).then_inc(s_lg, 1)
            act.wait_ge(s_ex, 2)
            act.activation(r5[:, 4, :], r5[:, 4, :], ACT.Exp).then_inc(s_lg, 1)
            for t in range(2, NT):
                token_hi(t)
            for c in range(ESPL):
                expert_hi(c, used=False)

            def tokens_hi(a, count):
                act.wait_ge(e_gat, count)
                act.activation(xgh[:, 4 * a:4 * a + 4, :].rearrange("p (b k) n -> p b (k n)", b=2),
                               ps[:, 4 + 2 * a:6 + 2 * a, :], ACT.Copy).then_inc(e_xgh, 1)

            def tanh_gate(x, n):
                act.wait_ge(e_mm, n * ECH + 4 * x + 4)
                act.activation(th[:, :], ps[:, 0, :], ACT.Tanh, scale=0.5).then_inc(e_th, 1)

            def act_hi(x, n):
                act.wait_ge(e_aTp, n * 2 + x + 1)
                act.activation(aTh[:, :, :].rearrange("p f n -> p (f n)"), ps[:, 0, :],
                               ACT.Copy).then_inc(e_aTh, 1)

            def out_hi(x, n):
                act.wait_ge(e_mm, n * ECH + 10 + 2 * x)
                act.wait_ge(e_ws, n + 1)
                act.activation(yh[:, x, :].rearrange("p (a n) -> p a n", a=2), ps[:, 2:4, :],
                               ACT.Copy, scale=wslot[:, x:x + 1]).then_inc(e_yh, 1)

            for a in range(2):
                tokens_hi(a, a + 1)
            act.wait_ge(s_cnt, 1)
            rounds = act.value_load(rounds_i[0:1, 0:1], min_val=1, max_val=ROUNDS)
            with act.Fori(0, rounds) as r:
                with act.Fori(0, NPAIR) as q:
                    n = r * NPAIR + q
                    for c in (3, 4, 5):
                        expert_hi(c, n)
                    tanh_gate(0, n)
                    expert_hi(6, n)
                    act_hi(0, n)
                    for c in (7, 8, 9):
                        expert_hi(c, n)
                    tanh_gate(1, n)
                    expert_hi(10, n)
                    act.wait_ge(e_selp, n + 1)
                    st_i = Steps(act, a_head)
                    flat = selT[:, :, :].rearrange("p x n -> p (x n)")
                    st_i.on(act.activation(flat[:, 0:1024].rearrange("p (a n) -> p a n", a=2),
                                           ps[:, 4:6, :], ACT.Copy))
                    act.activation(flat[:, 1024:2 * T], ps[:, 6, 0:2 * P], ACT.Copy)\
                       .then_inc(e_selT, 1)
                    expert_hi(11, n)
                    out_hi(0, n)
                    expert_hi(12, n)
                    act_hi(1, n)
                    for a in range(2):
                        tokens_hi(a, n * 2 + 3 + a)
                    expert_hi(13, n)
                    expert_hi(14, n)
                    out_hi(1, n)
            for k in range(KT):
                act.wait_ge(e_add, rounds * (NPAIR * KT) + k + 1)
                act.activation(h2[:, k, :], xres[:, k, :], ACT.Square).then_inc(s_sqf, 1)
            act.wait_ge(s_ssf, 1)
            inv_rms(halves(rs2[:, :]), ps[:, 0:2, 0:HALF], D, s_rsf)

        @block.vector
        def _(dve):
            st = Steps(dve, v_steps)

            def split_lo(slot, p, ci):
                dve.wait_ge(hi_ready, ci + 1)
                dve.tensor_tensor(wlo[p][:, :], raw[slot][:, :], f32(whi[p][:, :]), ALU.subtract)\
                   .then_inc(raw_free[slot], 1)

            def by(ap, shape):
                return ap.broadcast_to(shape)

            dve.sem_inc(m_free, 1)
            dve.sem_inc(s_nm, 1)
            dve.sem_inc(qc5_free, 1)
            dve.sem_inc(qc1_free, 1)
            dve.sem_inc(pv6_free, 1)
            dve.sem_inc(pv7_free, 1)
            dve.memset(csil[:, :, 0:2], 0.0).then_inc(s_csil, 1)
            dve.memset(csil[:, :, 4:6], 0.0).then_inc(s_csil, 1)
            dve.wait_ge(d_const, 16 * N_SMALL)
            dve.wait_ge(s_csil, 3)
            sl = csil[:, :, 2:4]
            st.do(dve.scalar_tensor_tensor(sl, sl, 1.0, cin[:, :, :], ALU.add, ALU.mult))
            dve.tensor_scalar(sl, sl, 0.5, None, ALU.mult).then_inc(s_csil, 1)
            st.on(dve.tensor_scalar(col[:, 28:52], col[:, 28:52], 0.5, None, ALU.mult))
            st.on(dve.tensor_scalar(half_gn[:, :], col[:, G_N:G_N + KT], 0.5, None, ALU.mult))
            dve.wait_ge(s_wgh, 1)
            dve.tensor_tensor(wgl[:, :, :], wgr[:, :, :], f32(wgh[:, :, :]), ALU.subtract)\
               .then_inc(s_wgl, 1)
            dve.wait_ge(s_rstd, 1)
            for k in range(KT):
                st.on(dve.tensor_tensor(hn[:, k, :], xT[:, k, :], rstd[:, :], ALU.mult))
            split_lo(AT_QK % NRAW, 0, 0)
            dve.wait_ge(s_modT, 1)
            rows = ps[:, 4, 0:32].rearrange("p (j c) -> p j c", c=2)
            st.do(dve.tensor_tensor(mod[:, 0:16, :], rows,
                                    by(col[:, B_MOD:B_MOD + 16].unsqueeze(2), [P, 16, 2]), ALU.add))
            st.do(dve.scalar_tensor_tensor(gain[:, :, :], mod[:, 8:16, :], 1.0,
                                           by(col[:, G_1:G_1 + KT].unsqueeze(2), [P, KT, 2]),
                                           ALU.add, ALU.mult))

            def input_lo(k):
                dve.wait_ge(s_hhi, k + 1)
                dve.tensor_tensor(hlo[:, k, :], hn[:, k, :], f32(hhi[:, k, :]), ALU.subtract)\
                   .then_inc(s_hlo, 1)

            for k in range(KT):
                for c, a, b in ((0, 0, TC), (1, TC, T)):
                    ins = dve.tensor_scalar(hn[:, k, a:b], hn[:, k, a:b], gain[:, k, c:c + 1],
                                            mod[:, k, c:c + 1], ALU.mult, ALU.add)
                ins.then_inc(s_hn, 1)
                if k:
                    input_lo(k - 1)
            input_lo(KT - 1)
            dve.wait_ge(s_gate, 2)
            st.on(dve.tensor_scalar(gB[:, :], gF[:, :], 0.0, None, ALU.min))
            dve.scalar_tensor_tensor(gC[:, :], gF[:, :], -1.0, gF[:, :], ALU.mult, ALU.max)\
               .then_inc(s_lsg, 1)
            dve.wait_ge(s_gate, 3)
            st.wait()
            st.do(dve.tensor_tensor(gF[:, :], gB[:, :], gC[:, :], ALU.subtract))
            with dve.Fori(0, N_QK // NRAW) as i:
                for j in range(NRAW):
                    split_lo((j + 1) % NRAW, (j + 1) % 2, i * 4 + j + 1)
            split_lo((AT_V + 1) % NRAW, 1, CV + 1)

            mf, mb = cst[0:R16, C_MF:C_MF + 1], cst[0:R16, C_MB:C_MB + 1]
            segs = ((0, TC), (TC, T))

            def scans(dst_f, dst_b, src, initial, op):
                for (a, b), ini in zip(segs, initial):
                    st.on(dve.tensor_tensor_scan(dst_f[:, a:b], gOne[:, a:b], src[:, a:b], ini,
                                                 ALU.mult, op))
                    rev = slice(b - 1, a - 1 if a else None, -1)
                    st.on(dve.tensor_tensor_scan(dst_b[:, rev], gOne[:, rev], src[:, rev], ini,
                                                 ALU.mult, op))
                st.wait()

            def pick(dst, f, b):
                st.do(dve.tensor_scalar(f, f, mf, None, ALU.mult))
                st.do(dve.scalar_tensor_tensor(dst, b, mb, f, ALU.mult, ALU.add))

            dve.wait_ge(s_init, 1)
            scans(gA, gB, gF, (0.0, 0.0), ALU.add)
            pick(gF[:, :], gA[:, :], gB[:, :])
            split_lo((AT_V + 2) % NRAW, 0, CV + 2)
            st.do(dve.tensor_tensor(gA[:, :], gI[:, :], gF[:, :], ALU.subtract))
            scans(gB, gC, gA, (NEG, m0[:, :]), ALU.max)
            pick(gB[:, :], gB[:, :], gC[:, :])
            st.on(dve.tensor_scalar(negM[:, :], gB[:, :], -1.0, None, ALU.mult))
            st.on(dve.scalar_tensor_tensor(gC[:, :], gF[:, :], -1.0, gB[:, :], ALU.mult, ALU.subtract))
            for c, src in ((0, gB), (1, gF)):
                st.on(dve.tensor_scalar(mlast[:, 3:4], src[:, TC - 1:TC], mf, None, ALU.mult))
                st.wait()
                st.do(dve.scalar_tensor_tensor(mlast[:, c:c + 1], src[:, 0:1], mb, mlast[:, 3:4],
                                               ALU.mult, ALU.add))
            st.on(dve.tensor_tensor(mlast[:, 2:3], mlast[:, 0:1], mlast[:, 1:2], ALU.add))
            st.on(dve.tensor_scalar(gI[:, TC:T], negM[:, TC:T], m0[:, :], None, ALU.add))
            dve.tensor_scalar(gF[:, 0:TC], gA[:, 0:TC], mlast[:, 0:1], None, ALU.subtract)\
               .then_inc(s_grow, 1)
            split_lo((AT_V + 3) % NRAW, 1, CV + 3)
            split_lo(AT_U % NRAW, 0, CU)
            split_lo((AT_U + 1) % NRAW, 1, CU + 1)


            def exponents(i, hp):
                h = i * 2 + hp
                dve.wait_ge(s_m, h + 1)
                for d in range(2):
                    neg = cst[:, (C_NEGF, C_NEGB)[d]:(C_NEGF, C_NEGB)[d] + P]
                    for t in range(NT):
                        src = ps[:, 4, d * P:(d + 1) * P] if t == 0 else \
                            ps[:, 2 + d, (t - 1) * P:t * P]
                        ins = dve.scalar_tensor_tensor(
                            DG[hp][d][:, t, :], src, a_tok[:, t, bass.ds(h + d * H, 1)], neg,
                            ALU.add, ALU.min)
                    ins.then_inc(s_tdg, 1)

            def products(i, hp):
                h, dg, off = i * 2 + hp, DG[hp], OFF[hp]
                dve.wait_ge(s_sev, h * 5 + 5)
                for d in range(2):
                    dve.wait_ge(s_exp, h * 2 + d + 1)
                    if d == 1:
                        dve.wait_ge(s_kw, h * 2 + 2)
                    diag = dg[d][:, 1:NT, :]
                    ins = dve.tensor_tensor(diag, diag, S[:, :].rearrange(
                        "p (j x) -> p j x", x=TL + P)[:, 0:NL, 0:P], ALU.mult)
                    if d == 1:
                        ins.then_inc(m_free, 1)
                    dve.tensor_tensor(dg[d][:, 0, :], dg[d][:, 0, :], S[:, 2048:2048 + P], ALU.mult)
                    for j in (range(0, 3), range(1, 4))[d]:
                        o = (OFF_F, OFF_B)[d][j - d]
                        t0, n = ((j + 1) * P, (3 - j) * P) if d == 0 else (0, j * P)
                        ins = dve.tensor_tensor(off[d][:, o:o + n], off[d][:, o:o + n],
                                                S[:, j * TL + t0:j * TL + t0 + n], ALU.mult)
                ins.then_inc(s_p, 1)

            def numerators(i, hp):
                h = i * 2 + hp
                dve.wait_ge(s_modT, h + 2)
                dve.tensor_tensor(mod[:, bass.ds(h * 4 + 16, 4), :],
                                  ps[:, 5, 0:8].rearrange("p (j c) -> p j c", c=2),
                                  by(col[:, bass.ds(h * 4 + B_MOD + 16, 4)].unsqueeze(2),
                                     [P, 4, 2]), ALU.add).then_inc(qc5_free, 1)
                dve.wait_ge(s_nm, h + 1)
                dve.wait_ge(s_pv, h * 6 + 1)
                dve.tensor_copy(num[:, 0, :, :], ps[:, 6, 0:2 * V1].rearrange(
                    "p (d n) -> p d n", n=V1)).then_inc(pv6_free, 1)
                for t in range(NL):
                    dve.wait_ge(s_pv, h * 6 + 2 + t)
                    qc, qs = ((5, qc5_free), (1, qc1_free))[t % 2]
                    wi = wi_tok[:, t + 1, :].rearrange("p (d h) -> p d h", d=2)[:, :, bass.ds(h, 1)]
                    dve.tensor_tensor(num[:, t + 1, :, :], ps[:, qc, 0:2 * V1].rearrange(
                        "p (d n) -> p d n", n=V1), by(wi, [P, 2, V1]), ALU.mult).then_inc(qs, 1)
                    dve.wait_ge(qs, (h * 3 + 3 if qc == 5 else h * 2 + 2) + t // 2)
                    pb, pf = ((7, pv7_free), (6, pv6_free))[t % 2]
                    dve.tensor_tensor(num[:, t + 1, :, :], num[:, t + 1, :, :],
                                      ps[:, pb, 0:2 * V1].rearrange("p (d n) -> p d n", n=V1),
                                      ALU.add).then_inc(pf, 1)

            def outputs(i, hp, last=False):
                h = i * 2 + hp
                hs = Steps(dve, v_head)
                hs.enter(h * HEAD_STEPS)
                dve.wait_ge(pv6_free, h * 3 + 4)
                dve.wait_ge(pv7_free, h * 3 + 3)
                em = em_tok[:, :, :].rearrange("p t (d h) -> p t d h", d=2)[:, :, :, bass.ds(h, 1)]
                den = num[:, :, :, DH:V1]
                rv = rinv[:, :, :].unsqueeze(3)
                hs.do(dve.scalar_tensor_tensor(rv, den, -1.0, den, ALU.mult, ALU.max))
                hs.do(dve.tensor_tensor(rv, rv, em, ALU.max))
                hs.do(dve.reciprocal(rinv[:, :, :], rinv[:, :, :]))
                nn = num[:, :, :, 0:DH]
                hs.do(dve.tensor_tensor(nn, nn, by(rinv[:, :, :].unsqueeze(3), [P, NT, 2, DH]),
                                        ALU.mult))
                dve.wait_ge(s_pv, h * 6 + 6)
                dve.tensor_tensor(Vt[:, :, h, 0:DH], num[:, :, 0, 0:DH], num[:, :, 1, 0:DH],
                                  ALU.add).then_inc(s_nm, 1)
                if not last:
                    dve.tensor_copy(qst[:, :], QK[:, h + 1, TC:T]).then_inc(s_qst, 1)
                assert hs.n == HEAD_STEPS, hs.n

            dve.tensor_copy(qst[:, :], QK[:, 0, TC:T]).then_inc(s_qst, 1)
            exponents(0, 0)
            products(0, 0)
            with dve.Fori(0, H // 2 - 1) as i:
                for hp in range(2):
                    after = (i, 1) if hp == 0 else (i + 1, 0)
                    exponents(*after)
                    numerators(i, hp)
                    products(*after)
                    outputs(i, hp)
            i = H // 2 - 1
            exponents(i, 1)
            numerators(i, 0)
            products(i, 1)
            outputs(i, 0)
            numerators(i, 1)
            split_lo(AT_O % NRAW, 0, CO)
            outputs(i, 1, last=True)

            dve.wait_ge(s_nm, 1 + H)
            split_lo((AT_O + 1) % NRAW, 1, CO + 1)
            tmp = Y[:, 0:2, :].rearrange("p a n -> p (a n)")[:, 0:H * DH].rearrange(
                "p (h n) -> p h n", n=DH)
            for t in range(NT):
                hv = Vt[:, t, :, 0:DH]
                st.do(dve.tensor_tensor(tmp, hv, hv, ALU.mult))
                ins = dve.tensor_reduce(hss[:, t, :], tmp, AX, ALU.add)
                if t < NT - 1:
                    st.do(ins)
                else:
                    ins.then_inc(s_hd, 1)
            split_lo((AT_O + 2) % NRAW, 0, CO + 2)
            split_lo((AT_O + 3) % NRAW, 1, CO + 3)
            dve.wait_ge(s_o, 1)
            for t in range(NT):
                hv = Vt[:, t, :, 0:DH]
                dve.tensor_tensor(hv, hv, by(hss[:, t, :].unsqueeze(2), [P, H, DH]), ALU.mult)\
                   .then_inc(s_hd, 1)
            split_lo(AT_G % NRAW, 0, CTH)
            for k in range(KT):
                e = E_Y + k
                dve.wait_ge(blk_free, 4 + E_Y)
                dve.wait_ge(blk_ready, e + 1)
                st.on(dve.scalar_tensor_tensor(Y[:, k, 0:3 * P], O[:, k, 0:3 * P], 1.0,
                                               ps[:, 2 * (e % 4), 0:3 * P], ALU.add, ALU.mult))
                dve.scalar_tensor_tensor(Y[:, k, 3 * P:T], O[:, k, 3 * P:T], 1.0,
                                         ps[:, 2 * (e % 4) + 1, 0:2 * P], ALU.add, ALU.mult)\
                   .then_inc(blk_free, 1)
            with dve.Fori(0, N_G // NRAW) as i:
                for j in range(NRAW):
                    split_lo((AT_G + j + 1) % NRAW, (j + 1) % 2, i * 4 + CTH + j + 1)
            for g in range(NG):
                dve.wait_ge(s_ybh, g + 1)
                dve.scalar_tensor_tensor(halves(ybl[:, g, :]), pair(E_PL + g),
                                         col[:, P_S + g:P_S + g + 1], halves(f32(ybh[:, g, :])),
                                         ALU.mult, ALU.subtract).then_inc(blk_free, 1)
            split_lo((AT_B + 1) % NRAW, 1, CB + 1)
            for k in range(KT):
                dve.wait_ge(s_yh, k + 1)
                dve.scalar_tensor_tensor(hlo[:, k, :], Y[:, k, :], half_gn[:, k:k + 1],
                                         f32(hhi[:, k, :]), ALU.mult, ALU.subtract).then_inc(s_yl, 1)
                e = E_B + k
                dve.wait_ge(blk_ready, e + 1)
                dve.scalar_tensor_tensor(halves(TH[:, k, :]), halves(TH[:, k, :]), 1.0, pair(e),
                                         ALU.add, ALU.mult).then_inc(blk_free, 1)
                if k in (3, 7):
                    split_lo((AT_A + k // 4) % NRAW, (k // 4) % 2, CA + k // 4)
            dve.tensor_scalar(half_gate[:, :, :], mod[:, 16:24, :], 0.5, None, ALU.mult)\
               .then_inc(v_steps, 1)
            st.n += 1
            for k in range(KT):
                e = E_A + k
                dve.wait_ge(blk_free, 4 + E_B + k + 1)
                dve.wait_ge(blk_ready, e + 1)
                dve.scalar_tensor_tensor(halves(TH[:, KT + k, :]), halves(TH[:, KT + k, :]), 1.0,
                                         pair(e), ALU.add, ALU.mult).then_inc(blk_free, 1)
                dve.wait_ge(blk_free, 4 + e + 1)
                dve.tensor_tensor(TH[:, k, :], TH[:, k, :], TH[:, KT + k, :], ALU.add)\
                   .then_inc(s_mg, 1)
                if k % 2 == 1:
                    ci = CA + 2 + k // 2
                    if k < KT - 1:
                        split_lo((AT_A + 2 + k // 2) % NRAW, ci % 2, ci)
                    for kk in (k - 1, k):
                        dve.wait_ge(s_mgh, kk + 1)
                        dve.tensor_tensor(mgl[:, kk, :], TH[:, kk, :], f32(mgh[:, kk, :]),
                                          ALU.subtract).then_inc(s_mgl, 1)
                    if k == KT - 1:
                        split_lo((AT_A + 2 + k // 2) % NRAW, ci % 2, ci)
            dve.wait_ge(d_xr, 16)
            st.wait()
            for k in range(KT):
                e = E_OUT + k
                dve.wait_ge(blk_ready, e + 1)
                pa, pb = ps[:, 2 * (e % 4), :], ps[:, 2 * (e % 4) + 1, :]
                for j, (c, src, a, b) in enumerate(((0, pa[:, 0:TC], 0, TC),
                                                    (1, pa[:, TC:HALF], TC, HALF),
                                                    (1, pb[:, 0:HALF], HALF, T))):
                    st.on(dve.scalar_tensor_tensor(xres[:, k, a:b], src, half_gate[:, k, c:c + 1],
                                                   xres[:, k, a:b], ALU.mult, ALU.add))
                st.wait()
                dve.sem_inc(blk_free, 1)
                dve.sem_inc(s_xr, 1)
                if k in (0, 2):
                    ci = COUT + 2 + k // 2
                    split_lo((AT_OUT + 2 + k // 2) % NRAW, ci % 2, ci)

            def expert_lo(c, n=0):
                dve.wait_ge(e_hi, n * ECH + c + 1)
                dve.tensor_tensor(elo[c % ESPL][:, :], eraw[c % ERAW][:, :],
                                  f32(ehi[c % ESPL][:, :]), ALU.subtract)\
                   .then_inc(e_free[c % ERAW], 1)

            st.do(dve.scalar_tensor_tensor(gain[:, :, :], mod[:, 32:40, :], 1.0,
                                           by(col[:, G_2:G_2 + KT].unsqueeze(2), [P, KT, 2]),
                                           ALU.add, ALU.mult))
            st.on(dve.memset(am[:, NT, :], 0.0))
            st.on(dve.memset(cum[:, 0, :], 0.0))
            dve.wait_ge(s_rs2, 1)
            for k in range(KT):
                dve.tensor_tensor(h2[:, k, :], xres[:, k, :], rs2[:, :], ALU.mult).then_inc(s_hn2, 1)

            def token_lo(t):
                dve.wait_ge(s_tk, t + 1)
                dve.tensor_tensor(tkl[:, t, :].rearrange("p (a n) -> p a n", a=2),
                                  ps[:, 4 + 2 * (t % 2):6 + 2 * (t % 2), :],
                                  f32(tkh[:, t, :]).rearrange("p (a n) -> p a n", a=2),
                                  ALU.subtract).then_inc(s_tkl, 1)

            def choose(q):
                at_ = slice(0, 2) if q is None else bass.ds(q * 2 + 2, 2)
                shape = [P, NT, 2, SLOTS]
                dve.tensor_tensor(sel[:, :, :].rearrange("p t (x n) -> p t x n", x=2),
                                  by(iota.unsqueeze(1).unsqueeze(1), shape),
                                  by(rank[:, :, at_].unsqueeze(3), shape), ALU.is_equal)\
                   .then_inc(e_sel, 1)

            gm, se, v1, v2, ed, pw, wa, wb = (r5[:, i, :] for i in range(8))

            def over(ap, n):
                return by(ap.unsqueeze(2), [P, NT, n])

            def first_max(out, vals, mx):
                st.do(dve.tensor_tensor(t5[:, :, :], vals, over(mx, 4), ALU.is_equal))
                wt = cst[:, C_WT:C_WT + 4 * NT].rearrange("p (t n) -> p t n", n=4)
                st.do(dve.tensor_tensor(t5[:, :, :], t5[:, :, :], wt, ALU.mult))
                st.do(dve.tensor_reduce(r5[:, 8, :], t5[:, :, :], AX, ALU.max))
                st.do(dve.tensor_tensor(out, t5[:, :, :], over(r5[:, 8, :], 4), ALU.is_equal))

            for t in range(2):
                token_lo(t)
            dve.wait_ge(s_rk, 1)
            st.do(dve.tensor_tensor(lg[:, :, :], ps[:, 0, 0:NT * (EG + NE)].rearrange(
                "p (t n) -> p t n", t=NT), by(br[:, :].unsqueeze(1), [P, NT, EG + NE]), ALU.add))
            gl = lg[:, :, 0:EG]
            st.do(dve.tensor_reduce(gm, gl, AX, ALU.max))
            dve.tensor_tensor(t4[:, :, :], gl, over(gm, EG), ALU.subtract).then_inc(s_ex, 1)
            first_max(goh[:, :, :], gl, gm)
            le = lg[:, :, EG:].rearrange("p t (g e) -> p t g e", g=EG)
            st.do(dve.tensor_tensor(t16[:, :, :, :], le, by(goh[:, :, :].unsqueeze(3),
                                                            [P, NT, EG, EE]), ALU.mult))
            st.do(dve.tensor_reduce(les[:, :, :], t16[:, :, :, :].rearrange("p t g e -> p t e g"),
                                    AX, ALU.add))
            st.do(dve.tensor_reduce(v1, les[:, :, :], AX, ALU.max))
            first_max(o1[:, :, :], les[:, :, :], v1)
            st.do(dve.scalar_tensor_tensor(les[:, :, :], o1[:, :, :], NEG, les[:, :, :],
                                           ALU.mult, ALU.add))
            st.do(dve.tensor_reduce(v2, les[:, :, :], AX, ALU.max))
            dve.tensor_tensor(ed, v2, v1, ALU.subtract).then_inc(s_ex, 1)
            first_max(o2[:, :, :], les[:, :, :], v2)
            st.on(dve.tensor_tensor(t5[:, :, :], o1[:, :, :], o2[:, :, :], ALU.add))
            dve.wait_ge(s_lg, 2)
            st.wait()
            am4 = am[:, 0:NT, :].rearrange("p t (g e) -> p t g e", g=EG)
            gb = by(goh[:, :, :].unsqueeze(3), [P, NT, EG, EE])
            dve.tensor_tensor(am4, by(t5[:, :, :].unsqueeze(2), [P, NT, EG, EE]), gb, ALU.mult)\
               .then_inc(s_am, 1)
            dve.wait_ge(s_am, 1)
            for t in range(NT):
                st.do(dve.tensor_tensor(cum[:, t + 1, :], cum[:, t, :], am[:, t, :], ALU.add))
            dve.sem_inc(s_am, 1)
            token_lo(2)
            dve.wait_ge(s_rk, 2)
            rk = ps[:, 1, 0:NT * NE].rearrange("p (t n) -> p t n", t=NT)
            st.do(dve.scalar_tensor_tensor(rank[:, :, 0:NE], rk, 1.0, am[:, 0:NT, :], ALU.add,
                                            ALU.mult))
            st.do(dve.tensor_scalar(rank[:, :, 0:NE], rank[:, :, 0:NE], -1.0, None, ALU.add))
            st.do(dve.tensor_scalar(rank[:, :, NE:NE + 2], rank[:, :, 0:2], -float(SLOTS), None,
                                    ALU.add))
            choose(None)
            for t in range(3, NT):
                token_lo(t)
            st.do(dve.tensor_reduce(se, t4[:, :, :], AX, ALU.add))
            st.do(dve.scalar_tensor_tensor(pw, ed, 1.0, se, ALU.add, ALU.mult))
            st.do(dve.reciprocal(wa, pw))
            st.do(dve.tensor_scalar(wa, wa, 0.5, None, ALU.mult))
            st.do(dve.tensor_tensor(wb, wa, ed, ALU.mult))
            st.on(dve.tensor_tensor(o1[:, :, :], o1[:, :, :], over(wa, EE), ALU.mult))
            st.do(dve.tensor_tensor(o2[:, :, :], o2[:, :, :], over(wb, EE), ALU.mult))
            st.do(dve.tensor_tensor(o1[:, :, :], o1[:, :, :], o2[:, :, :], ALU.add))
            st.do(dve.tensor_tensor(wtok[:, :, :].rearrange("p t (g e) -> p t g e", g=EG),
                                    by(o1[:, :, :].unsqueeze(2), [P, NT, EG, EE]), gb, ALU.mult))
            st.do(dve.tensor_copy(wtr[:, :, :, 0], wtok[:, :, :]))
            dve.tensor_tensor(wtr[:, :, :, 1], wtok[:, :, :], f32(wtr[:, :, :, 0]), ALU.subtract)\
               .then_inc(s_wtr, 1)
            st.do(dve.tensor_reduce(thr[:, 5:6], ps[:, 1, NT * NE:NT * NE + NE], AX, ALU.max))
            st.do(dve.tensor_scalar(thr[:, 0:5], cst[:, C_THR:C_THR + ROUNDS], thr[:, 5:6], None,
                                    ALU.is_lt))
            st.do(dve.tensor_reduce(thr[:, 6:7], thr[:, 0:5], AX, ALU.add))
            dve.tensor_copy(rounds_i[0:1, 0:1], thr[0:1, 6:7]).then_inc(s_cnt, 1)
            for c in range(ESPL):
                expert_lo(c)

            def tokens_lo(a, count):
                dve.wait_ge(e_xgh, count)
                hi, lo = (x[:, 4 * a:4 * a + 4, :].rearrange("p (b k) n -> p b (k n)", b=2)
                          for x in (xgh, xgl))
                dve.tensor_tensor(lo, ps[:, 4 + 2 * a:6 + 2 * a, :], f32(hi), ALU.subtract)\
                   .then_inc(e_xgl, 1)

            def add_out(k, count, steps):
                dve.wait_ge(e_cmb, count)
                b = 2 + 2 * (k % 3)
                for c, src, a0, b0 in ((0, ps[:, b, 0:TC], 0, TC), (1, ps[:, b, TC:HALF], TC, HALF)):
                    steps.on(dve.scalar_tensor_tensor(xres[:, k, a0:b0], src,
                                                      mod[:, 40 + k, c:c + 1],
                                                      xres[:, k, a0:b0], ALU.mult, ALU.add))
                dve.scalar_tensor_tensor(xres[:, k, HALF:T], ps[:, b + 1, 0:HALF],
                                         mod[:, 40 + k, 1:2], xres[:, k, HALF:T],
                                         ALU.mult, ALU.add).then_inc(e_add, 1)

            def inner(x, n, steps):
                dve.wait_ge(e_th, n * 2 + x + 1)
                steps.do(dve.scalar_tensor_tensor(act_[:, :], th[:, :], 1.0, ps[:, 0, :],
                                                  ALU.add, ALU.mult))
                dve.tensor_tensor(act_[:, :], act_[:, :], ps[:, 1, :], ALU.mult)\
                   .then_inc(e_act, 1)

            def act_lo(x, n):
                dve.wait_ge(e_aTh, n * 2 + x + 1)
                dve.tensor_tensor(aTl[:, :, :].rearrange("p f n -> p (f n)"), ps[:, 0, :],
                                  f32(aTh[:, :, :]).rearrange("p f n -> p (f n)"),
                                  ALU.subtract).then_inc(e_aTl, 1)

            def out_lo(x, n):
                dve.wait_ge(e_yh, n * 2 + 3 + x)
                dve.wait_ge(e_ws, n + 1)
                dve.scalar_tensor_tensor(yl[:, x, :].rearrange("p (a n) -> p a n", a=2),
                                         ps[:, 2:4, :], wslot[:, x:x + 1],
                                         f32(yh[:, x, :]).rearrange("p (a n) -> p a n", a=2),
                                         ALU.mult, ALU.subtract).then_inc(e_yl, 1)

            for a in range(2):
                tokens_lo(a, a + 1)
            dve.wait_ge(s_cnt, 1)
            rounds = dve.value_load(rounds_i[0:1, 0:1], min_val=1, max_val=ROUNDS)
            with dve.Fori(0, rounds) as r:
                with dve.Fori(0, NPAIR) as q:
                    n = r * NPAIR + q
                    it = Steps(dve, v_item)
                    it.enter(n * PAIR_STEPS)
                    for c in (3, 4, 5):
                        expert_lo(c, n)
                    inner(0, n, it)
                    for k in range(4):
                        add_out(k, n * KT + k + 1, it)
                    act_lo(0, n)
                    for k in range(4, KT):
                        add_out(k, n * KT + k + 1, it)
                    for c in (6, 7, 8, 9):
                        expert_lo(c, n)
                    inner(1, n, it)
                    dve.wait_ge(e_selp, n + 1)
                    ws = ps[:, 7, 0:4].rearrange("p (x c) -> p x c", c=2)
                    dve.tensor_reduce(wslot[:, :], ws, AX, ALU.add).then_inc(e_ws, 1)
                    choose(q)
                    expert_lo(10, n)
                    expert_lo(11, n)
                    out_lo(0, n)
                    act_lo(1, n)
                    expert_lo(12, n)
                    for a in range(2):
                        tokens_lo(a, n * 2 + 3 + a)
                    expert_lo(13, n)
                    expert_lo(14, n)
                    out_lo(1, n)
                    assert it.n == PAIR_STEPS, it.n
                dve.tensor_scalar(rank[:, :, :], rank[:, :, :], -float(SLOTS), None, ALU.add)\
                   .then_inc(s_round, 1)
                dve.wait_ge(s_round, r + 1)
            for k in range(KT):
                add_out(k, rounds * (NPAIR * KT) + k + 1, st)
            dve.wait_ge(e_add, rounds * (NPAIR * KT) + KT)
            for k in range(KT):
                dve.tensor_scalar(yout[:, k, :], xres[:, k, :], col[:, G_F + k:G_F + k + 1], None,
                                  ALU.mult).then_inc(s_yg, 1)
            dve.wait_ge(s_yg, KT)
            dve.wait_ge(s_rsf, 1)
            for k in range(N_YD):
                dve.tensor_tensor(yout[:, k, :], yout[:, k, :], rs2[:, :], ALU.mult)\
                   .then_inc(s_yo, 1)

        @block.tensor
        def _(pe):
            def mm(out, lhsT, rhs, start, stop):
                return nc.tensor.matmul(out, lhsT, rhs, start=start, stop=stop)

            def three(groups, lh, ll, rh, rl, start, stop):
                for l, r, a, b in ((lh, rh, start, False), (lh, rl, False, False),
                                   (ll, rh, False, stop)):
                    for out, cut in groups:
                        last = mm(out, l, cut(r), a, b)
                return last

            def cut_half(a):
                return lambda r: r[:, a * HALF:(a + 1) * HALF]

            def block_out(e, wh, wl, kt, at_w, rh, rl, ready=None):
                groups = [(pair(e)[:, a, :], cut_half(a)) for a in range(2)]
                for k in range(kt):
                    if ready is not None:
                        pe.wait_ge(ready, k + 1)
                    o = at_w + k * P
                    last = three(groups, wh[:, o:o + P], wl[:, o:o + P], rh[:, k, :], rl[:, k, :],
                                 k == 0, k == kt - 1)
                return last

            def chunk_split(slot, use):
                pe.wait_ge(raw_free[slot], use + 2)

            def dense(c, p, e0, i=0, rh=hhi, rl=hlo, kt=KT, per_i=0, ready=None):
                chunk_split(c % NRAW, i + c // NRAW)
                for b in range(CH // (kt * P)):
                    pe.wait_ge(blk_free, i * per_i + e0 + b + 1)
                    block_out(e0 + b, whi[p], wlo[p], kt, b * kt * P, rh, rl,
                              ready if b == 0 else None).then_inc(blk_ready, 1)

            def mod_chunk(slot, use, out, c2):
                pe.wait_ge(raw_full[slot], (use + 1) * 16)
                for k in range(KT):
                    last = mm(out, csil[:, k, 2 - 2 * c2:6 - 2 * c2],
                              raw[slot][:, k * 2 * P:(k + 1) * 2 * P],
                              k == 0 and c2 == 0, k == KT - 1 and c2 == 1)
                last.then_inc(raw_free[slot], 1)

            def square_sums(sq, summed, done):
                pe.wait_ge(summed, KT - 1)
                for a in range(2):
                    last = mm(ps[:, a, 0:HALF], ones, sq[:, 0, a * HALF:(a + 1) * HALF], True, True)
                last.then_inc(done, 1)

            pe.wait_ge(d_const, 16 * N_SMALL)
            pe.wait_ge(s_csil, 4)
            for c in range(N_MOD1):
                q = c // 2
                mod_chunk(c % NRAW, c // NRAW, ps[0:4, 2 + q // 2, (q % 2) * 2 * P:
                                                  (q % 2 + 1) * 2 * P], c % 2)
                if c == 5:
                    square_sums(hn, s_sum1, s_ssq)
            for b in range(8):
                pe.wait_ge(s_mrow, b // 4 + 1)
                last = nc.tensor.transpose(ps[:, 4, 4 * b:4 * b + 4], mrow1[:, b * P:(b + 1) * P],
                                           ident[0:4, 0:4])
            last.then_inc(s_modT, 1)
            pe.wait_ge(s_wgl, 1)
            for k in range(KT):
                pe.wait_ge(s_hlo, k + 1)
                last = three([(ps[0:GP, 6 + a, 0:HALF], cut_half(a)) for a in range(2)],
                             wgh[:, k, :], wgl[:, k, :], hhi[:, k, :], hlo[:, k, :],
                             k == 0, k == KT - 1)
            last.then_inc(s_gps, 1)
            pe.wait_ge(s_gate, 2)
            with pe.Fori(0, N_QK // NRAW) as i:
                for j in range(NRAW):
                    dense(AT_QK + j, j % 2, 2 * j, i, per_i=8)

            def v_rows(v, e):
                pe.wait_ge(blk_free, 4 + E_V + max(2 * v - 1, 0) + 1)
                pe.wait_ge(blk_free, e + 1)
                for t in range(NT):
                    last = nc.tensor.transpose(
                        ps[:, 2 * (e % 4) + t // 3, (t % 3) * P:(t % 3 + 1) * P],
                        vst[v % 2][:, t * P:(t + 1) * P], ident)
                last.then_inc(blk_ready, 1)

            e = E_V
            for v in range(H):
                c, p = AT_V + v // 2, (v // 2) % 2
                if v % 2 == 0:
                    chunk_split(c % NRAW, c // NRAW)
                pe.wait_ge(blk_free, e + 1)
                block_out(e, whi[p], wlo[p], KT, (v % 2) * KT * P, hhi, hlo).then_inc(blk_ready, 1)
                e += 1
                if v:
                    v_rows(v - 1, e)
                    e += 1
            v_rows(H - 1, e)
            pe.wait_ge(s_grow, 1)
            pe.wait_ge(blk_free, E_G8 + 1)
            g0 = 2 * (E_G8 % 4)
            for t in range(NT):
                for src, o in ((gA, 0), (gI, 64), (gC, 144)):
                    if t or src is not gI:
                        nc.tensor.transpose(ps[:, g0, o + t * R16:o + (t + 1) * R16],
                                            src[:, t * P:(t + 1) * P], ident[0:R16, 0:R16])
            nc.tensor.transpose(ps[:, g0, 224:240], gF[:, 0:P], ident[0:R16, 0:R16])\
              .then_inc(blk_ready, 1)
            for j in range(N_U):
                dense(AT_U + j, j % 2, E_U + 2 * j)

            pe.wait_ge(blk_free, 4 + E_O)
            pe.wait_ge(d_st, 16)
            pe.wait_ge(s_init, 2)

            def mod_columns(h):
                pe.wait_ge(s_mrow, h + 3)
                pe.wait_ge(qc5_free, h * 3 + 1)
                for b in range(2):
                    ins = mm(ps[:, 5, 4 * b:4 * b + 4], mrow[:, b * P:(b + 1) * P], ident[0:4, 0:4],
                             True, True)
                ins.then_inc(s_modT, 1)

            def scores(i, hp):
                h = i * 2 + hp
                first = isinstance(h, int) and h == 0
                pe.wait_ge(s_pick, h * 2 + 2)
                pe.wait_ge(m_free, h + 1)
                for d in range(2):
                    mm(ps[:, 2 + d, :], pick[d][:, :], negM[:, TC:T], True, True)
                for d in range(2):
                    mm(ps[:, 4, d * P:(d + 1) * P], pick[d][:, :], negM[:, 0:TC], True, True)
                pe.wait_ge(s_kst, h + 1)
                nc.tensor.transpose(ps[:, 4, 2 * P:3 * P], kst[:, 0:P], ident).then_inc(s_m, 1)
                if not first:
                    pe.wait_ge(s_mrow, h + 2)
                    pe.wait_ge(s_sev, h * 5)
                mm(ps[:, 0, 0:P], kst[:, 0:P], QK[:, h, 0:P], True, True).then_inc(s_sc, 1)
                if not first:
                    pe.wait_ge(qc1_free, h * 2 - 1)
                for j in range(NL):
                    if j == 2 and not first:
                        mod_columns(h - 1)
                    if j:
                        pe.wait_ge(s_sev, h * 5 + j)
                    mm(ps[:, (j + 1) % 2, :], kst[:, (j + 1) * P:(j + 2) * P], QK[:, h, TC:T],
                       True, True).then_inc(s_sc, 1)

            def values(i, hp, last=False):
                h = i * 2 + hp

                def pv(t, bank, free):
                    pe.wait_ge(*free)
                    for d in range(2):
                        tiles = [t] if t == 0 else (range(1, t + 1), range(t, NT))[d]
                        for s in tiles:
                            if s == t:
                                w = DG[hp][d][:, t, :]
                            elif d == 0:
                                o = OFF_F[s - 1] + (t - s - 1) * P
                                w = OFF[hp][0][:, o:o + P]
                            else:
                                o = OFF_B[s - 2] + (t - 1) * P
                                w = OFF[hp][1][:, o:o + P]
                            ins = mm(ps[:, bank, d * V1:(d + 1) * V1], w, Vt[:, s, h, :],
                                     s == tiles[0], s == tiles[-1])
                    ins.then_inc(s_pv, 1)

                if last:
                    mod_columns(h)
                pe.wait_ge(s_p, h + 1)
                pv(0, 6, (pv6_free, h * 3 + 1))
                pe.wait_ge(s_qst, h + 1)
                if not last:
                    pe.wait_ge(s_sev, h * 5 + 10)
                for t in range(NL):
                    if t % 2 == 0:
                        pe.wait_ge(qc5_free, h * 3 + 2 + t // 2)
                    else:
                        pe.wait_ge(qc1_free, h * 2 + 1 + t // 2)
                    mm(ps[:, (5, 1)[t % 2], 0:2 * V1].rearrange("p (d n) -> p d n", n=V1),
                       qst[:, t * P:(t + 1) * P], stC[:, :, h, :], True, True)
                    pv(t + 1, (7, 6)[t % 2],
                       (pv7_free, h * 3 + 1 + t // 2) if t % 2 == 0
                       else (pv6_free, h * 3 + 2 + t // 2))
                pe.wait_ge(s_kw, h * 2 + 2)
                pe.wait_ge(pv7_free, h * 3 + 3)
                for d in range(2):
                    ins = mm(ps[:, 7, d * V1:(d + 1) * V1], kw[hp][d][:, :], Vt[:, 0, h, :],
                             True, True)
                ins.then_inc(s_pv, 1)

            def mod_pair(i, hp):
                for c2 in range(2):
                    c = AT_MOD2 + 2 * hp + c2
                    mod_chunk(c % NRAW, i + c // NRAW, ps[0:4, 0, 0:2 * P], c2)

            scores(0, 0)
            pe.wait_ge(s_sev, 5)
            mod_pair(0, 0)
            with pe.Fori(0, H // 2 - 1) as i:
                scores(i, 1)
                values(i, 0)
                mod_pair(i, 1)
                scores(i + 1, 0)
                values(i, 1)
                mod_pair(i + 1, 0)
            i = H // 2 - 1
            scores(i, 1)
            values(i, 0)
            mod_pair(i, 1)
            values(i, 1, last=True)

            for s_, v_ in ((pv6_free, 1 + 3 * H), (pv7_free, 1 + 3 * H), (qc1_free, 1 + 2 * H),
                           (qc5_free, 1 + 3 * H), (m_free, 1 + H), (s_sev, 5 * H)):
                pe.wait_ge(s_, v_)
            for j in range(N_O):
                dense(AT_O + j, j % 2, E_O + 2 * j)
            for k in range(H):
                e = E_Y + k
                pe.wait_ge(s_hd, 1 + NT)
                pe.wait_ge(blk_free, e + 1)
                for t in range(NT):
                    last = nc.tensor.transpose(
                        ps[:, 2 * (e % 4) + t // 3, (t % 3) * P:(t % 3 + 1) * P],
                        Vt[:, t, k, 0:DH], ident)
                last.then_inc(blk_ready, 1)
            with pe.Fori(0, N_G // NRAW) as i:
                for j in range(NRAW):
                    dense(AT_G + j, j % 2, E_TH + 2 * j, i, per_i=8)
            pe.wait_ge(s_pool, 1)
            pe.wait_ge(d_wp, 16)
            for g in range(NG):
                e = E_PL + g
                pe.wait_ge(blk_free, e + 1)
                for a in range(2):
                    last = mm(pair(e)[:, a, :], wpool[:, g, :], U[:, g, a * HALF:(a + 1) * HALF],
                              True, True)
                last.then_inc(blk_ready, 1)
            pe.wait_ge(blk_free, 4 + E_B)
            for j in range(N_B):
                dense(AT_B + j, j % 2, E_B + 4 * j, rh=ybh, rl=ybl, kt=NG)
            pe.wait_ge(s_yl, KT)
            for j in range(N_A):
                dense(AT_A + j, j % 2, E_A + 2 * j)
            for j in range(N_OUT):
                dense(AT_OUT + j, j % 2, E_OUT + 2 * j, rh=mgh, rl=mgl,
                      ready=s_mgl if j == 0 else None)
            pe.wait_ge(blk_free, 4 + E_END)
            square_sums(n2, s_sum, s_ssq2)
            for k in range(KT):
                pe.wait_ge(s_h2, k + 1)
                for a in range(2):
                    last = mm(ps[0:EG + NE, 2 + a, 0:HALF], wr[:, k, :],
                              h2[:, k, a * HALF:(a + 1) * HALF], k == 0, k == KT - 1)
            last.then_inc(s_lgp, 1)

            def token_major(t):
                if t >= 2:
                    pe.wait_ge(s_tkl, t - 1)
                for k in range(KT):
                    last = nc.tensor.transpose(ps[:, 4 + 2 * (t % 2) + k // 4, (k % 4) * P:
                                                  (k % 4 + 1) * P], h2[:, k, t * P:(t + 1) * P], ident)
                last.then_inc(s_tkp, 1)

            token_major(0)
            pe.wait_ge(s_rs2, 1)
            pe.wait_ge(s_lgT, 1)
            n = EG + NE
            for t in range(NT):
                last = nc.tensor.transpose(ps[:, 0, t * n:(t + 1) * n], lgT[:, t * P:(t + 1) * P],
                                           ident[0:n, 0:n])
            last.then_inc(s_rk, 1)
            for t in range(1, 4):
                token_major(t)
            pe.wait_ge(s_am, 2)
            out = ps[:, 1, 0:(NT + 1) * NE].rearrange("p (t n) -> p t n", n=NE)
            mm(out, cst[:, C_STRICT:C_STRICT + P], am[:, :, :], True, False)
            mm(out, ones, cum[:, :, :], False, True).then_inc(s_rk, 1)
            for t in range(4, NT):
                token_major(t)

            def gather():
                for k in range(KT):
                    out = ps[:, 4 + k // 2, (k % 2) * 2 * SLOTS:(k % 2 + 1) * 2 * SLOTS]
                    for t in range(NT):
                        for src in (tkh, tkl):
                            last = mm(out, src[:, t, k * P:(k + 1) * P], sel[:, t, :],
                                      t == 0 and src is tkh, t == NT - 1 and src is tkl)
                    if k % 4 == 3:
                        last.then_inc(e_gat, 1)

            def combine(adds, k):
                if k >= 3:
                    pe.wait_ge(e_add, adds + k - 2)
                b = 2 + 2 * (k % 3)
                parts = [(x, src) for x in range(2) for src in (yh, yl)]
                for x, src in parts:
                    for a in range(2):
                        last = mm(ps[:, b + a, 0:HALF], src[:, x, k * P:(k + 1) * P],
                                  selT[:, x, a * HALF:(a + 1) * HALF],
                                  (x, src) == parts[0], (x, src) == parts[-1])
                last.then_inc(e_cmb, 1)

            def outputs_split(n):
                pe.wait_ge(e_yh, n * 2 + 2)
                pe.wait_ge(e_yl, n * 2 + 2)
                pe.wait_ge(e_selT, n + 1)

            def chunk(c, n):
                pe.wait_ge(e_free[c % ERAW], n * (ECH // ERAW) + c // ERAW + 2)
                return ehi[c % ESPL], elo[c % ESPL]

            def gate_up(x, n):
                for c in range(4):
                    if x == 0 and c < 2:
                        pe.wait_ge(e_xgl, n * 2 + c + 1)
                    hi, lo = chunk(4 * x + c, n)
                    for k in range(4):
                        kk = (c % 2) * 4 + k
                        last = three([(ps[:, c // 2, :], lambda w, k=k: w[:, k * DE:(k + 1) * DE])],
                                     xgh[:, kk, x * SLOTS:(x + 1) * SLOTS],
                                     xgl[:, kk, x * SLOTS:(x + 1) * SLOTS], hi, lo,
                                     kk == 0, kk == KT - 1)
                    last.then_inc(e_mm, 1)

            def inner_T(x, n):
                pe.wait_ge(e_act, n * 2 + x + 1)
                for f in range(FT):
                    last = nc.tensor.transpose(ps[:, 0, f * P:(f + 1) * P],
                                               act_[:, f * P:(f + 1) * P], ident)
                last.then_inc(e_aTp, 1)

            def down(x, n):
                for c in range(2):
                    hi, lo = chunk(8 + 2 * x + c, n)
                    for f2 in range(2):
                        f = 2 * c + f2
                        groups = [(ps[:, 2 + a, :], lambda w, a=a, f2=f2:
                                   w[:, (2 * f2 + a) * 512:(2 * f2 + a + 1) * 512])
                                  for a in range(2)]
                        last = three(groups, aTh[:, f, :], aTl[:, f, :], hi, lo,
                                     f == 0, f == FT - 1)
                    last.then_inc(e_mm, 1)

            pe.wait_ge(s_tkl, NT)
            pe.wait_ge(e_sel, 1)
            gather()
            pe.wait_ge(s_wtr, 1)
            pe.wait_ge(s_cnt, 1)
            rounds = pe.value_load(rounds_i[0:1, 0:1], min_val=1, max_val=ROUNDS)
            with pe.Fori(0, rounds) as r:
                with pe.Fori(0, NPAIR) as q:
                    n = r * NPAIR + q
                    gate_up(0, n)
                    outputs_split(n)
                    for k in range(4):
                        combine(n * KT, k)
                    inner_T(0, n)
                    for k in range(4, KT):
                        combine(n * KT, k)
                    pe.wait_ge(e_aTl, n * 2 + 1)
                    gate_up(1, n)
                    pe.wait_ge(e_add, n * KT + KT)
                    for x in range(2):
                        for t in range(NT):
                            o = x * NT + t
                            nc.tensor.transpose(ps[:, 4 + o // 4, (o % 4) * P:(o % 4 + 1) * P],
                                                f32(sel[:, t, x * SLOTS:(x + 1) * SLOTS]), ident)
                        for t in range(NT):
                            last = mm(ps[:, 7, 2 * x:2 * x + 2],
                                      sel[:, t, x * SLOTS:(x + 1) * SLOTS],
                                      wtr[:, t, bass.ds(q * 2 + x, 1), :].rearrange(
                                          "p e c -> p (e c)"), t == 0, t == NT - 1)
                    last.then_inc(e_selp, 1)
                    down(0, n)
                    inner_T(1, n)
                    pe.wait_ge(e_sel, n + 2)
                    pe.wait_ge(e_selT, n + 2)
                    pe.wait_ge(e_ws, n + 1)
                    gather()
                    pe.wait_ge(e_aTl, n * 2 + 2)
                    pe.wait_ge(e_yl, n * 2 + 3)
                    down(1, n)
            pe.wait_ge(e_xgl, rounds * (NPAIR * 2) + 2)
            outputs_split(rounds * NPAIR)
            for k in range(KT):
                combine(rounds * (NPAIR * KT), k)
            for k in [*range(KT // 2, KT), 0]:
                if k:
                    pe.wait_ge(s_sqf, k + 1)
                else:
                    pe.wait_ge(s_sumf, KT // 2 - 1)
                for a in range(2):
                    last = mm(ps[:, a, 0:HALF], ones, h2[:, k, a * HALF:(a + 1) * HALF],
                              k == KT // 2, k == 0)
            last.then_inc(s_ssf, 1)


def _constants():
    c = np.zeros((P, C_END), np.float32)
    r, q = np.arange(P)[:, None], np.arange(P)[None, :]
    c[:, C_ID:C_ID + P] = r == q
    c[:, C_ONE:C_ONE + P] = 1
    c[:, C_STRICT:C_STRICT + P] = r < q
    c[:, C_IOTA:C_IOTA + P] = q
    c[:, C_NEGF:C_NEGF + P] = np.where(r <= q, 0, NEG)
    c[:, C_NEGB:C_NEGB + P] = np.where(r >= q, 0, NEG)
    c[:H, C_MF] = 1
    c[H:R16, C_MB] = 1
    c[:, C_WT:C_WT + 4 * NT] = np.tile([8, 4, 2, 1], NT)
    c[:, C_THR:C_THR + ROUNDS] = np.arange(ROUNDS) * SLOTS
    c[:, C_EPS] = EPS
    cnt = np.zeros((NG, T), np.float32)

    def width(n, w):
        i = np.arange(n)
        return np.clip(i - w // 2 + w, 0, n) - np.clip(i - w // 2, 0, n)

    for g, w in enumerate(WIN):
        cnt[g, :TC] = width(TC, w)
        cnt[g, TC:] = np.outer(width(GR, w), width(GW, w)).ravel()
    return c, np.ascontiguousarray(np.broadcast_to(1 / cnt, (P, NG, T)), dtype=np.float32)


def _layout(i):
    i = {k: np.asarray(v) for k, v in i.items()}
    fm = lambda a: a.T.reshape(KT, P, -1).transpose(1, 0, 2)
    cols = lambda v: v.reshape(-1, P).T

    def chunks(w, kt):
        nb, per = w.shape[1] // P, CH // (kt * P)
        return w.reshape(kt, P, nb, P).transpose(2, 1, 0, 3).reshape(
            nb // per, per, P, kt * P).transpose(0, 2, 1, 3).reshape(nb // per, P, CH)

    w, b = i["w_in"][0], i["b_in"][0]
    g0 = 4 * D
    pool, ga, gb = g0 + 4 * H, g0 + 4 * H + NG * P, g0 + 4 * H + NG * P + D
    qkvu = np.r_[0:3 * D, pool:pool + NG * P]
    late = np.r_[3 * D:4 * D, gb:gb + D, ga:ga + D]
    wm = i["w_mod"][0].reshape(KT, P, -1, 2, 2, P).transpose(2, 4, 1, 0, 3, 5).reshape(-1, P, CH)
    wst = np.concatenate([wm[:N_MOD1], chunks(w[:, qkvu], KT), wm[N_MOD1:], chunks(w[:, late], KT),
                          chunks(i["w_proj_b"][0], NG), chunks(i["w_proj_a"][0], KT),
                          chunks(i["w_out"][0], KT)])
    wg = np.zeros((P, KT, GP), np.float32)
    bg = np.zeros((GP, 1), np.float32)
    for dst, src in ((0, 0), (8, 16), (32, 8), (40, 24)):
        wg[:, :, dst:dst + H] = w[:, g0 + src:g0 + src + H].reshape(KT, P, H).transpose(1, 0, 2)
        bg[dst:dst + H, 0] = b[g0 + src:g0 + src + H]
    col = np.concatenate([cols(b[qkvu]), cols(b[late]), cols(i["b_mod"][0]), cols(i["g_norm1"][0]),
                          cols(i["g_norm2"][0]), cols(i["g_final"]), cols(i["gn_gain"][0]),
                          cols(i["pool_scale"][0])], axis=1)
    wr = np.concatenate([i["w_router_grp"][0], i["w_router_exp"][0].reshape(D, NE)], 1)
    br = np.concatenate([i["b_router_grp"][0], i["b_router_exp"][0].reshape(NE)])
    st = np.concatenate([i["state_C"][0, 0], i["state_n"][0, 0][..., None]], -1)
    up = lambda a: a.reshape(NPAIR, 2, 2, 4, P, DE).transpose(0, 1, 2, 4, 3, 5).reshape(
        NPAIR, 2, 2, P, CH)
    down = i["w_exp_down"][0].reshape(NPAIR, 4, 2, P, D).transpose(0, 1, 3, 2, 4).reshape(
        NPAIR, 4, P, CH)
    gu = np.stack([up(i["w_exp_gate"][0]), up(i["w_exp_up"][0])], 2).reshape(NPAIR, 8, P, CH)
    ex = np.concatenate([gu, down], 1)
    cst, rcnt = _constants()
    return dict(
        x=fm(np.concatenate([i["x_prompt"][0], i["x_sample"][0]])),
        c=fm(np.stack([i["c_ctx"], i["c"][0]])), wst=wst, wg=wg, bg=bg, col=col,
        wpool=i["w_pool_grp"][0].transpose(1, 0, 2), wr=wr.reshape(KT, P, -1).transpose(1, 0, 2),
        br=np.broadcast_to(br, (P, EG + NE)), st=st.transpose(2, 0, 1, 3),
        m0=i["state_m"][0, 0].reshape(R16, 1), cst=cst, rcnt=rcnt,
        wexp=np.concatenate([ex, ex[:1]]))


_OUTS = (("y", (P, KT, T)), ("so", (P, 2, H, V1)), ("mo", (R16, 1)))


def kernel(**inputs):
    import concourse.bacc as bacc
    from concourse.bass_utils import run_bass_kernel_spmd

    nc = bacc.Bacc("TRN2", target_bir_lowering=False, num_devices=1)
    arrays, args = {}, []
    for name, a in _layout(inputs).items():
        arrays["in_" + name] = a = np.ascontiguousarray(a)
        args.append(nc.dram_tensor("in_" + name, a.shape, mybir.dt.from_np(a.dtype),
                                   kind="ExternalInput").ap())
    for name, shape in _OUTS:
        args.append(nc.dram_tensor("out_" + name, shape, F32, kind="ExternalOutput").ap())
    layer_kernel(nc, *args)
    got = run_bass_kernel_spmd(nc, [arrays], core_ids=[0]).results[0]
    y = got["out_y"].transpose(2, 1, 0).reshape(T, D)
    so = got["out_so"].transpose(1, 2, 0, 3)
    return (np.ascontiguousarray(y[:TC])[None], np.ascontiguousarray(y[TC:])[None],
            np.ascontiguousarray(so[..., :DH])[None, None],
            np.ascontiguousarray(so[..., DH])[None, None],
            np.ascontiguousarray(got["out_mo"].reshape(1, 1, 2, H)))
```
